# Optimizing a Trainium2 kernel written in Bass

```python
import math
import jax, jax.numpy as jnp
from jax import lax
import numpy as np
import jax
import jax.numpy as jnp

D_MODEL = 1024
BATCH = 1
SEQ = 512
DEPTH = 2

CHUNK = 64
N_A_LAYERS = DEPTH // 2
N_B_LAYERS = DEPTH - N_A_LAYERS

A_HEADS = 8
A_HEAD_K = 128
A_HEAD_V = 128
A_QK_WIDTH = A_HEADS * A_HEAD_K
A_V_WIDTH = A_HEADS * A_HEAD_V
A_CONV = 4
A_CONV_WIDTH = 2 * A_QK_WIDTH + A_V_WIDTH
A_IN_WIDTH = 2 * A_QK_WIDTH + 2 * A_V_WIDTH + 2 * A_HEADS

B_HEADS = 16
B_HEAD_DIM = 64
B_WIDTH = B_HEADS * B_HEAD_DIM
LEFT_CHUNKS = 8
BAND = (LEFT_CHUNKS + 1) * CHUNK
REL_CLIP = 256

FFN_DIM = 2816
FFN_CONV = 3

EPS = 1e-6
NEG_INF = -1e30


def rmsnorm(x, g):
    xf = x.astype(jnp.float32)
    y = xf * lax.rsqrt(jnp.mean(xf * xf, axis=-1, keepdims=True) + EPS)
    return (y * g.astype(jnp.float32)).astype(x.dtype)

def causal_dwconv(x, w):
    width = w.shape[0]
    return lax.conv_general_dilated(
        x, w[:, None, :].astype(x.dtype), window_strides=(1,), padding=[(width - 1, 0)],
        dimension_numbers=("NWC", "WIO", "NWC"), feature_group_count=x.shape[-1])

def _l2norm(t):
    return t * lax.rsqrt(jnp.sum(t * t, axis=-1, keepdims=True) + EPS)

def chunk_gated_delta_rule(q, k, v, beta, g):
    bsz, seq, nh, dk = q.shape
    dv = v.shape[-1]
    nc = seq // CHUNK

    def chunks(t):
        return t.reshape(bsz, nc, CHUNK, nh, -1).transpose(0, 3, 1, 2, 4)

    q, k, v = chunks(q), chunks(k), chunks(v)
    beta = chunks(beta[..., None])[..., 0]
    gcum = jnp.cumsum(chunks(g[..., None])[..., 0], axis=-1)

    causal = jnp.tril(jnp.ones((CHUNK, CHUNK), dtype=bool))
    strict = jnp.tril(jnp.ones((CHUNK, CHUNK), dtype=bool), k=-1)
    diff = gcum[..., :, None] - gcum[..., None, :]
    decay = jnp.where(causal, jnp.exp(jnp.where(causal, diff, 0.0)), 0.0)

    k_beta = k * beta[..., None]
    m = jnp.where(strict, jnp.einsum("bhnid,bhnjd->bhnij", k_beta, k) * decay, 0.0)
    eye = jnp.eye(CHUNK, dtype=m.dtype)
    rhs = jnp.concatenate([v * beta[..., None], k_beta * jnp.exp(gcum)[..., None]], axis=-1)
    uw = lax.linalg.triangular_solve(m + eye, rhs, left_side=True, lower=True, unit_diagonal=True)
    u, w = uw[..., :dv], uw[..., dv:]

    attn_qk = jnp.einsum("bhnid,bhnjd->bhnij", q, k) * decay
    q_dec = q * jnp.exp(gcum)[..., None]
    k_end = k * jnp.exp(gcum[..., -1:] - gcum)[..., None]
    chunk_decay = jnp.exp(gcum[..., -1])

    xs = tuple(jnp.moveaxis(t, 2, 0) for t in (q_dec, k_end, u, w, attn_qk, chunk_decay))

    def step(state, inp):
        qd, ke, u_c, w_c, a_c, dec = inp
        v_new = u_c - jnp.einsum("bhcd,bhdv->bhcv", w_c, state)
        o_c = jnp.einsum("bhcd,bhdv->bhcv", qd, state) + jnp.einsum("bhcj,bhjv->bhcv", a_c, v_new)
        state = state * dec[..., None, None] + jnp.einsum("bhcd,bhcv->bhdv", ke, v_new)
        return state, o_c

    state0 = jnp.zeros((bsz, nh, dk, dv), jnp.float32)
    _, o = lax.scan(step, state0, xs)
    return o.transpose(1, 0, 3, 2, 4).reshape(bsz, seq, nh, dv)

def gated_deltanet(xn, w_in, conv_w, A_log, dt_bias, out_norm_w, w_out):
    bsz, seq, _ = xn.shape
    proj = xn @ w_in
    qkv = jax.nn.silu(causal_dwconv(proj[..., :A_CONV_WIDTH], conv_w))
    z = proj[..., A_CONV_WIDTH:A_CONV_WIDTH + A_V_WIDTH]
    b_raw = proj[..., A_CONV_WIDTH + A_V_WIDTH:A_CONV_WIDTH + A_V_WIDTH + A_HEADS]
    a_raw = proj[..., A_CONV_WIDTH + A_V_WIDTH + A_HEADS:]
    f32 = jnp.float32
    q = _l2norm(qkv[..., :A_QK_WIDTH].reshape(bsz, seq, A_HEADS, A_HEAD_K).astype(f32)) * (A_HEAD_K ** -0.5)
    k = _l2norm(qkv[..., A_QK_WIDTH:2 * A_QK_WIDTH].reshape(bsz, seq, A_HEADS, A_HEAD_K).astype(f32))
    v = qkv[..., 2 * A_QK_WIDTH:].reshape(bsz, seq, A_HEADS, A_HEAD_V).astype(f32)
    beta = jax.nn.sigmoid(b_raw.astype(f32))
    g = -jnp.exp(A_log.astype(f32)) * jax.nn.softplus(a_raw.astype(f32) + dt_bias.astype(f32))
    o = chunk_gated_delta_rule(q, k, v, beta, g).astype(xn.dtype)
    o = rmsnorm(o, out_norm_w) * jax.nn.silu(z.reshape(bsz, seq, A_HEADS, A_HEAD_V))
    return o.reshape(bsz, seq, A_V_WIDTH) @ w_out

def chunk_attention(xn, w_q, rel_bias, w_out, k_pad, v_pad):
    bsz, seq, _ = xn.shape
    nc = seq // CHUNK
    q = (xn @ w_q).reshape(bsz, nc, CHUNK, B_HEADS, B_HEAD_DIM).transpose(1, 0, 2, 3, 4)
    rel = jnp.arange(CHUNK)[:, None] + LEFT_CHUNKS * CHUNK - jnp.arange(BAND)[None, :]
    bias = rel_bias[:, jnp.clip(rel, -REL_CLIP, REL_CLIP) + REL_CLIP].astype(jnp.float32)
    scale = B_HEAD_DIM ** -0.5

    def one_chunk(args):
        n, q_n = args
        k_band = lax.dynamic_slice_in_dim(k_pad, n * CHUNK, BAND, axis=1)
        v_band = lax.dynamic_slice_in_dim(v_pad, n * CHUNK, BAND, axis=1)
        s = jnp.einsum("bqhd,bkhd->bhqk", q_n, k_band).astype(jnp.float32) * scale + bias
        valid = jnp.arange(BAND) >= (LEFT_CHUNKS - n) * CHUNK
        s = jnp.where(valid, s, NEG_INF)
        p = jax.nn.softmax(s, axis=-1).astype(v_band.dtype)
        return jnp.einsum("bhqk,bkhd->bqhd", p, v_band)

    o = lax.map(one_chunk, (jnp.arange(nc, dtype=jnp.int32), q))
    o = o.transpose(1, 0, 2, 3, 4).reshape(bsz, seq, B_WIDTH)
    return o @ w_out

def conv_ffn(xn, w_up, conv_w, conv_b, w_down):
    h = causal_dwconv(xn @ w_up, conv_w) + conv_b
    gate, val = h[..., :FFN_DIM], h[..., FFN_DIM:]
    return (jax.nn.silu(gate) * val) @ w_down

def first_inputs(seed: int = 0) -> dict:
    key = jax.random.key(seed)
    ks = jax.random.split(key, 22)

    def nrm(k, shape, scale):
        return jax.random.normal(k, shape, jnp.float32) * scale

    dt = jnp.exp(jax.random.uniform(ks[5], (N_A_LAYERS, A_HEADS), jnp.float32,
                                    minval=math.log(1e-3), maxval=math.log(1e-1)))
    return {
        "x": nrm(ks[0], (BATCH, SEQ, D_MODEL), 1.0),
        "a_norm": 1.0 + nrm(ks[1], (N_A_LAYERS, D_MODEL), 0.02),
        "a_w_in": nrm(ks[2], (N_A_LAYERS, D_MODEL, A_IN_WIDTH), D_MODEL ** -0.5),
        "a_conv": nrm(ks[3], (N_A_LAYERS, A_CONV, A_CONV_WIDTH), A_CONV ** -0.5),
        "a_A_log": jnp.log(jax.random.uniform(ks[4], (N_A_LAYERS, A_HEADS), jnp.float32, minval=1.0, maxval=16.0)),
        "a_dt_bias": dt + jnp.log(-jnp.expm1(-dt)),
        "a_out_norm": 1.0 + nrm(ks[6], (N_A_LAYERS, A_HEAD_V), 0.02),
        "a_w_out": nrm(ks[7], (N_A_LAYERS, A_V_WIDTH, D_MODEL), A_V_WIDTH ** -0.5),
        "kv_norm": 1.0 + nrm(ks[8], (D_MODEL,), 0.02),
        "w_kv": nrm(ks[9], (D_MODEL, 2 * B_WIDTH), D_MODEL ** -0.5),
        "b_norm": 1.0 + nrm(ks[10], (N_B_LAYERS, D_MODEL), 0.02),
        "b_w_q": nrm(ks[11], (N_B_LAYERS, D_MODEL, B_WIDTH), D_MODEL ** -0.5),
        "b_rel_bias": nrm(ks[12], (N_B_LAYERS, B_HEADS, 2 * REL_CLIP + 1), 0.1),
        "b_w_out": nrm(ks[13], (N_B_LAYERS, B_WIDTH, D_MODEL), B_WIDTH ** -0.5),
        "f_norm": 1.0 + nrm(ks[14], (DEPTH, D_MODEL), 0.02),
        "f_w_up": nrm(ks[15], (DEPTH, D_MODEL, 2 * FFN_DIM), D_MODEL ** -0.5),
        "f_conv": nrm(ks[16], (DEPTH, FFN_CONV, 2 * FFN_DIM), FFN_CONV ** -0.5),
        "f_conv_b": nrm(ks[17], (DEPTH, 2 * FFN_DIM), 0.01),
        "f_w_down": nrm(ks[18], (DEPTH, FFN_DIM, D_MODEL), FFN_DIM ** -0.5),
        "final_norm": 1.0 + nrm(ks[19], (D_MODEL,), 0.02),
    }

def first_block(x, a_norm, a_w_in, a_conv, a_A_log, a_dt_bias, a_out_norm, a_w_out,
              kv_norm, w_kv, b_norm, b_w_q, b_rel_bias, b_w_out,
              f_norm, f_w_up, f_conv, f_conv_b, f_w_down, final_norm):
    bsz, seq, _ = x.shape
    h = x
    k_pad = None
    v_pad = None
    for layer in range(DEPTH):
        if layer < N_A_LAYERS:
            i = layer
            h = h + gated_deltanet(rmsnorm(h, a_norm[i]), a_w_in[i], a_conv[i], a_A_log[i],
                                   a_dt_bias[i], a_out_norm[i], a_w_out[i])
        else:
            if layer == N_A_LAYERS:
                kv = rmsnorm(h, kv_norm) @ w_kv
                pad = ((0, 0), (LEFT_CHUNKS * CHUNK, 0), (0, 0), (0, 0))
                k_pad = jnp.pad(kv[..., :B_WIDTH].reshape(bsz, seq, B_HEADS, B_HEAD_DIM), pad)
                v_pad = jnp.pad(kv[..., B_WIDTH:].reshape(bsz, seq, B_HEADS, B_HEAD_DIM), pad)
            j = layer - N_A_LAYERS
            h = h + chunk_attention(rmsnorm(h, b_norm[j]), b_w_q[j], b_rel_bias[j], b_w_out[j], k_pad, v_pad)
        h = h + conv_ffn(rmsnorm(h, f_norm[layer]), f_w_up[layer], f_conv[layer], f_conv_b[layer], f_w_down[layer])
    return rmsnorm(h, final_norm)


N_MIXERS = 2
N_A_LAYERS_2 = (DEPTH + 1) // 2
N_B_LAYERS_2 = DEPTH // 2
NORM_EPS = 1e-5
D_FF = 4 * D_MODEL
N_MOD = 6

S5_WIDTH = D_MODEL
S5_GROUP = 16
S5_GROUPS = S5_WIDTH // S5_GROUP
S5_STATE = 64
S5_CHUNK = 128
S5_DT_MIN = 0.001
S5_DT_MAX = 0.1

M2_D_INNER = 2 * D_MODEL
M2_HEADDIM = 64
M2_HEADS = M2_D_INNER // M2_HEADDIM
M2_GROUPS = 4
M2_HPG = M2_HEADS // M2_GROUPS
M2_STATE = 128
M2_CONV = 4
M2_CHUNK = 128
M2_CONV_DIM = M2_D_INNER + 2 * M2_GROUPS * M2_STATE
M2_IN_DIM = M2_D_INNER + M2_CONV_DIM + M2_HEADS
M2_DT_MIN = 0.001
M2_DT_MAX = 0.1


def _rmsnorm(x, g):
    xf = x.astype(jnp.float32)
    y = xf * lax.rsqrt(jnp.mean(xf * xf, axis=-1, keepdims=True) + NORM_EPS)
    return (y * g.astype(jnp.float32)).astype(x.dtype)

def _modulate(h, shift, scale):
    return h * (1 + scale) + shift

def _sq_relu_mlp(h, w1, w2):
    a = jax.nn.relu(h @ w1)
    return (a * a) @ w2

def _s5_combine(e1, e2):
    a1, b1 = e1
    a2, b2 = e2
    return a2 * a1, a2 * b1 + b2

def _s5_mixer(h, w_in, lam_re, lam_im, log_dt, b_re, b_im, c_re, c_im, d, w_glu, b_glu):
    f32 = jnp.float32
    bsz, L, _ = h.shape
    nc = L // S5_CHUNK
    u = (h @ w_in).astype(f32)
    lam = lax.complex(lam_re.astype(f32), lam_im.astype(f32))
    dt = jnp.exp(log_dt.astype(f32))[:, None]
    lam_dt = lam * dt
    lam_bar = jnp.exp(lam_dt)
    b_bar = ((lam_bar - 1) / lam)[..., None] * lax.complex(b_re.astype(f32), b_im.astype(f32))
    c_mat = lax.complex(c_re.astype(f32), c_im.astype(f32))
    steps = jnp.arange(1, S5_CHUNK + 1, dtype=f32)[:, None, None]
    a_pow = jnp.exp(lam_dt[None] * steps)
    a_elems = jnp.broadcast_to(lam_bar, (bsz, S5_CHUNK, S5_GROUPS, S5_STATE))
    u_blocks = u.reshape(bsz, nc, S5_CHUNK, S5_GROUPS, S5_GROUP).transpose(1, 0, 2, 3, 4)

    def block_step(carry, u_blk):
        bu = jnp.einsum('btgh,gph->btgp', u_blk.astype(jnp.complex64), b_bar)
        _, hs = lax.associative_scan(_s5_combine, (a_elems, bu), axis=1)
        hs = hs + a_pow[None] * carry[:, None]
        y = jnp.einsum('btgp,ghp->btgh', hs, c_mat).real
        return hs[:, -1], y

    carry0 = jnp.zeros((bsz, S5_GROUPS, S5_STATE), jnp.complex64)
    _, ys = lax.scan(block_step, carry0, u_blocks)
    y = ys.transpose(1, 0, 2, 3, 4).reshape(bsz, L, S5_WIDTH) + d.astype(f32) * u
    g = jax.nn.gelu(y)
    ab = g @ w_glu.astype(f32) + b_glu.astype(f32)
    val, gate = jnp.split(ab, 2, axis=-1)
    return (val * jax.nn.sigmoid(gate)).astype(h.dtype)

def _causal_dwconv(u, w):
    return lax.conv_general_dilated(u, w[:, None, :].astype(u.dtype), (1,), [(M2_CONV - 1, 0)],
                                    dimension_numbers=('NWC', 'WIO', 'NWC'),
                                    feature_group_count=u.shape[-1])

def _segsum(a):
    t = a.shape[-1]
    cs = jnp.cumsum(a, axis=-1)
    diff = cs[..., :, None] - cs[..., None, :]
    mask = jnp.tril(jnp.ones((t, t), dtype=bool))
    return jnp.where(mask, diff, -jnp.inf)

def _ssd_mixer(h, w_in, conv_w, conv_b, dt_bias, a_log, d, norm_g, w_out):
    f32 = jnp.float32
    bsz, L, _ = h.shape
    nc = L // M2_CHUNK
    G, R, P, N, Q = M2_GROUPS, M2_HPG, M2_HEADDIM, M2_STATE, M2_CHUNK
    zxbcdt = h @ w_in
    z, xbc, dt_raw = jnp.split(zxbcdt, [M2_D_INNER, M2_D_INNER + M2_CONV_DIM], axis=-1)
    xbc = jax.nn.silu(_causal_dwconv(xbc, conv_w) + conv_b)
    xs, b_in, c_in = jnp.split(xbc, [M2_D_INNER, M2_D_INNER + G * N], axis=-1)
    dt = jax.nn.softplus(dt_raw.astype(f32) + dt_bias.astype(f32))
    a = -jnp.exp(a_log.astype(f32)).reshape(G, R)
    xs = xs.astype(f32).reshape(bsz, nc, Q, G, R, P)
    b_in = b_in.astype(f32).reshape(bsz, nc, Q, G, N)
    c_in = c_in.astype(f32).reshape(bsz, nc, Q, G, N)
    dt = dt.reshape(bsz, nc, Q, G, R)
    xdt = xs * dt[..., None]
    a_dt = jnp.transpose(dt * a, (0, 3, 4, 1, 2))
    a_cs = jnp.cumsum(a_dt, axis=-1)
    l_mat = jnp.exp(_segsum(a_dt))
    cb = jnp.einsum('bclgn,bcsgn->bcgls', c_in, b_in)
    y_diag = jnp.einsum('bcgls,bgrcls,bcsgrp->bclgrp', cb, l_mat, xdt)
    decay_states = jnp.exp(a_cs[..., -1:] - a_cs)
    states = jnp.einsum('bclgn,bgrcl,bclgrp->bcgrpn', b_in, decay_states, xdt)
    chunk_decay = jnp.exp(a_cs[..., -1])

    def carry_step(carry, inp):
        st, dec = inp
        return dec[..., None, None] * carry + st, carry

    _, prev = lax.scan(carry_step, jnp.zeros((bsz, G, R, P, N), f32),
                       (jnp.moveaxis(states, 1, 0), jnp.moveaxis(chunk_decay, -1, 0)))
    prev = jnp.moveaxis(prev, 0, 1)
    y_off = jnp.einsum('bclgn,bcgrpn,bgrcl->bclgrp', c_in, prev, jnp.exp(a_cs))
    y = y_diag + y_off + xs * d.astype(f32).reshape(G, R, 1)
    y = y.reshape(bsz, L, M2_D_INNER) * jax.nn.silu(z.astype(f32))
    yg = y.reshape(bsz, L, G, M2_D_INNER // G)
    yg = yg * lax.rsqrt(jnp.mean(yg * yg, axis=-1, keepdims=True) + NORM_EPS)
    y = yg.reshape(bsz, L, M2_D_INNER) * norm_g.astype(f32)
    return y.astype(h.dtype) @ w_out

def second_inputs(seed: int = 0) -> dict:
    f32 = jnp.float32
    key = jax.random.key(seed)
    it = iter(jax.random.split(key, 28))

    def nrm(shape, scale):
        return scale * jax.random.normal(next(it), shape, f32)

    D, F = D_MODEL, D_FF
    NA, NB = N_A_LAYERS_2, N_B_LAYERS_2
    G, P, H = S5_GROUPS, S5_STATE, S5_GROUP
    x = nrm((BATCH, SEQ, D), 1.0)
    c = nrm((BATCH, D), 1.0)
    ada_w = nrm((DEPTH, D, N_MOD * D), 0.5 * D ** -0.5)
    ada_b = nrm((DEPTH, N_MOD * D), 0.02)
    norm_mix_g = 1.0 + nrm((DEPTH, D), 0.05)
    norm_mlp_g = 1.0 + nrm((DEPTH, D), 0.05)
    mlp_w1 = nrm((DEPTH, D, F), D ** -0.5)
    mlp_w2 = nrm((DEPTH, F, D), F ** -0.5)
    s5_w_in = nrm((NA, D, S5_WIDTH), D ** -0.5)
    s5_lambda_re = -0.5 + nrm((NA, G, P), 0.01)
    s5_lambda_im = math.pi * jnp.arange(P, dtype=f32) + nrm((NA, G, P), 0.01)
    s5_log_dt = jax.random.uniform(next(it), (NA, G), f32, minval=math.log(S5_DT_MIN), maxval=math.log(S5_DT_MAX))
    s5_b_re = nrm((NA, G, P, H), (2 * H) ** -0.5)
    s5_b_im = nrm((NA, G, P, H), (2 * H) ** -0.5)
    s5_c_re = nrm((NA, G, H, P), (2 * P) ** -0.5)
    s5_c_im = nrm((NA, G, H, P), (2 * P) ** -0.5)
    s5_d = nrm((NA, S5_WIDTH), 1.0)
    s5_w_glu = nrm((NA, S5_WIDTH, 2 * D), S5_WIDTH ** -0.5)
    s5_b_glu = nrm((NA, 2 * D), 0.02)
    m2_w_in = nrm((NB, D, M2_IN_DIM), D ** -0.5)
    m2_conv_w = nrm((NB, M2_CONV, M2_CONV_DIM), M2_CONV ** -0.5)
    m2_conv_b = nrm((NB, M2_CONV_DIM), 0.02)
    dt0 = jnp.exp(jax.random.uniform(next(it), (NB, M2_HEADS), f32, minval=math.log(M2_DT_MIN), maxval=math.log(M2_DT_MAX)))
    m2_dt_bias = dt0 + jnp.log(-jnp.expm1(-dt0))
    m2_a_log = jnp.log(jax.random.uniform(next(it), (NB, M2_HEADS), f32, minval=1.0, maxval=16.0))
    m2_d = 1.0 + nrm((NB, M2_HEADS), 0.1)
    m2_norm_g = 1.0 + nrm((NB, M2_D_INNER), 0.05)
    m2_w_out = nrm((NB, M2_D_INNER, D), M2_D_INNER ** -0.5)
    final_norm_g = 1.0 + nrm((D,), 0.05)
    return {'x': x, 'c': c, 'ada_w': ada_w, 'ada_b': ada_b,
            'norm_mix_g': norm_mix_g, 'norm_mlp_g': norm_mlp_g,
            'mlp_w1': mlp_w1, 'mlp_w2': mlp_w2,
            's5_w_in': s5_w_in, 's5_lambda_re': s5_lambda_re, 's5_lambda_im': s5_lambda_im,
            's5_log_dt': s5_log_dt, 's5_b_re': s5_b_re, 's5_b_im': s5_b_im,
            's5_c_re': s5_c_re, 's5_c_im': s5_c_im, 's5_d': s5_d,
            's5_w_glu': s5_w_glu, 's5_b_glu': s5_b_glu,
            'm2_w_in': m2_w_in, 'm2_conv_w': m2_conv_w, 'm2_conv_b': m2_conv_b,
            'm2_dt_bias': m2_dt_bias, 'm2_a_log': m2_a_log, 'm2_d': m2_d,
            'm2_norm_g': m2_norm_g, 'm2_w_out': m2_w_out,
            'final_norm_g': final_norm_g}

def second_block(x, c, ada_w, ada_b, norm_mix_g, norm_mlp_g, mlp_w1, mlp_w2,
              s5_w_in, s5_lambda_re, s5_lambda_im, s5_log_dt, s5_b_re, s5_b_im,
              s5_c_re, s5_c_im, s5_d, s5_w_glu, s5_b_glu,
              m2_w_in, m2_conv_w, m2_conv_b, m2_dt_bias, m2_a_log, m2_d,
              m2_norm_g, m2_w_out, final_norm_g):
    cond = jax.nn.silu(c)
    for i in range(DEPTH):
        mod = cond @ ada_w[i] + ada_b[i]
        sh1, sc1, g1, sh2, sc2, g2 = jnp.split(mod[:, None, :], N_MOD, axis=-1)
        h = _modulate(_rmsnorm(x, norm_mix_g[i]), sh1, sc1)
        j = i // N_MIXERS
        if i % N_MIXERS == 0:
            y = _s5_mixer(h, s5_w_in[j], s5_lambda_re[j], s5_lambda_im[j], s5_log_dt[j],
                          s5_b_re[j], s5_b_im[j], s5_c_re[j], s5_c_im[j], s5_d[j],
                          s5_w_glu[j], s5_b_glu[j])
        else:
            y = _ssd_mixer(h, m2_w_in[j], m2_conv_w[j], m2_conv_b[j], m2_dt_bias[j],
                           m2_a_log[j], m2_d[j], m2_norm_g[j], m2_w_out[j])
        x = x + g1 * y
        h = _modulate(_rmsnorm(x, norm_mlp_g[i]), sh2, sc2)
        x = x + g2 * _sq_relu_mlp(h, mlp_w1[i], mlp_w2[i])
    return _rmsnorm(x, final_norm_g)


def setup_inputs(seed=0):
    out = dict(first_inputs(seed))
    for name, value in second_inputs(seed + 1).items():
        if name != "x":
            out[name + "_2"] = value
    return out


def reference(
    x, a_norm, a_w_in, a_conv, a_A_log, a_dt_bias, a_out_norm, a_w_out, kv_norm, w_kv, b_norm,
    b_w_q, b_rel_bias, b_w_out, f_norm, f_w_up, f_conv, f_conv_b, f_w_down, final_norm, c_2,
    ada_w_2, ada_b_2, norm_mix_g_2, norm_mlp_g_2, mlp_w1_2, mlp_w2_2, s5_w_in_2, s5_lambda_re_2,
    s5_lambda_im_2, s5_log_dt_2, s5_b_re_2, s5_b_im_2, s5_c_re_2, s5_c_im_2, s5_d_2, s5_w_glu_2,
    s5_b_glu_2, m2_w_in_2, m2_conv_w_2, m2_conv_b_2, m2_dt_bias_2, m2_a_log_2, m2_d_2,
    m2_norm_g_2, m2_w_out_2, final_norm_g_2,
):
    x = first_block(
        x, a_norm, a_w_in, a_conv, a_A_log, a_dt_bias, a_out_norm, a_w_out, kv_norm, w_kv,
        b_norm, b_w_q, b_rel_bias, b_w_out, f_norm, f_w_up, f_conv, f_conv_b, f_w_down,
        final_norm,
    )
    return second_block(
        x, c_2, ada_w_2, ada_b_2, norm_mix_g_2, norm_mlp_g_2, mlp_w1_2, mlp_w2_2, s5_w_in_2,
        s5_lambda_re_2, s5_lambda_im_2, s5_log_dt_2, s5_b_re_2, s5_b_im_2, s5_c_re_2, s5_c_im_2,
        s5_d_2, s5_w_glu_2, s5_b_glu_2, m2_w_in_2, m2_conv_w_2, m2_conv_b_2, m2_dt_bias_2,
        m2_a_log_2, m2_d_2, m2_norm_g_2, m2_w_out_2, final_norm_g_2,
    )


_drawn_inputs = setup_inputs


def setup_inputs(seed=0):
    import zlib

    import numpy as np

    out = dict(_drawn_inputs(seed))
    spreads = {}
    factors = {'a_out_norm': 4.13,
     'kv_norm': 8.0,
     'b_norm': 8.0,
     'b_rel_bias': 5.776,
     'f_norm': 2.758,
     'f_conv_b': 5.638,
     'norm_mix_g_2': 2.798,
     's5_lambda_re_2': 64.0,
     's5_lambda_im_2': 50.52,
     's5_log_dt_2': 57.92,
     's5_b_re_2': 64.0,
     's5_b_im_2': 64.0,
     's5_c_re_2': 64.0,
     's5_c_im_2': 64.0,
     's5_b_glu_2': 8.0,
     'm2_conv_b_2': 8.0,
     'm2_d_2': 25.608,
     'm2_norm_g_2': 4.203}
    for name, (base, spread) in spreads.items():
        noise = np.random.default_rng([zlib.crc32(name.encode()), seed]).standard_normal(out[name].shape)
        drawn = base * np.exp(spread * noise) if base else spread * noise
        out[name] = jnp.asarray(drawn.astype(out[name].dtype))
    for name, factor in factors.items():
        out[name] = (out[name] * factor).astype(out[name].dtype)
    return out
```

```python
from contextlib import ExitStack

import numpy as np
import concourse.bass as bass
from concourse import mybir

F32 = mybir.dt.float32
F32R = mybir.dt.float32r
ALU = mybir.AluOpType
ACT = mybir.ActivationFunctionType
AX = mybir.AxisListType

P = 128
T = 512
TT = T // P
D = 1024
KD = D // P
SLOT = 2048
AH = 8
A_W = 1024
F_DIM = 2816
F_TILES = F_DIM // P
F_CHUNKS = (8, 8, 6)
F_START = (0, 8, 16)
BH = 16
BD = 64
EPS1 = 1e-6
NEG = -1e30
EPS2 = 1e-5
S5Q = 8
S5N = 32
D_FF = 4096
M_H = 32
M_P = 64
M_G = 4
M_INNER = 2048
M_TILES = M_INNER // P
XBC_TILES = 24

SLOTS = {}
TOTAL = 0
for _name, _n in (("a_in", 16), ("a_out", 4),
                  ("f0_up0", 8), ("f0_dn0", 4), ("f0_up1", 8), ("f0_dn1", 4), ("f0_up2", 6), ("f0_dn2", 4),
                  ("b_k", 4), ("b_v", 4), ("b_q", 4), ("b_out", 4),
                  ("f1_up0", 8), ("f1_dn0", 4), ("f1_up1", 8), ("f1_dn1", 4), ("f1_up2", 6), ("f1_dn2", 4),
                  ("s_in", 4), ("s_glu", 8), ("p0", 32), ("m_in", 20), ("m_out", 8), ("p1", 32)):
    SLOTS[_name] = TOTAL
    TOTAL += _n

PAR = {}
PAR_N = 0
for _name, _n in (("a_norm", 8), ("kv_norm", 8), ("b_norm", 8), ("f_norm", 16), ("final_norm", 8),
                  ("mix_g", 16), ("mlp_g", 16), ("final_g", 8), ("a_conv", 4 * 24), ("a_out_norm", 1),
                  ("f_conv", 2 * 3 * 44), ("f_conv_b", 2 * 44), ("cond", 8), ("ada_b", 2 * 48),
                  ("s5_d", 8), ("s5_b_glu", 16), ("lam_re", 32), ("lam_im", 32), ("log_dt", 32),
                  ("m_conv", 4 * 24), ("m_conv_b", 24), ("m_d", 16), ("m_norm_g", 16), ("qmask", 4)):
    PAR[_name] = PAR_N
    PAR_N += _n
ROW = {"a_A_log": 0, "a_dt_bias": 8, "m_a_log": 16, "m_dt_bias": 48}
ROW_N = 80


def ge(eng, sem, value):
    if isinstance(value, int) and value <= 0:
        return
    eng.wait_ge(sem, value)


def turns(eng, count, step, body, peel=False, start=0):
    if peel:
        body(start)
        start += step
    if start < count:
        if count - start == step:
            body(start)
        else:
            with eng.Fori(start // step, count // step) as i:
                body(i * step if step > 1 else i)


def ds(start, size):
    return slice(start, start + size) if isinstance(start, int) else bass.ds(start, size)


def build(nc, t, out):
    ctx = ExitStack()
    with ctx:
        def sb(name, shape, dt=F32):
            return ctx.enter_context(nc.sbuf_tensor(name, shape, dt))

        def sem(name):
            return ctx.enter_context(nc.semaphore(name))

        w_raw = [sb(f"w_raw{i}", [P, SLOT]) for i in range(2)]
        w_hi = [sb(f"w_hi{i}", [P, SLOT], F32R) for i in range(2)]
        w_lo = [sb(f"w_lo{i}", [P, SLOT], F32R) for i in range(2)]
        h = sb("h", [P, KD, T])
        par = sb("par", [P, PAR_N])
        rows = sb("rows", [P, ROW_N])
        ident = sb("ident", [P, P])
        triu = sb("triu", [P, P])
        upmask = sb("upmask", [P, P])
        ones = sb("ones", [P, P])
        mod = sb("mod", [P, 2, 48])
        gain = sb("gain", [P, 2, 16])
        cond = sb("cond", [P, 8])
        ncol = sb("ncol", [P, 3, TT])
        eps_col = sb("eps_col", [P, 4])
        nar_hi = sb("nar_hi", [P, KD, 32], F32R)
        nar_lo = sb("nar_lo", [P, KD, 32], F32R)
        arena = nc.sbuf_base
        room = nc.sbuf_usable_end - arena

        def at(name, kb, shape, dt=F32):
            size = 4 * int(np.prod(shape[1:]))
            assert kb * 1024 + size <= room, (name, kb, size, room)
            return nc.alloc_sbuf_tensor_at(name, shape, dt, offset=arena + int(kb * 1024))

        bank = [ctx.enter_context(nc.psum_tensor(f"bank{i}", [P, 512], F32)) for i in range(8)]

        def pcol(name, i=0):
            return par[:, PAR[name] + i:PAR[name] + i + 1] if isinstance(i, int) else par[:, bass.ds(i + PAR[name], 1)]

        raw_landed = [sem("raw_landed0"), sem("raw_landed1")]
        hi_done = sem("hi_done")
        lo_done = sem("lo_done")
        gemm_ready = sem("gemm_ready")
        bank_free = sem("bank_free")
        const_in = sem("const_in")
        x_in = sem("x_in")
        stored = sem("stored")

        lev = at("lev", 128, [P, 7, P])
        x_hi = at("x_hi", 0, [P, KD, T], F32R)
        x_lo = at("x_lo", 16, [P, KD, T], F32R)
        sq = at("sq", 32, [P, 2, T])
        xt = at("xt", 36, [P, 2, T])

        def sp_slots(sp, base, count, load, peel=False):
            def body(i):
                for s in range(2):
                    ge(sp, lo_done, base + i + s - 1)
                    for dst, src in load(i + s, s):
                        sp.dma_start(dst, src).then_inc(raw_landed[s], 16)
            turns(sp, count, 2, body, peel)

        def halves(w, s, col, kt=KD, k0=0):
            hk = kt // 2
            raw = w_raw[s][:, 0:kt * 256].rearrange("p (k n) -> p k n", n=256)
            return [(raw[:, 0:hk, :], w[:, ds(k0, hk), ds(col, 256)]),
                    (raw[:, hk:kt, :], w[:, ds(k0 + hk, kt - hk), ds(col, 256)])]

        def both(w, s, col_a, col_b):
            raw = w_raw[s][:, :].rearrange("p (k g n) -> p k g n", g=2, n=P)
            return [(raw[:, :, 0, :], w[:, :, ds(col_a, P)]), (raw[:, :, 1, :], w[:, :, ds(col_b, P)])]

        def rows_k(w):
            return w.rearrange("(k p) n -> p k n", p=P)

        def landed(n):
            return n * 16 + 32

        def slot_count(name):
            n = list(SLOTS.values()) + [TOTAL]
            k = list(SLOTS).index(name)
            return n[k + 1] - n[k]

        names = list(SLOTS)
        def split_hi(act, n, s, value):
            act.wait_ge(raw_landed[s], value)
            ge(act, gemm_ready, 2 * n - 2)
            act.activation(w_hi[s][:, :], w_raw[s][:, :], ACT.Copy).then_inc(hi_done, 1)

        def act_slots(act, name, evac, first=0, count=None, step=2, base=None, peel=False):
            base = SLOTS[name] if base is None else base
            count = slot_count(name) if count is None else count

            def body(i, ahead=True):
                for s in range(step):
                    n = base + first + i + s
                    if ahead or s < step - 2:
                        split_hi(act, n + 2, s % 2, landed(base + first + i + s - s % 2 + 2))
                    evac(first + i + s, s)
            if isinstance(base, int) and base + first + count == TOTAL:
                turns(act, count - step, step, body, peel)
                body(count - step, ahead=False)
            else:
                turns(act, count, step, body, peel)

        def pool_slots(pool, first, count):
            def body(i):
                for s in range(2):
                    n = first + i + s
                    pool.wait_ge(hi_done, n + 1)
                    ge(pool, gemm_ready, 2 * n - 2)
                    pool.tensor_tensor(w_lo[s][:, :], w_raw[s][:, :], w_hi[s][:, :].bitcast(F32),
                                       ALU.subtract).then_inc(lo_done, 1)
            turns(pool, count, 2, body, peel=first == 0)

        def pe_slot_start(pe, n):
            pe.wait_ge(lo_done, n + 1)
            ge(pe, bank_free, 2 * n - 2)

        def three(pe, dst, hi_l, lo_l, hi_r, lo_r, start, stop):
            pe.matmul(dst, hi_l, hi_r, start=start, stop=False)
            pe.matmul(dst, hi_l, lo_r, start=False, stop=False)
            return pe.matmul(dst, lo_l, hi_r, start=False, stop=stop)

        def first_turn(pe, base, rhs_hi, rhs_lo, ready, kt=KD):
            pe_slot_start(pe, base)
            for k in range(kt):
                pe.wait_ge(*ready(k))
                for o in range(2):
                    c = slice(k * 256 + o * P, k * 256 + o * P + P)
                    mm = three(pe, bank[o][:, :], w_hi[0][:, c], w_lo[0][:, c], rhs_hi[:, k, :], rhs_lo[:, k, :],
                               k == 0, k == kt - 1)
                    if k == kt - 1:
                        mm.then_inc(gemm_ready, 1)
            slot_body(pe, base + 1, rhs_hi, rhs_lo, kt, (1,))(0)

        def projection(pe, name, rhs_hi, rhs_lo, ready, kt=KD, count=None, base=None):
            base = SLOTS[name] if base is None else base
            first_turn(pe, base, rhs_hi, rhs_lo, ready, kt)
            turns(pe, slot_count(name) if count is None else count, 2, slot_body(pe, base, rhs_hi, rhs_lo, kt), start=2)

        def normed(lots):
            return lambda k: (n_lo, KD * lots + k + 1)

        def slot_body(pe, base, rhs_hi, rhs_lo, kt=KD, parities=(0, 1)):
            def body(i):
                for s in parities:
                    pe_slot_start(pe, base + i + (s - parities[0]))
                    for o in range(2):
                        for k in range(kt):
                            c = slice(k * 256 + o * P, k * 256 + o * P + P)
                            mm = three(pe, bank[2 * s + o][:, :], w_hi[s][:, c], w_lo[s][:, c],
                                       rhs_hi[:, k, :], rhs_lo[:, k, :], k == 0, k == kt - 1)
                        mm.then_inc(gemm_ready, 1)
            return body

        n_sq, n_ss, n_var, n_std, n_rcp = sem("n_sq"), sem("n_ss"), sem("n_var"), sem("n_std"), sem("n_rcp")
        n_acc = sem("n_acc")
        n_bc, n_xt, n_hi, n_lo = sem("n_bc"), sem("n_xt"), sem("n_hi"), sem("n_lo")
        hn_sq, hn_ss, hn_var, hn_std, hn_rcp = sem("hn_sq"), sem("hn_ss"), sem("hn_var"), sem("hn_std"), sem("hn_rcp")
        hn_hi, hn_lo = sem("hn_hi"), sem("hn_lo")
        tap_first, tap_mid = sem("tap_first"), sem("tap_mid")
        SS = bank[4][:, 0:TT]
        RSTD = bank[5][:, :]

        SQ_X = (at("sq_x", 0, [P, 2, T]), at("sq_x_sum", 4, [P, T]))
        SQ_B = (sq, at("sq_sum", 36, [P, T]))

        def squares_start(dve, c, sqs):
            ge(dve, n_ss, c)
            dve.memset(sqs[1][:, :], 0.0).then_inc(n_acc, 1)

        def squares(dve, c, k, sqs, done):
            acc = 9 * c + 1
            for o in range(2):
                dve.wait_ge(*done(o))
                dve.wait_ge(n_acc, k + (acc - 1 + o))
                hk = h[:, ds(k + o, 1), :]
                dve.tensor_tensor(sqs[0][:, o, :], hk, hk, ALU.mult).then_inc(n_sq, 1)
            for o in range(2):
                dve.wait_ge(n_sq, k + (KD * c + o + 1))
                dve.wait_ge(n_acc, k + (acc + o))
                dve.tensor_tensor(sqs[1][:, :], sqs[1][:, :], sqs[0][:, o, :], ALU.add).then_inc(n_acc, 1)

        def norm_pe(pe, c, sqs):
            pe.wait_ge(n_acc, 9 * (c + 1))
            for j in range(TT):
                mm = pe.matmul(bank[4][:, j:j + 1], sqs[1][:, j * P:j * P + P], ones[:, 0:1], start=True, stop=True)
            mm.then_inc(n_ss, 1)
            pe.wait_ge(n_rcp, c + 1)
            for j in range(TT):
                mm = pe.matmul(bank[5][:, j * P:j * P + P], ncol[:, 2, j:j + 1].to_broadcast([P, P]), ident[:, :],
                               start=True, stop=True)
            mm.then_inc(n_bc, 1)

        def norm_hi(act, lots, slot, shift=None):
            ge(act, gemm_ready, 2 * slot)
            for k in range(KD):
                act.wait_ge(n_xt, KD * lots + k + 1)
                if shift is None:
                    act.activation(x_hi[:, k, :], xt[:, k % 2, :], ACT.Copy).then_inc(n_hi, 1)
                else:
                    act.activation(x_hi[:, k, :], xt[:, k % 2, :], ACT.Identity, bias=shift(k)).then_inc(n_hi, 1)

        def norm_act(act, c, lots, shift=None, split=True, slot=0):
            act.wait_ge(n_var, c + 1)
            act.activation(ncol[:, 1, :], ncol[:, 0, :], ACT.Sqrt).then_inc(n_std, 1)
            if split:
                norm_hi(act, lots, slot, shift)

        def norm_root(dve, c, eps):
            dve.wait_ge(n_ss, c + 1)
            dve.tensor_scalar(ncol[:, 0, :], SS, 1.0 / D, eps, ALU.mult, ALU.add).then_inc(n_var, 1)
            dve.wait_ge(n_std, c + 1)
            dve.reciprocal(ncol[:, 2, :], ncol[:, 1, :]).then_inc(n_rcp, 1)
            dve.wait_ge(n_bc, c + 1)

        def norm_dve(dve, c, lots, g, eps, shift=None, slot=0, root=True):
            if root:
                norm_root(dve, c, eps)
            ge(dve, gemm_ready, 2 * slot)

            def low(k):
                dve.wait_ge(n_hi, KD * lots + k + 1)
                if shift is None:
                    dve.tensor_tensor(x_lo[:, k, :], xt[:, k % 2, :], x_hi[:, k, :].bitcast(F32),
                                      ALU.subtract).then_inc(n_lo, 1)
                else:
                    dve.scalar_tensor_tensor(x_lo[:, k, :], xt[:, k % 2, :], shift(k), x_hi[:, k, :].bitcast(F32),
                                             ALU.add, ALU.subtract).then_inc(n_lo, 1)
            for k in range(KD):
                if k >= 2:
                    dve.wait_ge(n_lo, KD * lots + k - 1)
                dve.scalar_tensor_tensor(xt[:, k % 2, :], h[:, k, :], g(k), RSTD, ALU.mult, ALU.mult).then_inc(n_xt, 1)
                if k >= 1:
                    low(k - 1)
            low(KD - 1)

        def add_h(dve, base, i, s):
            for o in range(2):
                dve.wait_ge(gemm_ready, 2 * (base + i) + o + 1)
                hk = h[:, ds(i * 2 + o, 1), :]
                dve.tensor_tensor(hk, bank[2 * s + o][:, :], hk, ALU.add).then_inc(bank_free, 1)

        x_tok = at("x_tok", 40, [P, TT, D])
        x_t, h_in = sem("x_t"), sem("h_in")

        def load_sp(sp):
            sp.dma_start(x_tok[:, :, :], t["x"].rearrange("b (c p) d -> p (b c) d", p=P)).then_inc(x_in, 16)
            sp.dma_start(ident[:, :], t["ident"]).then_inc(const_in, 16)
            sp.dma_start(par[:, :], t["par"]).then_inc(const_in, 16)
            sp.dma_start(triu[:, :], t["triu"]).then_inc(const_in, 16)
            sp.dma_start(upmask[:, :], t["upmask"]).then_inc(const_in, 16)
            sp.dma_start(lev[:, :, :], t["lev"]).then_inc(const_in, 16)
            sp.dma_start(rows[:, :], t["rows"].partition_broadcast(P)).then_inc(const_in, 16)
            sp.dma_start(nar_raw[:, :, 0:16], t["a_w_in"].rearrange("b (k p) n -> p (b k) n", p=P)[:, :, 4096:4112]).then_inc(const_in, 16)

        CONST = 16 * 7
        ones_set = sem("ones_set")

        def load_pe(pe):
            pe.wait_ge(x_in, 16)
            pe.wait_ge(const_in, CONST)
            for k in range(KD):
                if k >= 4:
                    pe.wait_ge(h_in, k - 3)
                for c in range(TT):
                    mm = pe.transpose(bank[4 + k % 4][:, c * P:c * P + P], x_tok[:, c, k * P:k * P + P], ident[:, :])
                mm.then_inc(x_t, 1)

        def load_act(act):
            act.wait_ge(const_in, CONST)
            act.wait_ge(ones_set, 4)
            narrow_hi_act(act)
            act.activation(cond[:, :], par[:, PAR["cond"]:PAR["cond"] + 8], ACT.Silu).then_inc(cond_in, 1)
            for k in range(KD):
                act.wait_ge(x_t, k + 1)
                act.activation(h[:, k, :], bank[4 + k % 4][:, :], ACT.Copy).then_inc(h_in, 1)

        cond_in = sem("cond_in")

        def load_dve(dve):
            dve.memset(ones[:, :], 1.0).then_inc(ones_set, 1)
            dve.memset(eps_col[:, 0:1], EPS1).then_inc(ones_set, 1)
            dve.memset(eps_col[:, 1:2], float(np.pi / 2)).then_inc(ones_set, 1)
            dve.memset(nar_raw[:, :, 16:32], 0.0).then_inc(ones_set, 1)
            narrow_lo_dve(dve, 1)
            squares_start(dve, 0, SQ_B)
            for k in range(0, KD, 2):
                squares(dve, 0, k, SQ_B, lambda o: (h_in, k + o + 1))

        qkvz = at("qkvz", 40, [P, 32, T])
        ba_ready = sem("ba_ready")
        silu_done = sem("silu_done")
        BA = bank[6][:, 0:TT * 16].rearrange("p (c n) -> p c n", n=16)

        def qkv(j, a=0, b=T):
            return qkvz[:, ds(j, 1), a:b]

        nar_raw = at("nar_raw", 124, [P, KD, 32])
        nar = at("nar", 122, [32, T])
        nar_split, nar_proj, nar_out = sem("nar_split"), sem("nar_proj"), sem("nar_out")

        def narrow_pe(pe, nth):
            pe.wait_ge(nar_split, 2 * nth)
            for k in range(KD):
                mm = three(pe, bank[7][0:32, :], nar_hi[:, k, :], nar_lo[:, k, :], x_hi[:, k, :], x_lo[:, k, :],
                           k == 0, k == KD - 1)
            mm.then_inc(nar_proj, 1)

        def narrow_turn_pe(pe, nth, dst, n, done):
            pe.wait_ge(nar_out, nth)
            for c in range(TT):
                mm = pe.matmul(dst[:, c, :], nar[:, c * P:c * P + P], ident[0:32, 0:n], start=True, stop=True)
            mm.then_inc(done, 1)

        def narrow_hi_act(act):
            act.activation(nar_hi[:, :, :], nar_raw[:, :, :], ACT.Copy).then_inc(nar_split, 1)

        def narrow_lo_dve(dve, nth):
            dve.wait_ge(nar_split, 2 * nth - 1)
            dve.tensor_tensor(nar_lo[:, :, :], nar_raw[:, :, :], nar_hi[:, :, :].bitcast(F32),
                              ALU.subtract).then_inc(nar_split, 1)

        def narrow_out_act(act, nth):
            act.wait_ge(nar_proj, nth)
            act.activation(nar[:, :], bank[7][0:32, :], ACT.Copy).then_inc(nar_out, 1)

        def a_in_sp(sp):
            w = rows_k(t["a_w_in"][0])
            sp_slots(sp, 0, 16, lambda i, s: halves(w, s, i * 256), peel=True)

        def a_in_pe(pe):
            first_turn(pe, 0, x_hi, x_lo, normed(0))
            narrow_pe(pe, 1)
            body = slot_body(pe, 0, x_hi, x_lo)
            body(2)
            narrow_turn_pe(pe, 1, BA, 16, ba_ready)
            turns(pe, 16, 2, body, start=4)

        def a_in_act(act):
            def silu(j):
                for o in range(2):
                    act.activation(qkv(j + o), qkv(j + o), ACT.Silu).then_inc(silu_done, 1)

            def conv(i, s):
                for o in range(2):
                    act.wait_ge(gemm_ready, 2 * i + o + 1)
                    act.activation(qkv(2 * i + o), bank[2 * s + o][:, :], ACT.Copy,
                                   scale=pcol("a_conv", 3 * 24 + 2 * i + o)).then_inc(tap_first, 1)
                if not (isinstance(i, int) and i == 0):
                    act.wait_ge(bank_free, 2 * i)
                    silu(2 * i - 2)

            def gate(i, s):
                for o in range(2):
                    act.wait_ge(gemm_ready, 2 * i + o + 1)
                    act.activation(qkv(2 * i + o), bank[2 * s + o][:, :], ACT.Silu).then_inc(bank_free, 1)
            act_slots(act, "a_in", conv, 0, 2, peel=True)
            narrow_out_act(act, 1)
            act_slots(act, "a_in", conv, 2, 10)
            act.wait_ge(bank_free, 24)
            silu(22)
            act_slots(act, "a_in", gate, 12, 4)

        def a_in_dve(dve):
            def body(i):
                for s in range(2):
                    for o in range(2):
                        j = 2 * (i + s) + o
                        dve.wait_ge(tap_first, j + 1)
                        for d in (1, 2, 3):
                            if d > 1:
                                dve.wait_ge(tap_mid, 2 * j + d - 1)
                            dve.scalar_tensor_tensor(qkv(j, d), bank[2 * s + o][:, 0:T - d], pcol("a_conv", (3 - d) * 24 + j),
                                                     qkv(j, d), ALU.mult, ALU.add).then_inc(tap_mid if d < 3 else bank_free, 1)
            turns(dve, 12, 2, body)

        gcols = at("gcols", 131.5, [P, 14, 32])

        def gc(n):
            return gcols[:, n, :].rearrange("p (c h) -> p c h", h=AH)
        BETA, A_X, A_ABS, A_E, A_U, A_L, A_G, GCUM, GEND, EGC, EDX, DEC, NBG, EXPA = range(14)
        sp_d, sp_a = sem("softplus_dve"), sem("softplus_act")
        g_pe, g_act, g_dve = sem("gates_pe"), sem("gates_act"), sem("gates_dve")

        def softplus_dve(dve, base, x, ab, e, u, l, res, d0, a0):
            dve.scalar_tensor_tensor(ab, x, -1.0, x, ALU.mult, ALU.min).then_inc(sp_d, 1)
            dve.wait_ge(sp_a, a0 + 1)
            dve.tensor_scalar(u, e, 1.0, None, ALU.add).then_inc(sp_d, 1)
            dve.wait_ge(sp_d, d0 + 2)
            dve.scalar_tensor_tensor(e, u, -1.0, e, ALU.add, ALU.subtract).then_inc(sp_d, 1)
            dve.wait_ge(sp_a, a0 + 2)
            dve.reciprocal(u, u).then_inc(sp_d, 1)
            dve.wait_ge(sp_d, d0 + 4)
            dve.tensor_tensor(e, e, u, ALU.mult).then_inc(sp_d, 1)
            dve.scalar_tensor_tensor(l, x, 0.0, l, ALU.max, ALU.add).then_inc(sp_d, 1)
            dve.wait_ge(sp_d, d0 + 6)
            dve.tensor_tensor(res, l, e, ALU.subtract).then_inc(sp_d, 1)

        def softplus_act(act, ab, e, u, l, d0):
            act.wait_ge(sp_d, d0 + 1)
            act.activation(e, ab, ACT.Exp).then_inc(sp_a, 1)
            act.wait_ge(sp_d, d0 + 2)
            act.activation(l, u, ACT.Ln).then_inc(sp_a, 1)

        def gates_dve(dve):
            dve.wait_ge(ba_ready, 1)
            dve.tensor_tensor(gc(A_X), BA[:, :, 8:16], rows[:, 8:16].unsqueeze(1).to_broadcast([P, TT, AH]),
                              ALU.add).then_inc(g_dve, 1)
            dve.wait_ge(g_dve, 1)
            softplus_dve(dve, 0, gc(A_X), gc(A_ABS), gc(A_E), gc(A_U), gc(A_L), gc(A_G), 0, 0)
            dve.wait_ge(sp_d, 7)
            dve.wait_ge(g_act, 2)
            dve.scalar_tensor_tensor(gc(A_G), gc(A_G), -1.0, gcols[:, EXPA, 0:AH].unsqueeze(1).to_broadcast([P, TT, AH]),
                                     ALU.mult, ALU.mult).then_inc(g_dve, 1)
            dve.wait_ge(g_pe, 1)
            dve.tensor_copy(gcols[:, GCUM, :], bank[7][:, 0:32]).then_inc(g_dve, 1)
            dve.tensor_copy(gcols[:, GEND, :], bank[7][:, 32:64]).then_inc(g_dve, 1)
            dve.wait_ge(g_dve, 4)
            dve.tensor_tensor(gcols[:, EDX, :], gcols[:, GEND, :], gcols[:, GCUM, :], ALU.subtract).then_inc(g_dve, 1)
            dve.wait_ge(g_act, 5)
            dve.scalar_tensor_tensor(gcols[:, NBG, :], gcols[:, BETA, :], -1.0, gcols[:, EGC, :],
                                     ALU.mult, ALU.mult).then_inc(g_dve, 1)

        def gates_act(act):
            act.wait_ge(ba_ready, 1)
            act.wait_ge(g_dve, 1)
            act.activation(gc(BETA), BA[:, :, 0:8], ACT.Sigmoid).then_inc(g_act, 1)
            act.activation(gcols[:, EXPA, 0:AH], rows[:, 0:8], ACT.Exp).then_inc(g_act, 1)
            softplus_act(act, gc(A_ABS), gc(A_E), gc(A_U), gc(A_L), 0)
            act.wait_ge(g_dve, 5)
            act.activation(gcols[:, EGC, :], gcols[:, GCUM, :], ACT.Exp).then_inc(g_act, 1)
            act.activation(gcols[:, EDX, :], gcols[:, EDX, :], ACT.Exp).then_inc(g_act, 1)
            act.activation(gcols[:, DEC, :], gcols[:, GEND, :], ACT.Exp).then_inc(g_act, 1)

        def gates_pe(pe):
            pe.wait_ge(g_dve, 2)
            pe.matmul(bank[7][:, 0:32], triu[:, :], gcols[:, A_G, :], start=True, stop=True)
            pe.matmul(bank[7][:, 32:64], ones[:, :], gcols[:, A_G, :], start=True, stop=True).then_inc(g_pe, 1)

        l_bc, l_done = sem("l_bc"), sem("l_done")
        lcol = at("lcol", 120, [P, 3, 64])
        LSS = bank[4][:, 0:64]

        def unit_pe(pe):
            for j in range(16):
                pe.wait_ge(hn_sq, j + 1)
                for c in range(TT):
                    mm = pe.matmul(bank[4][:, j * 4 + c:j * 4 + c + 1], sq[:, j % 2, c * P:c * P + P], ones[:, 0:1],
                                   start=(j == 0 and c == 0), stop=True, skip_group_check=True)
                mm.then_inc(hn_ss, 1)
            pe.wait_ge(hn_rcp, 1)
            for j in range(16):
                ge(pe, l_done, j - 1)
                for c in range(TT):
                    mm = pe.matmul(bank[5 + j % 2][:, c * P:c * P + P],
                                   lcol[:, 2, j * 4 + c:j * 4 + c + 1].to_broadcast([P, P]), ident[:, :],
                                   start=True, stop=True)
                mm.then_inc(l_bc, 1)

        def unit_act(act):
            act.wait_ge(silu_done, 24)
            for j in range(16):
                ge(act, hn_ss, j - 1)
                act.activation(sq[:, j % 2, :], qkvz[:, j, :], ACT.Square).then_inc(hn_sq, 1)
            act.wait_ge(hn_var, 2)
            act.activation(lcol[:, 1, :], lcol[:, 0, :], ACT.Sqrt).then_inc(hn_std, 1)

        def unit_dve(dve):
            dve.wait_ge(hn_ss, 16)
            dve.tensor_scalar(lcol[:, 0, 0:32], LSS[:, 0:32], 1e-6, float(P), ALU.add, ALU.mult).then_inc(hn_var, 1)
            dve.tensor_scalar(lcol[:, 0, 32:64], LSS[:, 32:64], 1e-6, None, ALU.add).then_inc(hn_var, 1)
            dve.wait_ge(hn_std, 1)
            dve.reciprocal(lcol[:, 2, :], lcol[:, 1, :]).then_inc(hn_rcp, 1)

            def body(j):
                for s in range(2):
                    dve.wait_ge(l_bc, j + s + 1)
                    dve.tensor_tensor(qkv(j + s), qkv(j + s), bank[5 + s][:, :], ALU.mult).then_inc(l_done, 1)
            turns(dve, 16, 2, body)

        Uall = at("Uall", 0, [P, AH, TT, P])
        Aall = at("Aall", 16, [P, AH, TT, P])
        Kend = at("Kend", 104, [P, AH, TT, P])
        X1 = [at(f"X1_{s}", 32 + 2 * s, [P, TT, P]) for s in range(2)]
        X2 = [at(f"X2_{s}", 36 + 2 * s, [P, TT, P]) for s in range(2)]
        Rm = [at(f"Rm_{s}", 120 + 2 * s, [P, TT, P]) for s in range(2)]
        Vm = [at(f"Vm_{s}", 124 + 2 * s, [P, TT, P]) for s in range(2)]
        (da_gb, da_kk, da_qk, da_bb, da_dt, da_eg, da_ex, da_r1, da_a, da_r, da_qd, da_vt, da_rv, da_kt, da_kend,
         da_mask, da_tr, da_p1, da_p1c, da_tv, da_tu, da_v, da_u) = (sem("da_" + n) for n in (
             "gb kk qk bb dt eg ex r1 a r qd vt rv kt kend mask tr p1 p1c tv tu v u".split()))

        def c4(x):
            return x[:, :].rearrange("p (c i) -> p c i", c=TT)

        def bc4(x):
            return x.unsqueeze(1).to_broadcast([P, TT, P])

        def hd(buf, j):
            return buf[:, ds(j, 1), :, :]

        def inside_pe(pe):
            pe.wait_ge(g_dve, 6)
            pe.wait_ge(l_done, 16)
            for i in range(AH // 2):
                for s in range(2):
                    j = 2 * i + s
                    ge(pe, da_u, 14 * i - 1 + s if i else 0)
                    ge(pe, da_kend, j - 1)
                    b = bank[4 * s:4 * s + 4]
                    for c in range(TT):
                        mm = pe.matmul(c4(b[0])[:, c, :], gc(A_G)[:, c, j:j + 1].to_broadcast([P, P]), triu[:, :],
                                       start=True, stop=True)
                    mm.then_inc(da_gb, 1)
                    for c in range(TT):
                        kc = qkvz[:, 8 + j, c * P:c * P + P]
                        mm = pe.matmul(c4(b[1])[:, c, :], kc, kc, start=True, stop=True)
                    mm.then_inc(da_kk, 1)
                    for c in range(TT):
                        mm = pe.matmul(c4(b[2])[:, c, :], qkvz[:, 8 + j, c * P:c * P + P], qkvz[:, j, c * P:c * P + P],
                                       start=True, stop=True)
                    mm.then_inc(da_qk, 1)
                    for c in range(TT):
                        mm = pe.matmul(c4(b[3])[:, c, :], gc(BETA)[:, c, j:j + 1].to_broadcast([P, P]), ident[:, :],
                                       start=True, stop=True)
                    mm.then_inc(da_bb, 1)
                for s in range(2):
                    j = 2 * i + s
                    pe.wait_ge(da_r1, j + 1)
                    for c in range(TT):
                        mm = pe.transpose(c4(bank[4 * s + 3])[:, c, :], qkvz[:, 16 + j, c * P:c * P + P], ident[:, :])
                    mm.then_inc(da_vt, 1)
                for s in range(2):
                    pe.wait_ge(da_mask, 14 * i + s + 1)
                    for c in range(TT):
                        mm = pe.transpose(c4(bank[4 * s + 1])[:, c, :], X2[s][:, c, :], ident[:, :])
                    mm.then_inc(da_tr, 1)
                for s in range(2):
                    j = 2 * i + s
                    pe.wait_ge(da_rv, j + 1)
                    for c in range(TT):
                        mm = pe.transpose(c4(bank[4 * s + 3])[:, c, :], qkvz[:, 8 + j, c * P:c * P + P], ident[:, :])
                    mm.then_inc(da_kt, 1)
                for l in range(1, 7):
                    for s in range(2):
                        pe.wait_ge(da_mask, 14 * i + 2 * l + s + 1)
                        pe.wait_ge(da_v, 12 * i + 2 * (l - 1) + s + 1)
                        if l > 1:
                            pe.wait_ge(da_p1c, 12 * i + 2 * (l - 2) + s + 1)
                        else:
                            pe.wait_ge(da_eg, 2 * i + s + 1)
                        for c in range(TT):
                            mm = pe.matmul(c4(bank[4 * s])[:, c, :], X2[s][:, c, :], Vm[s][:, c, :], start=True, stop=True)
                        mm.then_inc(da_p1, 1)
                    for s in range(2):
                        j = 2 * i + s
                        pe.wait_ge(da_p1c, 12 * i + 2 * (l - 1) + s + 1)
                        pe.wait_ge(da_u, 14 * i + 2 * (l - 1) + s + 1)
                        if l == 1:
                            pe.wait_ge(da_a, j + 1)
                        if l < 6:
                            for c in range(TT):
                                mm = pe.matmul(c4(bank[4 * s + 1])[:, c, :], Uall[:, j, c, :], X1[s][:, c, :],
                                               start=True, stop=True)
                            mm.then_inc(da_tv, 1)
                        for c in range(TT):
                            mm = pe.matmul(c4(bank[4 * s + 2])[:, c, :], X1[s][:, c, :], Uall[:, j, c, :],
                                           start=True, stop=True)
                        mm.then_inc(da_tu, 1)

        def inside_act(act):
            def body(j):
                for s in range(2):
                    act.wait_ge(da_dt, j + s + 1)
                    ge(act, da_mask, 7 * j - 1 + s if not isinstance(j, int) or j else 0)
                    ge(act, da_p1, 6 * j - 1 + s if not isinstance(j, int) or j else 0)
                    act.activation(X2[s][:, :, :], c4(bank[4 * s]), ACT.Exp).then_inc(da_eg, 1)
                    act.activation(X1[s][:, :, :], X1[s][:, :, :], ACT.Exp).then_inc(da_ex, 1)
                for l in range(1, 7):
                    for s in range(2):
                        act.wait_ge(da_p1, 6 * j + 2 * (l - 1) + s + 1)
                        if l == 1:
                            act.wait_ge(da_a, j + s + 1)
                        else:
                            act.wait_ge(da_tu, 6 * j + 2 * (l - 2) + s + 1)
                        act.activation(X1[s][:, :, :], c4(bank[4 * s]), ACT.Copy).then_inc(da_p1c, 1)
            turns(act, AH, 2, body, peel=True)

        def inside_pool(pool):
            def body(j):
                for s in range(2):
                    pool.wait_ge(da_eg, j + s + 1)
                    pool.wait_ge(da_qk, j + s + 1)
                    pool.tensor_tensor(qkv(j + s), qkv(j + s), X2[s][:, :, :].rearrange("p c i -> p (c i)"),
                                       ALU.mult).then_inc(da_qd, 1)
                for l in range(7):
                    for s in range(2):
                        if l == 0:
                            pool.wait_ge(da_r, j + s + 1)
                            pool.wait_ge(da_qd, j + s + 1)
                        elif l == 1:
                            pool.wait_ge(da_tr, j + s + 1)
                            pool.wait_ge(da_u, 7 * j + s + 1)
                        else:
                            pool.wait_ge(da_p1, 6 * j + 2 * (l - 2) + s + 1)
                        pool.tensor_tensor(X2[s][:, :, :], Rm[s][:, :, :], bc4(lev[:, l, :]), ALU.mult).then_inc(da_mask, 1)
            turns(pool, AH, 2, body, peel=False)

        def inside_dve(dve):
            def body(j):
                first = isinstance(j, int) and j == 0
                for s in range(2):
                    dve.wait_ge(da_gb, j + s + 1)
                    if not first:
                        dve.wait_ge(da_tu, 6 * j - 1 + s)
                    for c in range(TT):
                        op = dve.scalar_tensor_tensor(X1[s][:, c, :], c4(bank[4 * s])[:, c, :], gc(GCUM)[:, c, ds(j + s, 1)],
                                                      upmask[:, :], ALU.subtract, ALU.add)
                    op.then_inc(da_dt, 1)
                for s in range(2):
                    dve.wait_ge(da_ex, j + s + 1)
                    dve.wait_ge(da_bb, j + s + 1)
                    if not first:
                        dve.wait_ge(da_mask, 7 * j - 1 + s)
                    dve.tensor_tensor(Rm[s][:, :, :], X1[s][:, :, :], c4(bank[4 * s + 3]), ALU.mult).then_inc(da_r1, 1)
                    dve.wait_ge(da_qk, j + s + 1)
                    dve.tensor_tensor(hd(Aall, j + s), c4(bank[4 * s + 2]), X1[s][:, :, :], ALU.mult).then_inc(da_a, 1)
                    dve.wait_ge(da_kk, j + s + 1)
                    dve.wait_ge(da_r1, j + s + 1)
                    dve.tensor_tensor(Rm[s][:, :, :], c4(bank[4 * s + 1]), Rm[s][:, :, :], ALU.mult).then_inc(da_r, 1)
                for s in range(2):
                    dve.wait_ge(da_vt, j + s + 1)
                    dve.tensor_tensor(qkv(j + s + 16).rearrange("p o (c i) -> p (o c) i", c=TT), c4(bank[4 * s + 3]),
                                      gc(BETA)[:, :, ds(j + s, 1)].to_broadcast([P, TT, P]), ALU.mult).then_inc(da_rv, 1)
                for s in range(2):
                    dve.wait_ge(da_mask, 7 * j + s + 1)
                    dve.tensor_tensor(hd(Uall, j + s), bc4(ident[:, :]), X2[s][:, :, :], ALU.subtract).then_inc(da_u, 1)
                    dve.wait_ge(da_tr, j + s + 1)
                    dve.tensor_tensor(Vm[s][:, :, :], bc4(ident[:, :]), c4(bank[4 * s + 1]), ALU.subtract).then_inc(da_v, 1)
                for s in range(2):
                    dve.wait_ge(da_kt, j + s + 1)
                    dve.tensor_tensor(hd(Kend, j + s), c4(bank[4 * s + 3]), gc(EDX)[:, :, ds(j + s, 1)].to_broadcast([P, TT, P]),
                                      ALU.mult).then_inc(da_kend, 1)
                for l in range(1, 7):
                    for s in range(2):
                        if l < 6:
                            dve.wait_ge(da_tv, 5 * j + 2 * (l - 1) + s + 1)
                            dve.wait_ge(da_v, 6 * j + 2 * (l - 1) + s + 1)
                            dve.tensor_tensor(Vm[s][:, :, :], Vm[s][:, :, :], c4(bank[4 * s + 1]), ALU.subtract).then_inc(da_v, 1)
                        dve.wait_ge(da_tu, 6 * j + 2 * (l - 1) + s + 1)
                        dve.wait_ge(da_u, 7 * j + 2 * (l - 1) + s + 1)
                        dve.tensor_tensor(hd(Uall, j + s), hd(Uall, j + s), c4(bank[4 * s + 2]), ALU.subtract).then_inc(da_u, 1)
            turns(dve, AH, 2, body, peel=True)

        Sst = at("Sst", 120, [P, AH, P])
        Vnew = [at(f"Vnew{g}", 124 + 2 * g, [P, 4, P]) for g in range(2)]
        b_s, b_p, b_r, b_vn, b_vc, b_o, b_oc, b_su = (sem("b_" + n) for n in "s p r vn vc o oc su".split())

        def across_pe(pe):
            pe.wait_ge(da_u, 56)
            pe.wait_ge(da_qd, 8)
            pe.wait_ge(da_kend, 8)
            for c in range(TT):
                tc = slice(c * P, c * P + P)
                for g in range(2):
                    m = 2 * c + g
                    pe.wait_ge(b_s, m + 1)
                    if c:
                        pe.wait_ge(b_r, 2 * c + g - 1)
                    for q in range(4):
                        mm = pe.matmul(c4(bank[4 * g])[:, q, :], qkvz[:, 8 + 4 * g + q, tc], Sst[:, 4 * g + q, :],
                                       start=True, stop=True)
                    mm.then_inc(b_p, 1)
                for g in range(2):
                    m = 2 * c + g
                    pe.wait_ge(b_r, m + 1)
                    for q in range(4):
                        j = 4 * g + q
                        mm = pe.matmul(c4(bank[4 * g + 1])[:, q, :], Uall[:, j, c, :], qkvz[:, 16 + j, tc],
                                       start=True, stop=True)
                    mm.then_inc(b_vn, 1)
                for g in range(2):
                    m = 2 * c + g
                    pe.wait_ge(b_vc, m + 1)
                    if c:
                        pe.wait_ge(b_oc, m - 1)
                    for q in range(4):
                        mm = pe.matmul(c4(bank[4 * g + 3])[:, q, :], Kend[:, 4 * g + q, c, :], Vnew[g][:, q, :],
                                       start=True, stop=True)
                    mm.then_inc(b_su, 1)
                    for q in range(4):
                        j = 4 * g + q
                        pe.matmul(c4(bank[4 * g + 2])[:, q, :], Vnew[g][:, q, :], Aall[:, j, c, :], start=True, stop=False)
                        mm = pe.matmul(c4(bank[4 * g + 2])[:, q, :], Sst[:, j, :], qkvz[:, j, tc], start=False, stop=True)
                    mm.then_inc(b_o, 1)

        def across_dve(dve):
            dve.wait_ge(da_u, 56)
            dve.wait_ge(da_tu, 48)
            for g in range(2):
                dve.memset(Sst[:, 4 * g:4 * g + 4, :], 0.0).then_inc(b_s, 1)
            for c in range(TT):
                tc = slice(c * P, c * P + P)
                for g in range(2):
                    m = 2 * c + g
                    dve.wait_ge(b_p, m + 1)
                    for q in range(4):
                        j = 4 * g + q
                        rv = qkvz[:, 16 + j, tc]
                        op = dve.scalar_tensor_tensor(rv, c4(bank[4 * g])[:, q, :], gc(NBG)[:, c, j:j + 1], rv,
                                                      ALU.mult, ALU.add)
                    op.then_inc(b_r, 1)
                for g in range(2):
                    m = 2 * c + g
                    dve.wait_ge(b_su, m + 1)
                    dve.wait_ge(b_o, m + 1)
                    dve.wait_ge(b_s, m + 1)
                    for q in range(4):
                        j = 4 * g + q
                        op = dve.scalar_tensor_tensor(Sst[:, j, :], Sst[:, j, :], gc(DEC)[:, c, j:j + 1],
                                                      c4(bank[4 * g + 3])[:, q, :], ALU.mult, ALU.add)
                    op.then_inc(b_s, 1)

        def across_act(act):
            act.wait_ge(da_u, 56)
            for c in range(TT):
                tc = slice(c * P, c * P + P)
                for g in range(2):
                    m = 2 * c + g
                    act.wait_ge(b_vn, m + 1)
                    ge(act, b_o, m - 1)
                    act.activation(Vnew[g][:, :, :], c4(bank[4 * g + 1]), ACT.Copy).then_inc(b_vc, 1)
                for g in range(2):
                    m = 2 * c + g
                    act.wait_ge(b_o, m + 1)
                    act.activation(qkvz[:, 16 + 4 * g:20 + 4 * g, tc], c4(bank[4 * g + 2]), ACT.Copy).then_inc(b_oc, 1)

        o_bc, o_n, o_g = sem("o_bc"), sem("o_n"), sem("o_g")
        ocol = at("ocol", 133.5, [P, 3, 32])

        def onorm_pe(pe):
            for j in range(AH):
                pe.wait_ge(hn_sq, 16 + j + 1)
                for c in range(TT):
                    mm = pe.matmul(bank[4][:, j * 4 + c:j * 4 + c + 1], sq[:, j % 2, c * P:c * P + P], ones[:, 0:1],
                                   start=(j == 0 and c == 0), stop=True, skip_group_check=True)
                mm.then_inc(hn_ss, 1)
            pe.wait_ge(hn_rcp, 2)
            for j in range(AH):
                ge(pe, o_n, j - 1)
                for c in range(TT):
                    mm = pe.matmul(bank[6 + j % 2][:, c * P:c * P + P],
                                   ocol[:, 2, j * 4 + c:j * 4 + c + 1].to_broadcast([P, P]), ident[:, :],
                                   start=True, stop=True)
                mm.then_inc(o_bc, 1)

        def onorm_act(act):
            act.wait_ge(b_oc, 8)
            for j in range(AH):
                ge(act, hn_ss, 16 + j - 1)
                act.activation(sq[:, j % 2, :], qkvz[:, 16 + j, :], ACT.Square).then_inc(hn_sq, 1)
            act.wait_ge(hn_var, 3)
            act.activation(ocol[:, 1, :], ocol[:, 0, :], ACT.Sqrt).then_inc(hn_std, 1)

            def body(j):
                act.wait_ge(o_g, j + 1)
                act.activation(x_hi[:, ds(j, 1), :], qkv(j + 16), ACT.Copy).then_inc(hn_hi, 1)
            turns(act, AH, 1, body)

        def onorm_dve(dve):
            dve.wait_ge(hn_ss, 16 + AH)
            dve.tensor_scalar(ocol[:, 0, :], bank[4][:, 0:32], 1.0 / P, EPS1, ALU.mult, ALU.add).then_inc(hn_var, 1)
            dve.wait_ge(hn_std, 2)
            dve.reciprocal(ocol[:, 2, :], ocol[:, 1, :]).then_inc(hn_rcp, 1)

            def body(j):
                for s in range(2):
                    dve.wait_ge(o_bc, j + s + 1)
                    dve.scalar_tensor_tensor(qkv(j + s + 16), qkv(j + s + 16), pcol("a_out_norm"), bank[6 + s][:, :],
                                             ALU.mult, ALU.mult).then_inc(o_n, 1)
                    dve.wait_ge(o_n, j + s + 1)
                    dve.tensor_tensor(qkv(j + s + 16), qkv(j + s + 16), qkv(j + s + 24), ALU.mult).then_inc(o_g, 1)
                for s in range(2):
                    dve.wait_ge(hn_hi, j + s + 1)
                    dve.tensor_tensor(x_lo[:, ds(j + s, 1), :], qkv(j + s + 16), x_hi[:, ds(j + s, 1), :].bitcast(F32),
                                      ALU.subtract).then_inc(hn_lo, 1)
            turns(dve, AH, 2, body)

        def a_out_sp(sp):
            w = rows_k(t["a_w_out"][0])
            sp_slots(sp, SLOTS["a_out"], 4, lambda i, s: halves(w, s, i * 256))

        def a_out_pe(pe):
            projection(pe, "a_out", x_hi, x_lo, lambda k: (hn_lo, k + 1))

        def no_read(i, s):
            pass

        def add_h_slots(dve, base, c):
            squares_start(dve, c, SQ_B)

            def body(i):
                for s in range(2):
                    add_h(dve, base, i + s, s)
                    squares(dve, c, i * 2 + 2 * s, SQ_B, lambda o: (bank_free, i * 2 + 2 * (base + s) + o + 1))
            turns(dve, 4, 2, body)

        act_hi = at("act_hi", 40, [P, 8, T], F32R)
        act_lo = at("act_lo", 56, [P, 8, T], F32R)
        y_gate = at("y_gate", 72, [P, 2, T])
        y_val = at("y_val", 76, [P, 2, T])
        ada_acc = at("ada_acc", 80, [P, 6, D])
        ada_w = [at("ada_w0", 104, [P, 4, D]), at("ada_w1a", 120, [P, 2, D]), at("ada_w1b", 32, [P, 2, D])]
        (f_tap, f_g, f_v, f_silu, f_a, f_hi, f_lo, ada_in0, ada_in1, ada_used, mod_ready, mod_done) = (
            sem(n) for n in ("f_tap f_g f_v f_silu f_a f_hi f_lo ada_in0 ada_in1 ada_used "
                             "mod_ready mod_done").split())
        ada_in = [ada_in0, ada_in1]

        def ada_piece(s, r):
            return ada_w[0][:, r, :] if s == 0 else ada_w[1][:, r, :] if r < 2 else ada_w[2][:, r - 2, :]

        def ffn_sp(sp, f):
            up, dn = rows_k(t["f_w_up"][f]), rows_k(t["f_w_down"][f])
            for c in range(3):
                col = F_START[c] * P
                sp_slots(sp, SLOTS[f"f{f}_up{c}"], F_CHUNKS[c],
                         lambda i, s: both(up, s, i * P + col, i * P + (F_DIM + col)))
                sp_slots(sp, SLOTS[f"f{f}_dn{c}"], 4,
                         lambda i, s: halves(dn, s, i * 256, F_CHUNKS[c], F_START[c]))

        def ffn_pe(pe, f, lots):
            for c in range(3):
                if c == 0:
                    projection(pe, f"f{f}_up0", x_hi, x_lo, normed(lots))
                else:
                    turns(pe, F_CHUNKS[c], 2, slot_body(pe, SLOTS[f"f{f}_up{c}"], x_hi, x_lo))
                projection(pe, f"f{f}_dn{c}", act_hi, act_lo,
                           lambda k: (f_lo, 22 * f + F_START[c] + k + 1), F_CHUNKS[c])
            pe.wait_ge(ada_used, 48 * (f + 1))
            for n in range(48):
                mm = pe.matmul(bank[6][:, n:n + 1], ada_acc[:, n // 8, (n % 8) * P:(n % 8) * P + P], ones[:, 0:1],
                               start=True, stop=True)
            mm.then_inc(mod_ready, 1)

        def ffn_act(act, f, lots):
            w = t["ada_w"][f].rearrange("(k p) n -> p k n", p=P)

            def ada_load(s, pc):
                for r in range(4):
                    act.dma_start(ada_piece(s, r), w[:, 4 * s + r, ds(pc * D, D)]).then_inc(ada_in[s], 16)

            for c in range(3):
                base = SLOTS[f"f{f}_up{c}"]
                tile0 = 22 * f + F_START[c]

                def up(i, s):
                    n = base + i
                    act.wait_ge(gemm_ready, 2 * n + 1)
                    ge(act, f_lo, i + (tile0 - 1))
                    act.activation(y_gate[:, s, :], bank[2 * s][:, :], ACT.Identity, bias=pcol("f_conv_b", i + (44 * f + F_START[c])),
                                   scale=pcol("f_conv", i + (3 * 44 * f + 88 + F_START[c]))).then_inc(f_g, 1)
                    act.wait_ge(gemm_ready, 2 * n + 2)
                    act.activation(y_val[:, s, :], bank[2 * s + 1][:, :], ACT.Identity,
                                   bias=pcol("f_conv_b", i + (44 * f + 22 + F_START[c])),
                                   scale=pcol("f_conv", i + (3 * 44 * f + 88 + 22 + F_START[c]))).then_inc(f_v, 1)
                    act.wait_ge(bank_free, 2 * n + 1)
                    act.activation(y_gate[:, s, :], y_gate[:, s, :], ACT.Silu).then_inc(f_silu, 1)
                    act.wait_ge(f_a, i + (tile0 + 1))
                    act.activation(act_hi[:, ds(i, 1), :], y_gate[:, s, :], ACT.Copy).then_inc(f_hi, 1)
                act_slots(act, f"f{f}_up{c}", up, peel=(f == 0 and c == 0))

                if c == 0:
                    act.wait_ge(n_lo, KD * lots)
                    if f:
                        act.wait_ge(ada_used, 48 * f)
                    ada_load(0, 0)
                    ada_load(1, 0)
                for i in (0, 2):
                    for s in range(2):
                        n = SLOTS[f"f{f}_dn{c}"] + i + s
                        split_hi(act, n + 2, s, landed(n - s + 2))
                        nxt = 2 * c + i // 2 + 1
                        if nxt < 6:
                            act.wait_ge(ada_used, 48 * f + 16 * c + 4 * (i + s) + 4)
                            ada_load(s, nxt)
            act.wait_ge(ada_used, 48 * (f + 1))

        def ffn_dve(dve, f, c_norm):
            for c in range(3):
                base = SLOTS[f"f{f}_up{c}"]
                tile0 = 22 * f + F_START[c]

                def up(i):
                    for s in range(2):
                        j = i + (tile0 + s)
                        for o, y, first, col in ((0, y_gate, f_g, 0), (1, y_val, f_v, 22)):
                            dve.wait_ge(first, j + 1)
                            for d in (1, 2):
                                if d == 2:
                                    dve.wait_ge(f_tap, 2 * j + o + 1)
                                dve.scalar_tensor_tensor(
                                    y[:, s, d:T], bank[2 * s + o][:, 0:T - d],
                                    pcol("f_conv", i + (3 * 44 * f + 44 * (2 - d) + col + F_START[c] + s)), y[:, s, d:T],
                                    ALU.mult, ALU.add).then_inc(f_tap if d == 1 else bank_free, 1)
                        dve.wait_ge(f_silu, j + 1)
                        dve.wait_ge(bank_free, 2 * (base + i + s) + 2)
                        dve.tensor_tensor(y_gate[:, s, :], y_gate[:, s, :], y_val[:, s, :], ALU.mult).then_inc(f_a, 1)
                        dve.wait_ge(f_hi, j + 1)
                        dve.tensor_tensor(act_lo[:, ds(i + s, 1), :], y_gate[:, s, :],
                                          act_hi[:, ds(i + s, 1), :].bitcast(F32), ALU.subtract).then_inc(f_lo, 1)
                turns(dve, F_CHUNKS[c], 2, up, peel=(f == 0 and c == 0))
                base_dn = SLOTS[f"f{f}_dn{c}"]
                if c == 2:
                    squares_start(dve, c_norm, SQ_X)
                for i in (0, 2):
                    for s in range(2):
                        n = base_dn + i + s
                        pc = 2 * c + i // 2
                        q = 48 * f + 16 * c + 4 * (i + s)
                        dve.wait_ge(ada_in[s], 64 * (6 * f + pc + 1))
                        for r in range(4):
                            k = 4 * s + r
                            if k == 0:
                                if f and pc == 0:
                                    dve.wait_ge(mod_ready, f)
                                dve.wait_ge(cond_in, 1)
                                dve.tensor_scalar(ada_acc[:, pc, :], ada_piece(s, r), cond[:, 0:1], None,
                                                  ALU.mult).then_inc(ada_used, 1)
                            else:
                                dve.wait_ge(ada_used, q + r)
                                dve.scalar_tensor_tensor(ada_acc[:, pc, :], ada_piece(s, r), cond[:, k:k + 1], ada_acc[:, pc, :],
                                                         ALU.mult, ALU.add).then_inc(ada_used, 1)
                        add_h(dve, base_dn, i + s, s)
                        if c == 2:
                            squares(dve, c_norm, 2 * (i + s), SQ_X, lambda o: (bank_free, 2 * n + o + 1))
            dve.wait_ge(mod_ready, f + 1)
            dve.tensor_tensor(mod[:, f, :], bank[6][:, 0:48], par[:, PAR["ada_b"] + 48 * f:PAR["ada_b"] + 48 * f + 48],
                              ALU.add).then_inc(mod_done, 1)
            dve.wait_ge(mod_done, 3 * f + 1)
            dve.scalar_tensor_tensor(gain[:, f, 0:8], mod[:, f, 8:16], 1.0, par[:, PAR["mix_g"] + 8 * f:PAR["mix_g"] + 8 * f + 8],
                                     ALU.add, ALU.mult).then_inc(mod_done, 1)
            dve.scalar_tensor_tensor(gain[:, f, 8:16], mod[:, f, 32:40], 1.0, par[:, PAR["mlp_g"] + 8 * f:PAR["mlp_g"] + 8 * f + 8],
                                     ALU.add, ALU.mult).then_inc(mod_done, 1)

        qT = at("qT", 40, [P, KD, T])
        kT = at("kT", 56, [P, KD, T])
        v_tok = at("v_tok", 72, [P, TT, D])
        strip = [at(f"strip{i}", 88 + 2 * i, [P, T]) for i in range(2)]
        prob = [at(f"prob{i}", 102 + 2 * i, [P, T]) for i in range(4)]
        sbank = [bank[i] for i in (0, 1, 6, 7)]
        probT = [at(f"probT{i}", 96 + 2 * i, [P, TT, P]) for i in range(2)]
        acol = at("acol", 100, [P, 4, 8])
        (at_strip0, at_strip1, at_mask, at_s, at_sb, at_m, at_nm, at_e, at_rs, at_pn, at_t, at_tc, at_o, at_hi, at_lo) = (
            sem(n) for n in "at_strip0 at_strip1 at_mask at_s at_sb at_m at_nm at_e at_rs at_pn at_t at_tc at_o at_hi at_lo".split())

        def kvq_sp(sp):
            wkv, wq = rows_k(t["w_kv"]), rows_k(t["b_w_q"][0])
            sp_slots(sp, SLOTS["b_k"], 8, lambda i, s: halves(wkv, s, i * 256))
            sp_slots(sp, SLOTS["b_q"], 4, lambda i, s: halves(wq, s, i * 256))

        def strip_sp(sp):
            for j in range(BH):
                if j >= 2:
                    sp.wait_ge(at_sb, 4 * (j - 1))
                sp.dma_start(strip[j % 2][:, :], t["strips"][j]).then_inc((at_strip0, at_strip1)[j % 2], 16)

        def strip_pool(pool):
            for j in range(BH):
                pool.wait_ge((at_strip0, at_strip1)[j % 2], 16 * (j // 2) + 16)
                pool.memset(strip[j % 2][0:64, 448:512], NEG).then_inc(at_mask, 1)

        def v_pe(pe):
            def body(i):
                for s in range(2):
                    pe_slot_start(pe, SLOTS["b_v"] + i + s)
                    for o in range(2):
                        for c in (2 * o, 2 * o + 1):
                            tc = slice(c * P, c * P + P)
                            for k in range(KD):
                                wc = slice(k * 256, k * 256 + 256)
                                mm = three(pe, bank[2 * s + o][:, (c % 2) * 256:(c % 2) * 256 + 256], x_hi[:, k, tc], x_lo[:, k, tc],
                                           w_hi[s][:, wc], w_lo[s][:, wc], k == 0, k == KD - 1)
                        mm.then_inc(gemm_ready, 1)
            turns(pe, 4, 2, body)

        def kvq_pe(pe, lots):
            projection(pe, "b_k", x_hi, x_lo, normed(lots))
            v_pe(pe)
            projection(pe, "b_q", x_hi, x_lo, normed(lots + 1))

        def kv_act(act):
            def k_out(i, s):
                for o in range(2):
                    act.wait_ge(gemm_ready, 2 * (SLOTS["b_k"] + i) + o + 1)
                    act.activation(kT[:, ds(2 * i + o, 1), :], bank[2 * s + o][:, :], ACT.Copy).then_inc(bank_free, 1)

            def v_out(i, s):
                for o in range(2):
                    act.wait_ge(gemm_ready, 2 * (SLOTS["b_v"] + i) + o + 1)
                    act.activation(v_tok[:, 2 * o:2 * o + 2, ds(i * 256, 256)],
                                   bank[2 * s + o][:, :].rearrange("p (c n) -> p c n", c=2), ACT.Copy).then_inc(bank_free, 1)
            act_slots(act, "b_k", k_out)
            act_slots(act, "b_v", v_out)

        def q_act(act):
            def q_out(i, s):
                for o in range(2):
                    act.wait_ge(gemm_ready, 2 * (SLOTS["b_q"] + i) + o + 1)
                    act.activation(qT[:, ds(2 * i + o, 1), :], bank[2 * s + o][:, :], ACT.Copy,
                                   scale=float(BD) ** -0.5).then_inc(bank_free, 1)
            act_slots(act, "b_q", q_out)

        def attn_pe(pe):
            pe.wait_ge(bank_free, 2 * SLOTS["b_out"])
            units = 4 * BH

            def scores(u):
                j, it = u // 4, u % 4
                r = slice(64 * (j % 2), 64 * (j % 2) + 64)
                n = P * (it + 1)
                ge(pe, at_sb, u - 3)
                pe.matmul(sbank[u % 4][:, 0:n], qT[r, j // 2, it * P:it * P + P], kT[r, j // 2, 0:n],
                          start=True, stop=True).then_inc(at_s, 1)

            def turn(u):
                it = u % 4
                pe.wait_ge(at_pn, u + 1)
                ge(pe, at_tc, u - 1)
                for c in range(it + 1):
                    mm = pe.transpose(bank[2 + u % 2][:, c * P:c * P + P], prob[u % 4][:, c * P:c * P + P], ident[:, :])
                mm.then_inc(at_t, 1)

            def values(u):
                j, it = u // 4, u % 4
                r = slice(64 * (j % 2), 64 * (j % 2) + 64)
                pe.wait_ge(at_tc, u + 1)
                if u % 8 == 0:
                    ge(pe, at_lo, j // 2 - 1)
                for c in range(it + 1):
                    mm = pe.matmul(bank[4 + (j // 2) % 2][r, it * P:it * P + P], v_tok[:, c, j * BD:j * BD + BD],
                                   probT[u % 2][:, c, :], start=(c == 0), stop=(c == it))
                mm.then_inc(at_o, 1)
            for u in range(units + 3):
                if u < units:
                    scores(u)
                if 2 <= u < units + 2:
                    turn(u - 2)
                if u >= 3:
                    values(u - 3)

        def attn_act(act):
            def tcopy(u, k):
                n = P * (k % 4 + 1)
                act.wait_ge(at_t, u + 1)
                ge(act, at_o, u - 1)
                act.activation(probT[k % 2][:, :, :].rearrange("p c i -> p (c i)")[:, 0:n], bank[2 + k % 2][:, 0:n],
                               ACT.Copy).then_inc(at_tc, 1)

            def body(m):
                for k in range(16):
                    u = 8 * m + k
                    n = P * (k % 4 + 1)
                    act.wait_ge(at_nm, u + 1)
                    act.activation(prob[k % 4][:, 0:n], prob[k % 4][:, 0:n], ACT.Exp, bias=acol[:, 1, k % 8:k % 8 + 1],
                                   accum_out=acol[:, 2, k % 8:k % 8 + 1]).then_inc(at_e, 1)
                    if k >= 2 or not isinstance(m, int):
                        tcopy(u - 2, (k - 2) % 16)
                    if k in (4, 12) and not (k == 4 and isinstance(m, int)):
                        pair = m + (k == 12) - 1
                        act.wait_ge(at_o, 8 * pair + 8)
                        act.activation(x_hi[:, ds(pair, 1), :], bank[4 + (k == 4)][:, :], ACT.Copy).then_inc(at_hi, 1)
            turns(act, KD, 2, body, peel=True)
            tcopy(62, 14)
            tcopy(63, 15)
            act.wait_ge(at_o, 64)
            act.activation(x_hi[:, 7, :], bank[5][:, :], ACT.Copy).then_inc(at_hi, 1)

        def attn_dve(dve):
            def norm(u, k):
                n = P * (k % 4 + 1)
                dve.wait_ge(at_e, u + 1)
                dve.reciprocal(acol[:, 3, k % 8:k % 8 + 1], acol[:, 2, k % 8:k % 8 + 1]).then_inc(at_rs, 1)
                dve.wait_ge(at_rs, u + 1)
                dve.tensor_scalar(prob[k % 4][:, 0:n], prob[k % 4][:, 0:n], acol[:, 3, k % 8:k % 8 + 1], None,
                                  ALU.mult).then_inc(at_pn, 1)

            def low(pair, b):
                dve.wait_ge(at_hi, pair + 1)
                dve.tensor_tensor(x_lo[:, ds(pair, 1), :], bank[4 + b][:, :], x_hi[:, ds(pair, 1), :].bitcast(F32),
                                  ALU.subtract).then_inc(at_lo, 1)

            def body(m):
                for k in range(16):
                    u = 8 * m + k
                    n = P * (k % 4 + 1)
                    dve.wait_ge(at_s, u + 1)
                    ge(dve, at_mask, 2 * m + k // 4 + 1)
                    if k >= 4 or not isinstance(m, int):
                        dve.wait_ge(at_t, u - 3)
                    dve.tensor_tensor(prob[k % 4][:, 0:n], sbank[k % 4][:, 0:n], strip[(k // 4) % 2][:, T - n:T],
                                      ALU.add).then_inc(at_sb, 1)
                    dve.wait_ge(at_sb, u + 1)
                    dve.tensor_reduce(acol[:, 0, k % 8:k % 8 + 1], prob[k % 4][:, 0:n], AX.X, ALU.max).then_inc(at_m, 1)
                    dve.wait_ge(at_m, u + 1)
                    dve.tensor_scalar(acol[:, 1, k % 8:k % 8 + 1], acol[:, 0, k % 8:k % 8 + 1], -1.0, None,
                                      ALU.mult).then_inc(at_nm, 1)
                    if k or not isinstance(m, int):
                        norm(u - 1, k - 1 if k else 15)
                    if k in (6, 14) and not (k == 6 and isinstance(m, int)):
                        low(m + (k == 14) - 1, 1 if k == 6 else 0)
            turns(dve, KD, 2, body, peel=True)
            norm(63, 15)
            low(7, 1)

        def b_out_sp(sp):
            w = rows_k(t["b_w_out"][0])
            sp_slots(sp, SLOTS["b_out"], 4, lambda i, s: halves(w, s, i * 256))

        def b_out_pe(pe):
            projection(pe, "b_out", x_hi, x_lo, lambda k: (at_lo, k + 1))

        mid_done = sem("mid_done")

        def mid_dve(dve, c, c_next):
            norm_root(dve, c, EPS1)
            for k in range(KD):
                dve.scalar_tensor_tensor(h[:, k, :], h[:, k, :], pcol("final_norm", k), RSTD, ALU.mult, ALU.mult).then_inc(mid_done, 1)
            squares_start(dve, c_next, SQ_B)
            for k in range(0, KD, 2):
                squares(dve, c_next, k, SQ_B, lambda o: (mid_done, k + o + 1))

        uT = at("uT", 40, [P, KD, T])
        ct = at("ct", 56, [P, S5N, P])
        st = at("st", 72, [P, S5N, P])
        bt = at("bt", 88, [P, 2, S5Q, P])
        cw = at("cw", 96, [P, 2, S5N, 32])
        ck = at("ck", 104, [P, 3, S5N, 32])
        rt = at("rt", 116, [P, 4, P])
        gin = at("gin", 118, [P, 2, T])
        gs = at("gs", 122, [P, 2, T])
        s_t = [[at(f"s_t{u}{i}", (32, 16)[u] + 2 * i, [P, T]) for i in range(4)] for u in range(2)]
        ubank = [bank[0:2], bank[4:6]]
        pr = at("pr", 96, [P, 4, T])
        scol = at("scol", 126, [P, 16, S5N])
        carry = at("carry", 128, [P, 6, 4])
        um = [at(f"um{i}", 129 + 2 * i, [P, T]) for i in range(2)]
        s_um = sem("s_um")
        dbl = at("dbl", 118, [P, S5N, 64])
        (DT, RA, TH, RR, CO, SI, KR_, KI_, T0, T1, T2, T3, C64, S64, CN, SN) = range(16)
        (s_in, s_dve, s_act, s_bu, s_mul, s_re, s_im, s_gin, s_rc, s_scan, s_pr, s_pp, s_y, s_car, s_out, s_gelu,
         s_lo, s_rt) = (sem("s_" + n) for n in
                        "in dve act bu mul re im gin rc scan pr pp y car out gelu lo rt".split())

        def s_load_sp(sp):
            sp.wait_ge(gemm_ready, 2 * SLOTS["s_in"])
            sp.wait_ge(mod_done, 6)
            sp.dma_start(bt[:, :, :, :], t["s5_bt"]).then_inc(s_in, 16)
            sp.dma_start(cw[:, :, :, :], t["s5_ct"]).then_inc(s_in, 16)

        def s_in_sp(sp):
            w = rows_k(t["s5_w_in"][0])
            sp_slots(sp, SLOTS["s_in"], 4, lambda i, s: halves(w, s, i * 256))

        def s_in_pe(pe, lots):
            projection(pe, "s_in", x_hi, x_lo, normed(lots))

        def s_in_act(act):
            def u_out(i, s):
                for o in range(2):
                    act.wait_ge(gemm_ready, 2 * (SLOTS["s_in"] + i) + o + 1)
                    act.activation(uT[:, ds(2 * i + o, 1), :], bank[2 * s + o][:, :], ACT.Copy).then_inc(bank_free, 1)
            act_slots(act, "s_in", u_out)

        def sc(n):
            return scol[:, n, :]

        def s_par_act(act):
            act.wait_ge(gemm_ready, 2 * SLOTS["s_in"])
            act.activation(sc(DT), par[:, PAR["log_dt"]:PAR["log_dt"] + 32], ACT.Exp).then_inc(s_act, 1)
            act.wait_ge(s_dve, 1)
            act.activation(sc(RR), sc(RA), ACT.Exp).then_inc(s_act, 1)
            act.wait_ge(s_dve, 12)
            act.activation(sc(SI), sc(T0), ACT.Sin).then_inc(s_act, 1)
            act.activation(sc(CO), sc(T1), ACT.Sin).then_inc(s_act, 1)

        def s_par_dve(dve):
            count = [0]

            def step(op):
                count[0] += 1
                op.then_inc(s_dve, 1)
                dve.wait_ge(s_dve, count[0])
            lr, li = (par[:, PAR[n]:PAR[n] + 32] for n in ("lam_re", "lam_im"))
            two_pi = [6.28125, 0.0019350051879882812, 3.019916050561517e-07]
            magic = 1.5 * 2.0 ** 23
            dve.wait_ge(gemm_ready, 2 * SLOTS["s_in"])
            dve.wait_ge(s_act, 1)
            step(dve.tensor_tensor(sc(RA), lr, sc(DT), ALU.mult))
            step(dve.tensor_tensor(sc(TH), li, sc(DT), ALU.mult))
            step(dve.tensor_scalar(sc(T0), sc(TH), 1.0 / (2.0 * np.pi), None, ALU.mult))
            step(dve.tensor_scalar(sc(T1), sc(T0), magic, None, ALU.add))
            step(dve.tensor_scalar(sc(T1), sc(T1), magic, None, ALU.subtract))
            step(dve.scalar_tensor_tensor(sc(T0), sc(T1), -two_pi[0], sc(TH), ALU.mult, ALU.add))
            step(dve.scalar_tensor_tensor(sc(T0), sc(T1), -two_pi[1], sc(T0), ALU.mult, ALU.add))
            step(dve.scalar_tensor_tensor(sc(T0), sc(T1), -two_pi[2], sc(T0), ALU.mult, ALU.add))
            step(dve.tensor_scalar(sc(T0), sc(T0), 3.1415925, -3.1415925, ALU.min, ALU.max))
            step(dve.scalar_tensor_tensor(sc(T1), sc(T0), -1.0, sc(T0), ALU.mult, ALU.min))
            step(dve.tensor_scalar(sc(T1), sc(T1), float(np.pi / 2), None, ALU.add))
            step(dve.memset(sc(T2), 0.0))
            dve.wait_ge(s_act, 4)
            step(dve.tensor_tensor(sc(T0), sc(RR), sc(CO), ALU.mult))
            step(dve.tensor_scalar(sc(T0), sc(T0), -1.0, None, ALU.add))
            step(dve.tensor_tensor(sc(T1), sc(RR), sc(SI), ALU.mult))
            step(dve.tensor_tensor(sc(T2), lr, lr, ALU.mult))
            step(dve.tensor_tensor(sc(T3), li, li, ALU.mult))
            step(dve.tensor_tensor(sc(T2), sc(T2), sc(T3), ALU.add))
            step(dve.reciprocal(sc(T2), sc(T2)))
            step(dve.tensor_tensor(sc(KR_), sc(T0), lr, ALU.mult))
            step(dve.tensor_tensor(sc(T3), sc(T1), li, ALU.mult))
            step(dve.tensor_tensor(sc(KR_), sc(KR_), sc(T3), ALU.add))
            step(dve.tensor_tensor(sc(KR_), sc(KR_), sc(T2), ALU.mult))
            step(dve.tensor_tensor(sc(KI_), sc(T1), lr, ALU.mult))
            step(dve.tensor_tensor(sc(T3), sc(T0), li, ALU.mult))
            step(dve.tensor_tensor(sc(KI_), sc(KI_), sc(T3), ALU.subtract))
            step(dve.tensor_tensor(sc(KI_), sc(KI_), sc(T2), ALU.mult))
            dve.wait_ge(s_in, 32)
            kr, ki = (sc(n).unsqueeze(2).to_broadcast([P, S5N, 32]) for n in (KR_, KI_))
            step(dve.tensor_tensor(ck[:, 0], cw[:, 0], kr, ALU.mult))
            step(dve.tensor_tensor(ck[:, 1], cw[:, 1], ki, ALU.mult))
            step(dve.tensor_tensor(ck[:, 0], ck[:, 0], ck[:, 1], ALU.subtract))
            step(dve.tensor_scalar(ck[:, 1], ck[:, 0], -1.0, None, ALU.mult))
            step(dve.tensor_tensor(cw[:, 0], cw[:, 0], ki, ALU.mult))
            step(dve.tensor_tensor(cw[:, 1], cw[:, 1], kr, ALU.mult))
            step(dve.tensor_tensor(cw[:, 0], cw[:, 0], cw[:, 1], ALU.add))
            step(dve.tensor_scalar(ck[:, 2], cw[:, 0], -1.0, None, ALU.mult))
            step(dve.memset(ct[:, :, 0:1], 1.0))
            step(dve.memset(st[:, :, 0:1], 0.0))
            step(dve.tensor_copy(sc(C64), sc(CO)))
            step(dve.tensor_copy(sc(S64), sc(SI)))
            m = 1
            while m <= 64:
                cm, sm = (sc(n).unsqueeze(2).to_broadcast([P, S5N, m]) for n in (C64, S64))
                lo, up = slice(0, m), slice(m, 2 * m)
                tmp = dbl[:, :, 0:m]
                step(dve.tensor_tensor(ct[:, :, up], ct[:, :, lo], cm, ALU.mult))
                step(dve.tensor_tensor(tmp, st[:, :, lo], sm, ALU.mult))
                step(dve.tensor_tensor(ct[:, :, up], ct[:, :, up], tmp, ALU.subtract))
                step(dve.tensor_tensor(st[:, :, up], st[:, :, lo], cm, ALU.mult))
                step(dve.tensor_tensor(tmp, ct[:, :, lo], sm, ALU.mult))
                step(dve.tensor_tensor(st[:, :, up], st[:, :, up], tmp, ALU.add))
                step(dve.tensor_tensor(sc(T0), sc(C64), sc(C64), ALU.mult))
                step(dve.tensor_tensor(sc(T1), sc(S64), sc(S64), ALU.mult))
                step(dve.scalar_tensor_tensor(sc(S64), sc(S64), 2.0, sc(C64), ALU.mult, ALU.mult))
                step(dve.tensor_tensor(sc(C64), sc(T0), sc(T1), ALU.subtract))
                m *= 2
            step(dve.tensor_tensor(sc(CN), sc(RR), sc(C64), ALU.mult))
            step(dve.tensor_tensor(sc(SN), sc(RR), sc(S64), ALU.mult))

        def s5_pe(pe):
            pe.wait_ge(bank_free, 2 * SLOTS["s_glu"])
            pe.wait_ge(s_in, 32)

            def inputs(m):
                q, c = m // 4, m % 4
                ge(pe, s_mul, 4 * m - 4)
                pe.wait_ge(s_um, m + 1)
                for x in range(2):
                    mm = pe.matmul(ubank[m % 2][x][:, :], bt[:, x, q, :], um[m % 2][:, :], start=True, stop=True)
                mm.then_inc(s_bu, 1)

            def outputs(m):
                q, c = m // 4, m % 4
                pe.wait_ge(s_pr, 2 * m + 2)
                pe.wait_ge(s_pp, 2 * m + 2)
                ge(pe, s_out, m - 1)
                for k in range(4):
                    r = slice(32 * k, 32 * k + 32)
                    for x, part in ((0, 0), (1, 1), (2, 2), (2, 3)):
                        mm = pe.matmul(bank[2 + m % 2][r, 0:P], ck[:, x, 4 * q + k, :], pr[:, part, k * P:k * P + P],
                                       start=(part == 0), stop=(part == 3))
                mm.then_inc(s_y, 1)
            pe.wait_ge(s_dve, S_STEPS)
            for m in range(34):
                if m < 32:
                    inputs(m)
                if m >= 2:
                    outputs(m - 2)

        S_STEPS = 12 + 15 + 8 + 4 + 7 * 10 + 2

        def s5_dve(dve):
            def v4(x):
                return x.rearrange("p (k i) -> p k i", k=4)

            def inputs(q, c, m):
                def tab(x):
                    return x[:, ds(q * 4, 4), :]
                re, im = (v4(b[:, :]) for b in ubank[c % 2])
                s_to = s_t[c % 2]
                dve.wait_ge(s_bu, m + 1)
                if not isinstance(m, int) or m >= 2:
                    dve.wait_ge(s_im, m - 1)
                dve.tensor_tensor(v4(s_to[0][:, :]), re, tab(ct), ALU.mult).then_inc(s_mul, 1)
                dve.tensor_tensor(v4(s_to[1][:, :]), im, tab(st), ALU.mult).then_inc(s_mul, 1)
                dve.tensor_tensor(v4(s_to[2][:, :]), im, tab(ct), ALU.mult).then_inc(s_mul, 1)
                dve.tensor_tensor(v4(s_to[3][:, :]), re, tab(st), ALU.mult).then_inc(s_mul, 1)

            def yq(q, c, m):
                dve.wait_ge(s_y, m + 1)
                uc = uT[:, ds(q, 1), c * P:c * P + P]
                dve.scalar_tensor_tensor(uc, uc, pcol("s5_d", q), bank[2 + c % 2][:, 0:P], ALU.mult, ALU.add).then_inc(s_out, 1)

            def quad(q, last=False):
                def tab(x):
                    return x[:, ds(q * 4, 4), :]

                def col(n):
                    return scol[:, n, ds(q * 4, 4)]

                def chunk(c):
                    m = q * 4 + c
                    for x, done in ((0, s_re), (1, s_im)):
                        g0 = v4(gin[:, x, :])[:, :, 0]
                        dve.wait_ge(done, m + 1)
                        if c:
                            dve.wait_ge(s_car, q * 6 + 2 * c)
                            dve.tensor_tensor(g0, g0, carry[:, 4 + x, :], ALU.add).then_inc(s_gin, 1)
                            dve.wait_ge(s_gin, q * 6 + (2 * c - 1 + x))
                        if x == 0:
                            dve.wait_ge(s_rt, q + 1)
                        if not (isinstance(q, int) and q == 0 and c == 0):
                            dve.wait_ge(s_pp, 2 * m)
                            dve.wait_ge(s_pr, 2 * m)
                        dve.tensor_tensor_scan(gs[:, x, :], rt[:, :, :].rearrange("p k i -> p (k i)"), gin[:, x, :], 0.0,
                                               ALU.mult, ALU.add).then_inc(s_scan, 1)
                    if c < 3:
                        inputs(q, c + 1, m + 1)
                    elif not last:
                        inputs(q + 1, 0, m + 1)
                    dve.wait_ge(s_scan, 2 * m + 2)
                    gr, gi = v4(gs[:, 0, :]), v4(gs[:, 1, :])
                    if c < 3:
                        er, ei = gr[:, :, P - 1], gi[:, :, P - 1]
                        dve.tensor_tensor(carry[:, 0, :], er, col(CN), ALU.mult)
                        dve.tensor_tensor(carry[:, 1, :], ei, col(SN), ALU.mult)
                        dve.tensor_tensor(carry[:, 2, :], er, col(SN), ALU.mult)
                        dve.tensor_tensor(carry[:, 3, :], ei, col(CN), ALU.mult).then_inc(s_rc, 1)
                    if c >= 2:
                        yq(q, c - 2, m - 2)
                    elif not isinstance(q, int) or q:
                        yq(q - 1, c + 2, m - 2)
                    if not (isinstance(q, int) and q == 0 and c == 0):
                        dve.wait_ge(s_y, m)
                    dve.tensor_tensor(v4(pr[:, 0, :]), gr, tab(ct), ALU.mult).then_inc(s_pr, 1)
                    if c < 3:
                        dve.wait_ge(s_rc, q * 3 + (c + 1))
                        dve.tensor_tensor(carry[:, 4, :], carry[:, 0, :], carry[:, 1, :], ALU.subtract).then_inc(s_car, 1)
                        dve.tensor_tensor(carry[:, 5, :], carry[:, 2, :], carry[:, 3, :], ALU.add).then_inc(s_car, 1)
                    dve.tensor_tensor(v4(pr[:, 1, :]), gi, tab(st), ALU.mult).then_inc(s_pr, 1)

                for c in range(4):
                    chunk(c)
            inputs(0, 0, 0)
            quad(0)
            with dve.Fori(1, S5Q - 1, 1) as q:
                quad(q)
            quad(S5Q - 1, last=True)
            yq(S5Q - 1, 2, 30)
            yq(S5Q - 1, 3, 31)

        def s5_pool(pool):
            def v4(x):
                return x.rearrange("p (k i) -> p k i", k=4)

            def spread(m):
                q, c = m // 4, m % 4
                pool.tensor_tensor(v4(um[c % 2][:, :]), bc4(uT[:, q, c * P:c * P + P]),
                                   par[:, PAR["qmask"]:PAR["qmask"] + 4].unsqueeze(2).to_broadcast([P, 4, P]),
                                   ALU.mult).then_inc(s_um, 1)

            pool.wait_ge(s_dve, S_STEPS)
            pool.wait_ge(bank_free, 2 * SLOTS["s_glu"])
            spread(0)
            spread(1)
            for m in range(4 * S5Q):
                q, c = m // 4, m % 4
                ctab, stab = ct[:, 4 * q:4 * q + 4, :], st[:, 4 * q:4 * q + 4, :]
                if c == 0:
                    if q:
                        pool.wait_ge(s_scan, 2 * m)
                    pool.tensor_copy(rt[:, :, :], scol[:, RR, 4 * q:4 * q + 4].unsqueeze(2).to_broadcast([P, 4, P])).then_inc(s_rs, 1)
                    pool.wait_ge(s_rs, q + 1)
                    pool.memset(rt[:, :, 0:1], 0.0).then_inc(s_rt, 1)
                s_to = s_t[c % 2]
                pool.wait_ge(s_mul, 4 * m + 2)
                ge(pool, s_scan, 2 * m)
                pool.tensor_tensor(gin[:, 0, :], s_to[0][:, :], s_to[1][:, :], ALU.add).then_inc(s_re, 1)
                pool.wait_ge(s_mul, 4 * m + 4)
                pool.tensor_tensor(gin[:, 1, :], s_to[2][:, :], s_to[3][:, :], ALU.subtract).then_inc(s_im, 1)
                if m + 2 < 4 * S5Q:
                    spread(m + 2)
                pool.wait_ge(s_scan, 2 * m + 2)
                ge(pool, s_y, m)
                pool.tensor_tensor(v4(pr[:, 2, :]), v4(gs[:, 0, :]), stab, ALU.mult).then_inc(s_pp, 1)
                pool.tensor_tensor(v4(pr[:, 3, :]), v4(gs[:, 1, :]), ctab, ALU.mult).then_inc(s_pp, 1)

        s_rs = sem("s_rs")

        def s_gelu_act(act):
            def body(q):
                act.wait_ge(s_out, 4 * q + 4)
                act.activation(uT[:, ds(q, 1), :], uT[:, ds(q, 1), :], ACT.Gelu_apprx_tanh).then_inc(s_gelu, 1)
                act.wait_ge(s_gelu, 2 * q + 1)
                act.activation(x_hi[:, ds(q, 1), :], uT[:, ds(q, 1), :], ACT.Copy).then_inc(s_gelu, 1)
            turns(act, S5Q, 1, body)

        def s_gelu_dve(dve):
            def body(q):
                dve.wait_ge(s_gelu, 2 * q + 2)
                dve.tensor_tensor(x_lo[:, ds(q, 1), :], uT[:, ds(q, 1), :], x_hi[:, ds(q, 1), :].bitcast(F32),
                                  ALU.subtract).then_inc(s_lo, 1)
            turns(dve, S5Q, 1, body)

        glu = at("glu", 56, [P, 4, T])
        g_sig, g_h = sem("g_sig"), sem("g_h")

        def glu_sp(sp):
            w = rows_k(t["s5_w_glu"][0])
            sp_slots(sp, SLOTS["s_glu"], 8, lambda i, s: both(w, s, i * P, i * P + D))

        def glu_pe(pe):
            projection(pe, "s_glu", x_hi, x_lo, lambda k: (s_lo, k + 1))

        def glu_act(act):
            def gate(i, s):
                act.wait_ge(gemm_ready, 2 * (SLOTS["s_glu"] + i) + 2)
                if not (isinstance(i, int) and i < 2):
                    act.wait_ge(bank_free, 2 * (SLOTS["s_glu"] + i) - 2)
                act.activation(glu[:, s, :], bank[2 * s + 1][:, :], ACT.Sigmoid, bias=pcol("s5_b_glu", i + 8)).then_inc(g_sig, 1)
            act_slots(act, "s_glu", gate, peel=True)

        def glu_dve(dve, c):
            squares_start(dve, c, SQ_B)

            def body(i):
                for s in range(2):
                    dve.wait_ge(g_sig, i + s + 1)
                    dve.scalar_tensor_tensor(glu[:, 2 + s, :], bank[2 * s][:, :], pcol("s5_b_glu", i + s), glu[:, s, :],
                                             ALU.add, ALU.mult).then_inc(bank_free, 2)
                    dve.wait_ge(bank_free, 2 * (SLOTS["s_glu"] + i + s) + 2)
                    hk = h[:, ds(i + s, 1), :]
                    dve.scalar_tensor_tensor(hk, glu[:, 2 + s, :], modc(0, 16 + i + s), hk, ALU.mult, ALU.add).then_inc(g_h, 1)
                squares(dve, c, i, SQ_B, lambda o: (g_h, i + o + 1))
            turns(dve, 8, 2, body)

        def modc(f, i):
            return mod[:, f, ds(i, 1)]

        def gainc(f, i):
            return gain[:, f, i:i + 1]

        m_hi = at("m_hi", 40, [P, 8, T], F32R)
        m_lo = at("m_lo", 56, [P, 8, T], F32R)
        m_r = at("m_r", 72, [P, 2, T])
        p_r, p_hi, p_lo = (sem("p_" + n) for n in ("r", "hi", "lo"))
        PASS = 8

        def mlp_sp(sp, f):
            w1 = rows_k(t["mlp_w1"][f])
            w2 = rows_k(t["mlp_w2"][f])
            base = SLOTS[f"p{f}"]

            def one(c):
                sp_slots(sp, c * PASS + base, 4, lambda i, s: halves(w1, s, c * 1024 + i * 256))
                sp_slots(sp, c * PASS + (base + 4), 4, lambda i, s: halves(w2, s, i * 256, KD, c * KD))
            turns(sp, 4, 1, one)

        def mlp_pe(pe, f, lots):
            base = SLOTS[f"p{f}"]
            for c in range(4):
                if c == 0:
                    projection(pe, None, x_hi, x_lo, normed(lots), count=4, base=base)
                else:
                    turns(pe, 4, 2, slot_body(pe, c * PASS + base, x_hi, x_lo))
                projection(pe, None, m_hi, m_lo, lambda k: (p_lo, 32 * f + 8 * c + k + 1), count=4,
                           base=c * PASS + base + 4)

        def mlp_act(act, f):
            base = SLOTS[f"p{f}"]

            def one(c, end=False):
                def up(i, s):
                    n = c * PASS + base + i
                    for o in range(2):
                        j = c * 8 + 2 * i + (32 * f + o)
                        act.wait_ge(gemm_ready, 2 * n + o + 1)
                        if not (isinstance(j, int) and j < 2):
                            act.wait_ge(p_lo, j - 1)
                        act.activation(m_r[:, o, :], bank[2 * s + o][:, :], ACT.Relu).then_inc(p_r, 1)
                        act.wait_ge(bank_free, 2 * n + o + 1)
                        act.activation(m_hi[:, ds(2 * i + o, 1), :], m_r[:, o, :], ACT.Copy).then_inc(p_hi, 1)
                act_slots(act, None, up, 0, 4, base=c * PASS + base, peel=(f == 0 and isinstance(c, int)))
                act_slots(act, None, no_read, 0, 4, base=c * PASS + (base + 4))
            if f == 0:
                turns(act, 4, 1, one, peel=True)
            else:
                turns(act, 3, 1, one)
                one(3)

        def mlp_dve(dve, f, c_norm):
            base = SLOTS[f"p{f}"]

            def one(c, last=False):
                if last:
                    squares_start(dve, c_norm, SQ_B)

                def up(i):
                    for s in range(2):
                        n = c * PASS + base + i + s
                        for o in range(2):
                            j = c * 8 + 2 * i + (32 * f + 2 * s + o)
                            dve.wait_ge(p_r, j + 1)
                            dve.scalar_tensor_tensor(m_r[:, o, :], bank[2 * s + o][:, :], 0.0, m_r[:, o, :],
                                                     ALU.max, ALU.mult).then_inc(bank_free, 1)
                            dve.wait_ge(p_hi, j + 1)
                            lo = m_lo[:, ds(2 * i + (2 * s + o), 1), :]
                            dve.tensor_tensor(lo, m_r[:, o, :], m_hi[:, ds(2 * i + (2 * s + o), 1), :].bitcast(F32),
                                              ALU.subtract).then_inc(p_lo, 1)
                turns(dve, 4, 2, up)

                def down(i):
                    for s in range(2):
                        n = c * PASS + (base + 4) + i + s
                        for o in range(2):
                            k = 2 * i + (2 * s + o)
                            dve.wait_ge(gemm_ready, 2 * n + o + 1)
                            hk = h[:, ds(k, 1), :]
                            dve.scalar_tensor_tensor(hk, bank[2 * s + o][:, :], modc(f, 40 + k), hk, ALU.mult, ALU.add).then_inc(bank_free, 1)
                        if last:
                            squares(dve, c_norm, 2 * i + 2 * s, SQ_B, lambda o: (bank_free, 2 * n + o + 1))
                turns(dve, 4, 2, down)
            turns(dve, 3, 1, one)
            one(3, last=True)
        zT = at("zT", 40, [P, M_TILES, T])
        xbc = at("xbc", 72, [P, XBC_TILES, T])
        (m_dt, m_silu, wdt_in) = (sem("m_" + n) for n in "dt silu wdt".split())
        mcols = at("mcols", 128, [P, 10, TT * M_H])
        (M_X, M_ABS, M_E, M_U, M_L, M_DT, M_ADT, M_CS, M_EDX, M_DEC) = range(10)
        DTP = bank[6][:, 0:TT * M_H].rearrange("p (c n) -> p c n", n=M_H)

        def mc(n):
            return mcols[:, n, :].rearrange("p (c h) -> p c h", h=M_H)

        def m_in_sp(sp):
            w = t["m2_w_in"][0]
            sp.wait_ge(gemm_ready, 2 * SLOTS["p0"])
            sp.dma_start(nar_raw[:, :, :], rows_k(w)[:, :, 5120:5152]).then_inc(wdt_in, 16)
            sp_slots(sp, SLOTS["m_in"], 20, lambda i, s: halves(rows_k(w), s, i * 256))

        def m_in_pe(pe, lots):
            base = SLOTS["m_in"]
            first_turn(pe, base, x_hi, x_lo, normed(lots))
            narrow_pe(pe, 2)
            body = slot_body(pe, base, x_hi, x_lo)
            body(2)
            narrow_turn_pe(pe, 2, DTP, M_H, m_dt)
            turns(pe, 20, 2, body, start=4)

        def xb(j, a=0, b=T):
            return xbc[:, ds(j, 1), a:b]

        def m_in_act(act):
            base = SLOTS["m_in"]

            def silu(j):
                for o in range(2):
                    act.activation(xb(j + o), xb(j + o), ACT.Silu).then_inc(m_silu, 1)

            def gate(i, s):
                for o in range(2):
                    act.wait_ge(gemm_ready, 2 * (base + i) + o + 1)
                    act.activation(zT[:, ds(2 * i + o, 1), :], bank[2 * s + o][:, :], ACT.Silu).then_inc(bank_free, 1)

            def conv(i, s):
                for o in range(2):
                    j = 2 * i + (o - M_TILES)
                    act.wait_ge(gemm_ready, 2 * (base + i) + o + 1)
                    act.activation(xb(j), bank[2 * s + o][:, :], ACT.Identity, bias=pcol("m_conv_b", j),
                                   scale=pcol("m_conv", j + 3 * 24)).then_inc(tap_first, 1)
                if not (isinstance(i, int) and i == 8):
                    act.wait_ge(bank_free, 2 * (base + i))
                    silu(2 * i - (M_TILES + 2))
            act.wait_ge(wdt_in, 16)
            narrow_hi_act(act)
            act_slots(act, "m_in", gate, 0, 2, peel=True)
            narrow_out_act(act, 2)
            act_slots(act, "m_in", gate, 2, 6)
            act_slots(act, "m_in", lambda i, s: conv(i, s), 8, 2)
            act_slots(act, "m_in", conv, 10, 10)
            act.wait_ge(bank_free, 2 * (base + 20))
            silu(22)

        def m_in_dve(dve):
            narrow_lo_dve(dve, 2)

            def body(i):
                for s in range(2):
                    for o in range(2):
                        j = 2 * (i + s) + o
                        dve.wait_ge(tap_first, 24 + j + 1)
                        for d in (1, 2, 3):
                            if d > 1:
                                dve.wait_ge(tap_mid, 48 + 2 * j + d - 1)
                            dve.scalar_tensor_tensor(xb(j, d), bank[2 * s + o][:, 0:T - d], pcol("m_conv", j + (3 - d) * 24),
                                                     xb(j, d), ALU.mult, ALU.add).then_inc(tap_mid if d < 3 else bank_free, 1)
            turns(dve, 12, 2, body)

        d_pe, d_act, d_dve = sem("steps_pe"), sem("steps_act"), sem("steps_dve")

        def bch(row):
            return row.unsqueeze(1).to_broadcast([P, TT, M_H])

        def steps_dve(dve):
            dve.wait_ge(m_dt, 1)
            dve.tensor_tensor(mc(M_X), DTP, bch(rows[:, 48:80]), ALU.add).then_inc(d_dve, 1)
            dve.wait_ge(d_dve, 1)
            softplus_dve(dve, 0, mc(M_X), mc(M_ABS), mc(M_E), mc(M_U), mc(M_L), mc(M_DT), 7, 2)
            dve.wait_ge(sp_d, 14)
            dve.wait_ge(d_act, 1)
            dve.scalar_tensor_tensor(mc(M_ADT), mc(M_DT), -1.0, bch(mcols[:, M_EDX, 0:M_H]), ALU.mult, ALU.mult).then_inc(d_dve, 1)
            dve.wait_ge(d_pe, 1)
            dve.tensor_copy(mcols[:, M_CS, :], bank[7][:, 0:128]).then_inc(d_dve, 1)
            dve.tensor_copy(mcols[:, M_DEC, :], bank[7][:, 128:256]).then_inc(d_dve, 1)
            dve.wait_ge(d_dve, 4)
            dve.tensor_tensor(mcols[:, M_EDX, :], mcols[:, M_DEC, :], mcols[:, M_CS, :], ALU.subtract).then_inc(d_dve, 1)

        def steps_act(act):
            act.wait_ge(m_dt, 1)
            act.activation(mcols[:, M_EDX, 0:M_H], rows[:, 16:48], ACT.Exp).then_inc(d_act, 1)
            softplus_act(act, mc(M_ABS), mc(M_E), mc(M_U), mc(M_L), 7)
            act.wait_ge(d_dve, 5)
            act.activation(mcols[:, M_EDX, :], mcols[:, M_EDX, :], ACT.Exp).then_inc(d_act, 1)
            act.activation(mcols[:, M_DEC, :], mcols[:, M_DEC, :], ACT.Exp).then_inc(d_act, 1)

        def steps_pe(pe):
            pe.wait_ge(d_dve, 2)
            pe.matmul(bank[7][:, 0:128], triu[:, :], mcols[:, M_ADT, :], start=True, stop=True)
            pe.matmul(bank[7][:, 128:256], ones[:, :], mcols[:, M_ADT, :], start=True, stop=True).then_inc(d_pe, 1)

        xdt = [at(f"xdt{i}", 2 * i, [P, T]) for i in range(2)]
        xdec = [at(f"xdec{i}", 4 + 2 * i, [P, T]) for i in range(2)]
        b_tok = [at(f"b_tok{i}", 8 + 0.5 * i, [P, P]) for i in range(2)]
        egb = [at(f"egb{i}", 10 + 2 * i, [P, 4, P]) for i in range(2)]
        lw = [[at(f"lw{i}{j}", 14 + 4 * i + 2 * j, [P, 4, P]) for j in range(2)] for i in range(2)]
        cdec = [[at(f"cdec{i}{j}", 22 + 4 * i + 2 * j, [P, 4, P]) for j in range(2)] for i in range(2)]
        cbank = [bank[1], bank[7]]
        prev = at("prev", 120, [P, M_H, M_P])
        (m_xt, m_cb, m_gb, m_xd, m_dl, m_le, m_eg, m_w, m_bt, m_xe, m_cd, m_st, m_y, m_y1, m_yz, m_pd, m_pv) = (
            sem("m_" + n) for n in "xt cb gb xd dl le eg w bt xe cd st y y1 yz pd pv".split())

        def v8(x):
            return x.rearrange("p (h n) -> p h n", n=M_P)

        def ssd_pe(pe):
            pe.wait_ge(m_silu, XBC_TILES)
            pe.wait_ge(d_dve, 5)

            def pre(w):
                c, g = w // 4, w % 4
                tc = slice(c * P, c * P + P)
                ge(pe, m_xd, w)
                for k in range(4):
                    mm = pe.transpose(bank[0][:, k * P:k * P + P], xbc[:, 4 * g + k, tc], ident[:, :])
                mm.then_inc(m_xt, 1)
                ge(pe, m_w, 2 * w - 2)
                ge(pe, m_bt, w - 1)
                pe.transpose(cbank[g % 2][:, 0:P], xbc[:, 16 + g, tc], ident[:, :])
                pe.matmul(cbank[g % 2][:, P:2 * P], xbc[:, 16 + g, tc], xbc[:, 20 + g, tc], start=True, stop=True).then_inc(m_cb, 1)
                for f in range(2):
                    ge(pe, m_dl, 2 * w - 1 + f if w else 0)
                    ge(pe, m_eg, 2 * w - 1 + f if w else 0)
                    for k in range(4):
                        j = 8 * g + 4 * f + k
                        mm = pe.matmul(c4(bank[2 + f])[:, k, :], mc(M_ADT)[:, c, j:j + 1].to_broadcast([P, P]), triu[:, :],
                                       start=True, stop=True)
                    mm.then_inc(m_gb, 1)

            def main(w):
                c, g = w // 4, w % 4
                pe.wait_ge(m_bt, w + 1)
                pe.wait_ge(m_xe, w + 1)
                ge(pe, m_pv, w)
                pe.matmul(bank[6][:, :], b_tok[g % 2][:, :], xdec[g % 2][:, :], start=True, stop=True).then_inc(m_st, 1)
                for f in range(2):
                    pe.wait_ge(m_w, 2 * w + f + 1)
                    pe.wait_ge(m_cd, 2 * w + f + 1)
                    ge(pe, m_y1, w)
                    for k in range(4):
                        j = 4 * f + k
                        dst = bank[4 + f][64 * (k % 2):64 * (k % 2) + 64, (k // 2) * P:(k // 2) * P + P]
                        pe.matmul(dst, xdt[g % 2][:, j * M_P:j * M_P + M_P], lw[g % 2][f][:, k, :], start=True, stop=False)
                        mm = pe.matmul(dst, prev[:, 8 * g + j, :], cdec[g % 2][f][:, k, :], start=False, stop=True)
                    mm.then_inc(m_y, 1)
            pe.wait_ge(m_pv0, 1)
            pre(0)
            for w in range(16):
                if w < 15:
                    pre(w + 1)
                main(w)

        m_pv0 = sem("m_pv0")

        def ssd_act(act):
            def chunk(c):
                first = isinstance(c, int)
                for g in range(4):
                    w = c * 4 + g
                    act.wait_ge(m_cb, w + 1)
                    if not first or g >= 2:
                        act.wait_ge(m_st, w - 1)
                    act.activation(b_tok[g % 2][:, :], cbank[g % 2][:, 0:P], ACT.Copy).then_inc(m_bt, 1)
                    for f in range(2):
                        act.wait_ge(m_dl, 2 * w + f + 1)
                        if not first or g:
                            act.wait_ge(m_cd, 2 * w - 1 + f)
                        act.activation(egb[f][:, :, :], c4(bank[2 + f]), ACT.Exp).then_inc(m_eg, 1)
                        act.activation(lw[g % 2][f][:, :, :], lw[g % 2][f][:, :, :], ACT.Exp).then_inc(m_le, 1)
            turns(act, TT, 1, chunk, peel=True)

        def ssd_pool(pool):
            pool.wait_ge(d_act, 3)

            def past(c, g, w):
                pool.wait_ge(m_y, 2 * w + 2)
                ps = prev[:, 8 * g:8 * g + 8, :]
                pool.tensor_tensor(ps, ps, mcols[:, M_DEC, ds(c * M_H + 8 * g, 8)].unsqueeze(2).to_broadcast([P, 8, M_P]),
                                   ALU.mult).then_inc(m_pd, 1)
                pool.wait_ge(m_y1, w + 1)
                ys = xbc[:, 4 * g:4 * g + 4, ds(c * P, P)]
                pool.tensor_tensor(ys, ys, zT[:, 4 * g:4 * g + 4, ds(c * P, P)], ALU.mult).then_inc(m_yz, 1)

            def chunk(c):
                first = c == 0
                for g in range(4):
                    w = c * 4 + g
                    for f in range(2):
                        pool.wait_ge(m_eg, 2 * w + f + 1)
                        if not first or g >= 2:
                            pool.wait_ge(m_y, 2 * w - 3 + f)
                        pool.tensor_tensor(cdec[g % 2][f][:, :, :], bc4(xbc[:, 20 + g, ds(c * P, P)]), egb[f][:, :, :],
                                           ALU.mult).then_inc(m_cd, 1)
                    pool.wait_ge(m_xd, w + 1)
                    if not first or g >= 2:
                        pool.wait_ge(m_st, w - 1)
                    pool.tensor_tensor(v8(xdec[g % 2][:, :]), v8(xdt[g % 2][:, :]),
                                       mcols[:, M_EDX, ds(c * M_H + 8 * g, 8)].unsqueeze(2).to_broadcast([P, 8, M_P]),
                                       ALU.mult).then_inc(m_xe, 1)
                    if g:
                        past(c, g - 1, w - 1)
                    elif not first:
                        past(c - 1, 3, w - 1)
            for c in range(TT):
                chunk(c)
            past(3, 3, 15)

        def ssd_dve(dve):
            dve.memset(prev[:, :, :], 0.0).then_inc(m_pv0, 1)
            dve.wait_ge(d_act, 3)

            def finish(c, g, w):
                dve.wait_ge(m_y, 2 * w + 2)
                for k in range(4):
                    ys = xbc[:, 4 * g + k, ds(c * P, P)]
                    op = dve.scalar_tensor_tensor(ys, ys, pcol("m_d", 4 * g + k), bank[4 + k // 2][:, (k % 2) * P:(k % 2) * P + P],
                                                  ALU.mult, ALU.add)
                op.then_inc(m_y1, 1)
                dve.wait_ge(m_st, w + 1)
                dve.wait_ge(m_pd, w + 1)
                ps = prev[:, 8 * g:8 * g + 8, :]
                dve.tensor_tensor(ps, ps, v8(bank[6][:, :]), ALU.add).then_inc(m_pv, 1)

            def chunk(c):
                first = isinstance(c, int)
                for g in range(4):
                    w = c * 4 + g
                    dve.wait_ge(m_xt, w + 1)
                    if not first or g >= 2:
                        dve.wait_ge(m_y, 2 * w - 2)
                        dve.wait_ge(m_xe, w - 1)
                    dve.tensor_tensor(v8(xdt[g % 2][:, :]), v8(bank[0][:, :]),
                                      mcols[:, M_DT, ds(c * M_H + 8 * g, 8)].unsqueeze(2).to_broadcast([P, 8, M_P]),
                                      ALU.mult).then_inc(m_xd, 1)
                    for f in range(2):
                        dve.wait_ge(m_gb, 2 * w + f + 1)
                        for k in range(4):
                            op = dve.scalar_tensor_tensor(lw[g % 2][f][:, k, :], c4(bank[2 + f])[:, k, :],
                                                          mcols[:, M_CS, ds(c * M_H + (8 * g + 4 * f + k), 1)], upmask[:, :],
                                                          ALU.subtract, ALU.add)
                        op.then_inc(m_dl, 1)
                    if g:
                        finish(c, g - 1, w - 1)
                    elif not first:
                        finish(c - 1, 3, w - 1)
                    for f in range(2):
                        dve.wait_ge(m_le, 2 * w + f + 1)
                        dve.wait_ge(m_cb, w + 1)
                        dve.tensor_tensor(lw[g % 2][f][:, :, :], lw[g % 2][f][:, :, :], bc4(cbank[g % 2][:, P:2 * P]),
                                          ALU.mult).then_inc(m_w, 1)
            turns(dve, TT, 1, chunk, peel=True)
            finish(3, 3, 15)

        y_hi = at("y_hi", 0, [P, M_TILES, T], F32R)
        y_lo = at("y_lo", 40, [P, M_TILES, T], F32R)
        ycol = at("ycol", 120, [P, 3, 16])
        y_bc, y_n = sem("y_bc"), sem("y_n")

        def gnorm_pe(pe):
            for j in range(M_TILES):
                pe.wait_ge(hn_sq, 24 + j + 1)
                for c in range(TT):
                    n = (j // 4) * 4 + c
                    mm = pe.matmul(bank[2][:, n:n + 1], sq[:, j % 2, c * P:c * P + P], ones[:, 0:1],
                                   start=(j == 0 and c == 0), stop=(j % 4 == 3), skip_group_check=True)
                mm.then_inc(hn_ss, 1)
            pe.wait_ge(hn_rcp, 3)
            for g in range(M_G):
                ge(pe, y_n, 4 * (g - 1))
                for c in range(TT):
                    mm = pe.matmul(bank[6 + g % 2][:, c * P:c * P + P],
                                   ycol[:, 2, g * 4 + c:g * 4 + c + 1].to_broadcast([P, P]), ident[:, :],
                                   start=True, stop=True)
                mm.then_inc(y_bc, 1)

        def gnorm_act(act):
            act.wait_ge(m_yz, 16)
            for j in range(M_TILES):
                ge(act, hn_ss, 24 + j - 1)
                act.activation(sq[:, j % 2, :], xbc[:, j, :], ACT.Square).then_inc(hn_sq, 1)
            act.wait_ge(hn_var, 4)
            act.activation(ycol[:, 1, :], ycol[:, 0, :], ACT.Sqrt).then_inc(hn_std, 1)

            def body(j):
                act.wait_ge(y_n, j + 1)
                act.activation(y_hi[:, ds(j, 1), :], xb(j), ACT.Copy).then_inc(hn_hi, 1)
            turns(act, M_TILES, 1, body)

        def gnorm_dve(dve):
            dve.wait_ge(hn_ss, 24 + M_TILES)
            dve.tensor_scalar(ycol[:, 0, :], bank[2][:, 0:16], 1.0 / 512, EPS2, ALU.mult, ALU.add).then_inc(hn_var, 1)
            dve.wait_ge(hn_std, 3)
            dve.reciprocal(ycol[:, 2, :], ycol[:, 1, :]).then_inc(hn_rcp, 1)
            for g in range(M_G):
                dve.wait_ge(y_bc, g + 1)
                for k in range(4):
                    j = 4 * g + k
                    dve.scalar_tensor_tensor(xbc[:, j, :], xbc[:, j, :], pcol("m_norm_g", j), bank[6 + g % 2][:, :],
                                             ALU.mult, ALU.mult).then_inc(y_n, 1)
                for k in range(4):
                    j = 4 * g + k
                    dve.wait_ge(hn_hi, 8 + j + 1)
                    dve.tensor_tensor(y_lo[:, j, :], xbc[:, j, :], y_hi[:, j, :].bitcast(F32), ALU.subtract).then_inc(hn_lo, 1)

        def m_out_sp(sp):
            w = rows_k(t["m2_w_out"][0])
            sp_slots(sp, SLOTS["m_out"], 8, lambda i, s: halves(w, s, (i - s) * P, KD, KD * s))

        def m_out_pe(pe):
            pe.wait_ge(hn_lo, 8 + M_TILES)
            base = SLOTS["m_out"]

            def body(i):
                for s4 in range(4):
                    n, s, pair = base + i + s4, s4 % 2, s4 // 2
                    pe.wait_ge(lo_done, n + 1)
                    if s == 0:
                        pe.wait_ge(bank_free, 2 * n - 4)
                    for o in range(2):
                        for k in range(KD):
                            c = slice(k * 256 + o * P, k * 256 + o * P + P)
                            mm = three(pe, bank[2 * pair + o][:, :], w_hi[s][:, c], w_lo[s][:, c],
                                       y_hi[:, KD * s + k, :], y_lo[:, KD * s + k, :], s == 0 and k == 0, s == 1 and k == KD - 1)
                        mm.then_inc(gemm_ready, 1)
            turns(pe, 8, 4, body)

        def m_out_dve(dve, c):
            base = SLOTS["m_out"]
            squares_start(dve, c, SQ_B)

            def body(i):
                for pair in range(2):
                    for o in range(2):
                        dve.wait_ge(gemm_ready, 2 * (base + i + 2 * pair + 1) + o + 1)
                        hk = h[:, ds(i + (2 * pair + o), 1), :]
                        dve.scalar_tensor_tensor(hk, bank[2 * pair + o][:, :], modc(1, 16 + i + (2 * pair + o)), hk,
                                                 ALU.mult, ALU.add).then_inc(bank_free, 2)
                    squares(dve, c, i + 2 * pair, SQ_B, lambda o: (bank_free, i * 2 + 2 * (base + 2 * pair + o + 1)))
            turns(dve, 8, 4, body)

        o_tok = at("o_tok", 40, [P, TT, D])

        def end_pe(pe, c, lots):
            norm_pe(pe, c, SQ_B)
            for k in range(KD):
                pe.wait_ge(n_xt, KD * lots + k + 1)
                ge(pe, h_in, KD + k - 1)
                for b in range(TT):
                    mm = pe.transpose(bank[6 + k % 2][:, b * P:b * P + P], xt[:, k % 2, b * P:b * P + P], ident[:, :])
                mm.then_inc(x_t, 1)

        def end_act(act):
            for k in range(KD):
                act.wait_ge(x_t, KD + k + 1)
                act.activation(o_tok[:, :, k * P:k * P + P], c4(bank[6 + k % 2]), ACT.Copy).then_inc(h_in, 1)

        def end_dve(dve, c, lots):
            norm_root(dve, c, EPS2)
            for k in range(KD):
                if k >= 2:
                    dve.wait_ge(x_t, KD + k - 1)
                dve.scalar_tensor_tensor(xt[:, k % 2, :], h[:, k, :], pcol("final_g", k), RSTD, ALU.mult, ALU.mult).then_inc(n_xt, 1)

        def end_sp(sp):
            dst = out.rearrange("b (c p) d -> p (b c) d", p=P)
            for e in range(2):
                sp.wait_ge(h_in, KD + 4 * e + 4)
                sp.dma_start(dst[:, :, e * 512:e * 512 + 512], o_tok[:, :, e * 512:e * 512 + 512]).then_inc(stored, 16)
            sp.wait_ge(stored, 32)

        block = ctx.enter_context(nc.Block())

        @block.sync
        def _(sp):
            load_sp(sp)
            a_in_sp(sp)
            a_out_sp(sp)
            ffn_sp(sp, 0)
            kvq_sp(sp)
            b_out_sp(sp)
            strip_sp(sp)
            ffn_sp(sp, 1)
            s_in_sp(sp)
            s_load_sp(sp)
            glu_sp(sp)
            mlp_sp(sp, 0)
            m_in_sp(sp)
            m_out_sp(sp)
            mlp_sp(sp, 1)
            end_sp(sp)

        @block.gpsimd
        def _(pool):
            done = [0]

            def upto(name):
                n = SLOTS[name] + 2
                pool_slots(pool, done[0], n - done[0])
                done[0] = n
            upto("a_out")
            inside_pool(pool)
            upto("b_out")
            strip_pool(pool)
            upto("s_glu")
            s5_pool(pool)
            upto("m_out")
            ssd_pool(pool)
            pool_slots(pool, done[0], TOTAL - done[0])

        @block.scalar
        def _(act):
            load_act(act)
            for s in range(2):
                split_hi(act, s, s, landed(0))
            norm_act(act, 0, 0)
            a_in_act(act)
            gates_act(act)
            unit_act(act)
            inside_act(act)
            across_act(act)
            onorm_act(act)
            act_slots(act, "a_out", no_read)
            norm_act(act, 1, 1, slot=SLOTS["f0_up0"])
            ffn_act(act, 0, 2)
            norm_act(act, 2, 2, slot=SLOTS["b_k"])
            kv_act(act)
            norm_hi(act, 3, SLOTS["b_q"])
            q_act(act)
            attn_act(act)
            act_slots(act, "b_out", no_read)
            norm_act(act, 3, 4, slot=SLOTS["f1_up0"])
            ffn_act(act, 1, 5)
            norm_act(act, 4, None, split=False)
            norm_act(act, 5, 5, shift=lambda k: mod[:, 0, k:k + 1], slot=SLOTS["s_in"])
            s_par_act(act)
            s_in_act(act)
            s_gelu_act(act)
            glu_act(act)
            norm_act(act, 6, 6, shift=lambda k: mod[:, 0, 24 + k:25 + k], slot=SLOTS["p0"])
            mlp_act(act, 0)
            norm_act(act, 7, 7, shift=lambda k: mod[:, 1, k:k + 1], slot=SLOTS["m_in"])
            m_in_act(act)
            steps_act(act)
            ssd_act(act)
            gnorm_act(act)
            act_slots(act, "m_out", no_read)
            norm_act(act, 8, 8, shift=lambda k: mod[:, 1, 24 + k:25 + k], slot=SLOTS["p1"])
            mlp_act(act, 1)
            norm_act(act, 9, None, split=False)
            end_act(act)

        @block.tensor
        def _(pe):
            pe.wait_ge(ones_set, 4)
            load_pe(pe)
            norm_pe(pe, 0, SQ_B)
            a_in_pe(pe)
            gates_pe(pe)
            unit_pe(pe)
            inside_pe(pe)
            across_pe(pe)
            onorm_pe(pe)
            a_out_pe(pe)
            norm_pe(pe, 1, SQ_B)
            ffn_pe(pe, 0, 1)
            norm_pe(pe, 2, SQ_X)
            kvq_pe(pe, 2)
            attn_pe(pe)
            b_out_pe(pe)
            norm_pe(pe, 3, SQ_B)
            ffn_pe(pe, 1, 4)
            norm_pe(pe, 4, SQ_X)
            norm_pe(pe, 5, SQ_B)
            s_in_pe(pe, 5)
            s5_pe(pe)
            glu_pe(pe)
            norm_pe(pe, 6, SQ_B)
            mlp_pe(pe, 0, 6)
            norm_pe(pe, 7, SQ_B)
            m_in_pe(pe, 7)
            steps_pe(pe)
            ssd_pe(pe)
            gnorm_pe(pe)
            m_out_pe(pe)
            norm_pe(pe, 8, SQ_B)
            mlp_pe(pe, 1, 8)
            end_pe(pe, 9, 9)

        @block.vector
        def _(dve):
            load_dve(dve)
            norm_dve(dve, 0, 0, lambda k: pcol("a_norm", k), EPS1)
            a_in_dve(dve)
            gates_dve(dve)
            unit_dve(dve)
            inside_dve(dve)
            across_dve(dve)
            onorm_dve(dve)
            add_h_slots(dve, SLOTS["a_out"], 1)
            norm_dve(dve, 1, 1, lambda k: pcol("f_norm", k), EPS1, slot=SLOTS["f0_up0"])
            ffn_dve(dve, 0, 2)
            norm_dve(dve, 2, 2, lambda k: pcol("kv_norm", k), EPS1, slot=SLOTS["b_k"])
            norm_dve(dve, 2, 3, lambda k: pcol("b_norm", k), EPS1, slot=SLOTS["b_q"], root=False)
            attn_dve(dve)
            add_h_slots(dve, SLOTS["b_out"], 3)
            norm_dve(dve, 3, 4, lambda k: pcol("f_norm", 8 + k), EPS1, slot=SLOTS["f1_up0"])
            ffn_dve(dve, 1, 4)
            mid_dve(dve, 4, 5)
            norm_dve(dve, 5, 5, lambda k: gainc(0, k), EPS2, shift=lambda k: mod[:, 0, k:k + 1], slot=SLOTS["s_in"])
            s_par_dve(dve)
            s5_dve(dve)
            s_gelu_dve(dve)
            glu_dve(dve, 6)
            norm_dve(dve, 6, 6, lambda k: gainc(0, 8 + k), EPS2, shift=lambda k: mod[:, 0, 24 + k:25 + k], slot=SLOTS["p0"])
            mlp_dve(dve, 0, 7)
            norm_dve(dve, 7, 7, lambda k: gainc(1, k), EPS2, shift=lambda k: mod[:, 1, k:k + 1], slot=SLOTS["m_in"])
            m_in_dve(dve)
            steps_dve(dve)
            ssd_dve(dve)
            gnorm_dve(dve)
            m_out_dve(dve, 8)
            norm_dve(dve, 8, 8, lambda k: gainc(1, 8 + k), EPS2, shift=lambda k: mod[:, 1, 24 + k:25 + k], slot=SLOTS["p1"])
            mlp_dve(dve, 1, 9)
            end_dve(dve, 9, 9)


def lay_out(inp):
    def cols(v):
        return np.ascontiguousarray(np.asarray(v).reshape(-1, P).T)

    def a(name):
        return np.asarray(inp[name])
    parts = {
        "a_norm": cols(a("a_norm")), "kv_norm": cols(a("kv_norm")), "b_norm": cols(a("b_norm")),
        "f_norm": cols(a("f_norm")), "final_norm": cols(a("final_norm")), "mix_g": cols(a("norm_mix_g_2")),
        "mlp_g": cols(a("norm_mlp_g_2")), "final_g": cols(a("final_norm_g_2")), "a_conv": cols(a("a_conv")),
        "a_out_norm": cols(a("a_out_norm")), "f_conv": cols(a("f_conv")), "f_conv_b": cols(a("f_conv_b")),
        "cond": cols(a("c_2")), "ada_b": cols(a("ada_b_2")), "s5_d": cols(a("s5_d_2")), "s5_b_glu": cols(a("s5_b_glu_2")),
        "lam_re": cols(a("s5_lambda_re_2")), "lam_im": cols(a("s5_lambda_im_2")),
        "log_dt": cols(np.repeat(a("s5_log_dt_2").reshape(-1), 64)),
        "m_conv": cols(a("m2_conv_w_2")), "m_conv_b": cols(a("m2_conv_b_2")),
        "m_d": cols(np.repeat(a("m2_d_2").reshape(-1), M_P)), "m_norm_g": cols(a("m2_norm_g_2")),
        "qmask": np.kron(np.eye(4, dtype=np.float32), np.ones((32, 1), np.float32)),
    }
    par = np.zeros((P, PAR_N), np.float32)
    for name, v in parts.items():
        par[:, PAR[name]:PAR[name] + v.shape[1]] = v
    rows = np.concatenate([a(n).reshape(-1) for n in ("a_A_log", "a_dt_bias", "m2_a_log_2", "m2_dt_bias_2")])
    rel = np.clip(384 + np.arange(P)[:, None] - np.arange(T)[None, :], -256, 256) + 256
    strips = np.ascontiguousarray(a("b_rel_bias")[0][:, rel])
    bt = np.zeros((P, 2, S5Q, P), np.float32)
    ct = np.zeros((P, 2, S5N, 32), np.float32)
    for x, (b, c) in enumerate((("s5_b_re_2", "s5_c_re_2"), ("s5_b_im_2", "s5_c_im_2"))):
        for g in range(64):
            q, r = g // 8, 16 * (g % 8)
            e = 64 * (g % 2)
            bt[r:r + 16, x, q, e:e + 64] = a(b)[0, g].T
            ct[e:e + 64, x, g // 2, 16 * (g % 2):16 * (g % 2) + 16] = a(c)[0, g].T
    i = np.arange(P)
    lev = np.stack([(i[None, :] // (2 * s) == i[:, None] // (2 * s)) & (i[None, :] // s % 2 == 1) & (i[:, None] // s % 2 == 0)
                    for s in (1, 2, 4, 8, 16, 32, 64)], axis=1).astype(np.float32)
    upper = i[:, None] <= i[None, :]
    return {
        "x": a("x"), "par": par, "rows": rows[None, :], "strips": strips, "s5_bt": bt, "s5_ct": ct,
        "ident": np.eye(P, dtype=np.float32), "triu": upper.astype(np.float32),
        "upmask": np.where(upper, 0.0, NEG).astype(np.float32), "lev": lev,
        "a_w_in": a("a_w_in"), "a_w_out": a("a_w_out"), "f_w_up": a("f_w_up"), "f_w_down": a("f_w_down"),
        "w_kv": a("w_kv"), "b_w_q": a("b_w_q"), "b_w_out": a("b_w_out"), "ada_w": a("ada_w_2"),
        "s5_w_in": a("s5_w_in_2"), "s5_w_glu": a("s5_w_glu_2"), "mlp_w1": a("mlp_w1_2"), "mlp_w2": a("mlp_w2_2"),
        "m2_w_in": a("m2_w_in_2"), "m2_w_out": a("m2_w_out_2"),
    }


def kernel(**inputs):
    import concourse.bacc as bacc
    from concourse.bass_utils import run_bass_kernel_spmd

    nc = bacc.Bacc("TRN2", target_bir_lowering=False, num_devices=1)
    arrays = {f"in_{n}": np.ascontiguousarray(v) for n, v in lay_out(inputs).items()}
    t = {n[3:]: nc.dram_tensor(n, v.shape, mybir.dt.from_np(v.dtype), kind="ExternalInput").ap() for n, v in arrays.items()}
    out = nc.dram_tensor("out", (1, T, D), F32, kind="ExternalOutput").ap()
    build(nc, t, out)
    return run_bass_kernel_spmd(nc, [arrays], core_ids=[0]).results[0]["out"]
```

```python
from contextlib import ExitStack

import numpy as np
import concourse.bass as bass
from concourse import mybir

F32 = mybir.dt.float32
F32R = mybir.dt.float32r
ALU = mybir.AluOpType
ACT = mybir.ActivationFunctionType
AX = mybir.AxisListType

P = 128
T = 512
TT = T // P
D = 1024
KD = D // P
SLOT = 2048
AH = 8
A_W = 1024
F_DIM = 2816
F_TILES = F_DIM // P
F_CHUNKS = (8, 8, 6)
F_START = (0, 8, 16)
BH = 16
BD = 64
EPS1 = 1e-6
NEG = -1e30
EPS2 = 1e-5
S5Q = 8
S5N = 32
D_FF = 4096
M_H = 32
M_P = 64
M_G = 4
M_INNER = 2048
M_TILES = M_INNER // P
XBC_TILES = 24

SLOTS = {}
TOTAL = 0
for _name, _n in (("a_in", 16), ("a_out", 4),
                  ("f0_up0", 8), ("f0_dn0", 4), ("f0_up1", 8), ("f0_dn1", 4), ("f0_up2", 6), ("f0_dn2", 4),
                  ("b_k", 4), ("b_v", 4), ("b_q", 4), ("b_out", 4),
                  ("f1_up0", 8), ("f1_dn0", 4), ("f1_up1", 8), ("f1_dn1", 4), ("f1_up2", 6), ("f1_dn2", 4),
                  ("s_in", 4), ("s_glu", 8), ("p0", 32), ("m_in", 20), ("m_out", 8), ("p1", 32)):
    SLOTS[_name] = TOTAL
    TOTAL += _n

PAR = {}
PAR_N = 0
for _name, _n in (("a_norm", 8), ("kv_norm", 8), ("b_norm", 8), ("f_norm", 16), ("final_norm", 8),
                  ("mix_g", 16), ("mlp_g", 16), ("final_g", 8), ("a_conv", 4 * 24), ("a_out_norm", 1),
                  ("f_conv", 2 * 3 * 44), ("f_conv_b", 2 * 44), ("cond", 8), ("ada_b", 2 * 48),
                  ("s5_d", 8), ("s5_b_glu", 16), ("lam_re", 32), ("lam_im", 32), ("log_dt", 32),
                  ("m_conv", 4 * 24), ("m_conv_b", 24), ("m_d", 16), ("m_norm_g", 16), ("qmask", 4),
                  ("unit_scale", 1), ("unit_eps", 1), ("one_col", 63)):
    PAR[_name] = PAR_N
    PAR_N += _n
ROW = {"a_A_log": 0, "a_dt_bias": 8, "m_a_log": 16, "m_dt_bias": 48}
ROW_N = 80


def ge(eng, sem, value):
    if isinstance(value, int) and value <= 0:
        return
    eng.wait_ge(sem, value)


def turns(eng, count, step, body, peel=False, start=0):
    if peel:
        body(start)
        start += step
    if start < count:
        if count - start == step:
            body(start)
        else:
            with eng.Fori(start // step, count // step) as i:
                body(i * step if step > 1 else i)


def ds(start, size):
    return slice(start, start + size) if isinstance(start, int) else bass.ds(start, size)


def build(nc, t, out):
    ctx = ExitStack()
    with ctx:
        def sb(name, shape, dt=F32):
            return ctx.enter_context(nc.sbuf_tensor(name, shape, dt))

        def sem(name):
            return ctx.enter_context(nc.semaphore(name))

        w_raw = [sb(f"w_raw{i}", [P, SLOT]) for i in range(2)]
        w_hi = [sb(f"w_hi{i}", [P, SLOT], F32R) for i in range(2)]
        w_lo = [sb(f"w_lo{i}", [P, SLOT], F32R) for i in range(2)]
        h = sb("h", [P, KD, T])
        par = sb("par", [P, PAR_N])
        rows = sb("rows", [P, ROW_N])
        ident = sb("ident", [P, P])
        triu = sb("triu", [P, P])
        upmask = sb("upmask", [P, P])
        ones = sb("ones", [P, P])
        mod = sb("mod", [P, 2, 48])
        gain = sb("gain", [P, 2, 16])
        cond = sb("cond", [P, 8])
        ncol = sb("ncol", [P, 3, TT])
        eps_col = sb("eps_col", [P, 2])
        nar_hi = sb("nar_hi", [P, KD, 32], F32R)
        nar_lo = sb("nar_lo", [P, KD, 32], F32R)
        arena = nc.sbuf_base
        room = nc.sbuf_usable_end - arena

        def at(name, kb, shape, dt=F32):
            size = 4 * int(np.prod(shape[1:]))
            assert kb * 1024 + size <= room, (name, kb, size, room)
            return nc.alloc_sbuf_tensor_at(name, shape, dt, offset=arena + int(kb * 1024))

        bank = [ctx.enter_context(nc.psum_tensor(f"bank{i}", [P, 512], F32)) for i in range(8)]

        def pcol(name, i=0):
            return par[:, PAR[name] + i:PAR[name] + i + 1] if isinstance(i, int) else par[:, bass.ds(i + PAR[name], 1)]

        raw_landed = [sem("raw_landed0"), sem("raw_landed1")]
        hi_done = sem("hi_done")
        lo_done = sem("lo_done")
        gemm_ready = sem("gemm_ready")
        bank_free = sem("bank_free")
        const_in = sem("const_in")
        x_in = sem("x_in")
        stored = sem("stored")

        lev = at("lev", 128, [P, 7, P])
        x_hi = at("x_hi", 0, [P, KD, T], F32R)
        x_lo = at("x_lo", 16, [P, KD, T], F32R)
        sq = at("sq", 32, [P, 2, T])
        xt = at("xt", 36, [P, 2, T])

        def sp_slots(sp, base, count, load, peel=False):
            def body(i):
                for s in range(2):
                    ge(sp, lo_done, base + i + s - 1)
                    for dst, src in load(i + s, s):
                        sp.dma_start(dst, src).then_inc(raw_landed[s], 16)
            turns(sp, count, 2, body, peel)

        def halves(w, s, col, kt=KD, k0=0):
            hk = kt // 2
            raw = w_raw[s][:, 0:kt * 256].rearrange("p (k n) -> p k n", n=256)
            return [(raw[:, 0:hk, :], w[:, ds(k0, hk), ds(col, 256)]),
                    (raw[:, hk:kt, :], w[:, ds(k0 + hk, kt - hk), ds(col, 256)])]

        def both(w, s, col_a, col_b):
            raw = w_raw[s][:, :].rearrange("p (k g n) -> p k g n", g=2, n=P)
            return [(raw[:, :, 0, :], w[:, :, ds(col_a, P)]), (raw[:, :, 1, :], w[:, :, ds(col_b, P)])]

        def rows_k(w):
            return w.rearrange("(k p) n -> p k n", p=P)

        def landed(n):
            return n * 16 + 32

        def slot_count(name):
            n = list(SLOTS.values()) + [TOTAL]
            k = list(SLOTS).index(name)
            return n[k + 1] - n[k]

        names = list(SLOTS)
        def split_hi(act, n, s, value):
            act.wait_ge(raw_landed[s], value)
            ge(act, gemm_ready, 2 * n - 2)
            act.activation(w_hi[s][:, :], w_raw[s][:, :], ACT.Copy).then_inc(hi_done, 1)

        def act_slots(act, name, evac, first=0, count=None, step=2, base=None, peel=False):
            base = SLOTS[name] if base is None else base
            count = slot_count(name) if count is None else count

            def body(i, ahead=True):
                for s in range(step):
                    n = base + first + i + s
                    if ahead or s < step - 2:
                        split_hi(act, n + 2, s % 2, landed(base + first + i + s - s % 2 + 2))
                    evac(first + i + s, s)
            if isinstance(base, int) and base + first + count == TOTAL:
                turns(act, count - step, step, body, peel)
                body(count - step, ahead=False)
            else:
                turns(act, count, step, body, peel)

        def pool_slots(pool, first, count):
            def body(i):
                for s in range(2):
                    n = first + i + s
                    pool.wait_ge(hi_done, n + 1)
                    ge(pool, gemm_ready, 2 * n - 2)
                    pool.tensor_tensor(w_lo[s][:, :], w_raw[s][:, :], w_hi[s][:, :].bitcast(F32),
                                       ALU.subtract).then_inc(lo_done, 1)
            turns(pool, count, 2, body, peel=first == 0)

        def pe_slot_start(pe, n):
            pe.wait_ge(lo_done, n + 1)
            ge(pe, bank_free, 2 * n - 2)

        def three(pe, dst, hi_l, lo_l, hi_r, lo_r, start, stop):
            pe.matmul(dst, hi_l, hi_r, start=start, stop=False)
            pe.matmul(dst, hi_l, lo_r, start=False, stop=False)
            return pe.matmul(dst, lo_l, hi_r, start=False, stop=stop)

        def first_turn(pe, base, rhs_hi, rhs_lo, ready, kt=KD):
            pe_slot_start(pe, base)
            for k in range(kt):
                pe.wait_ge(*ready(k))
                for o in range(2):
                    c = slice(k * 256 + o * P, k * 256 + o * P + P)
                    mm = three(pe, bank[o][:, :], w_hi[0][:, c], w_lo[0][:, c], rhs_hi[:, k, :], rhs_lo[:, k, :],
                               k == 0, k == kt - 1)
                    if k == kt - 1:
                        mm.then_inc(gemm_ready, 1)
            slot_body(pe, base + 1, rhs_hi, rhs_lo, kt, (1,))(0)

        def projection(pe, name, rhs_hi, rhs_lo, ready, kt=KD, count=None, base=None):
            base = SLOTS[name] if base is None else base
            first_turn(pe, base, rhs_hi, rhs_lo, ready, kt)
            turns(pe, slot_count(name) if count is None else count, 2, slot_body(pe, base, rhs_hi, rhs_lo, kt), start=2)

        def normed(lots):
            return lambda k: (n_lo, KD * lots + k + 1)

        def slot_body(pe, base, rhs_hi, rhs_lo, kt=KD, parities=(0, 1)):
            def body(i):
                for s in parities:
                    pe_slot_start(pe, base + i + (s - parities[0]))
                    for o in range(2):
                        for k in range(kt):
                            c = slice(k * 256 + o * P, k * 256 + o * P + P)
                            mm = three(pe, bank[2 * s + o][:, :], w_hi[s][:, c], w_lo[s][:, c],
                                       rhs_hi[:, k, :], rhs_lo[:, k, :], k == 0, k == kt - 1)
                        mm.then_inc(gemm_ready, 1)
            return body

        n_sq, n_acc, n_ss, n_std, n_rcp, n_bc = (sem("n_" + n) for n in "sq acc ss std rcp bc".split())
        n_xt, n_hi, n_lo = sem("n_xt"), sem("n_hi"), sem("n_lo")
        hn_sq, hn_ss, hn_std, hn_rcp, hn_bc, hn_hi, hn_lo = (sem("hn_" + n) for n in "sq ss std rcp bc hi lo".split())
        tap_first, tap_mid = sem("tap_first"), sem("tap_mid")
        RSTD = bank[5][:, :]

        SQ_X = (at("sq_x", 0, [P, 2, T]), at("sq_x_sum", 4, [P, T]))
        SQ_B = (sq, at("sq_sum", 36, [P, T]))

        def squared(c):
            return TT + 9 * (c - 1)

        def squares_start(dve, c, sqs):
            ge(dve, n_ss, c - 1)
            dve.memset(sqs[1][:, :], 0.0).then_inc(n_acc, 1)

        def square(dve, c, k, o, sqs, sem_h, value):
            dve.wait_ge(sem_h, value)
            dve.wait_ge(n_acc, k + squared(c))
            hk = h[:, ds(k, 1), :]
            dve.tensor_tensor(sqs[0][:, o, :], hk, hk, ALU.mult).then_inc(n_sq, 1)
            dve.wait_ge(n_sq, k + (KD * c - KD + 1))
            dve.wait_ge(n_acc, k + (squared(c) + 1))
            dve.tensor_tensor(sqs[1][:, :], sqs[1][:, :], sqs[0][:, o, :], ALU.add).then_inc(n_acc, 1)

        def norm_pe(pe, c, sqs):
            norm_sums_pe(pe, c, sqs)
            norm_spread_pe(pe, c)

        def norm_sums_pe(pe, c, sqs):
            pe.wait_ge(n_acc, squared(c + 1))
            for j in range(TT):
                mm = pe.matmul(bank[4][:, j:j + 1], sqs[1][:, j * P:j * P + P], ones[:, 0:1], start=True, stop=True)
            mm.then_inc(n_ss, 1)

        def norm_spread_pe(pe, c):
            pe.wait_ge(n_rcp, c + 1)
            for j in range(TT):
                mm = pe.matmul(bank[5][:, j * P:j * P + P], ncol[:, 2, j:j + 1].to_broadcast([P, P]), ident[:, :],
                               start=True, stop=True)
            mm.then_inc(n_bc, 1)

        def norm_hi(act, lots, slot, shift=None):
            ge(act, gemm_ready, 2 * slot)
            for k in range(KD):
                act.wait_ge(n_xt, KD * lots + k + 1)
                if shift is None:
                    act.activation(x_hi[:, k, :], xt[:, k % 2, :], ACT.Copy).then_inc(n_hi, 1)
                else:
                    act.activation(x_hi[:, k, :], xt[:, k % 2, :], ACT.Identity, bias=shift(k)).then_inc(n_hi, 1)

        def norm_act(act, c, eps, lots=0, shift=None, split=True, slot=0):
            act.wait_ge(n_ss, c)
            act.activation(ncol[:, 1, :], bank[4][:, 0:TT], ACT.Sqrt, bias=eps_col[:, eps:eps + 1],
                           scale=1.0 / D).then_inc(n_std, 1)
            if split:
                norm_hi(act, lots, slot, shift)

        def norm_root(dve, c):
            dve.wait_ge(n_std, c + 1)
            dve.reciprocal(ncol[:, 2, :], ncol[:, 1, :]).then_inc(n_rcp, 1)
            dve.wait_ge(n_bc, c + 1)

        def norm_dve(dve, c, lots, g, shift=None, slot=0, root=True):
            if root:
                norm_root(dve, c)
            ge(dve, gemm_ready, 2 * slot)

            def low(k):
                dve.wait_ge(n_hi, KD * lots + k + 1)
                if shift is None:
                    dve.tensor_tensor(x_lo[:, k, :], xt[:, k % 2, :], x_hi[:, k, :].bitcast(F32),
                                      ALU.subtract).then_inc(n_lo, 1)
                else:
                    dve.scalar_tensor_tensor(x_lo[:, k, :], xt[:, k % 2, :], shift(k), x_hi[:, k, :].bitcast(F32),
                                             ALU.add, ALU.subtract).then_inc(n_lo, 1)
            for k in range(KD):
                if k >= 2:
                    dve.wait_ge(n_lo, KD * lots + k - 1)
                dve.scalar_tensor_tensor(xt[:, k % 2, :], h[:, k, :], g(k), RSTD, ALU.mult, ALU.mult).then_inc(n_xt, 1)
                if k >= 1:
                    low(k - 1)
            low(KD - 1)

        def add_h(dve, base, i, s, c, sqs):
            for o in range(2):
                n = 2 * (base + i) + o + 1
                dve.wait_ge(gemm_ready, n)
                hk = h[:, ds(i * 2 + o, 1), :]
                dve.tensor_tensor(hk, bank[2 * s + o][:, :], hk, ALU.add).then_inc(bank_free, 1)
                if c is not None:
                    square(dve, c, i * 2 + o, o, sqs, bank_free, n)

        x_tok = at("x_tok", 40, [P, TT, D])
        x_t, h_in = sem("x_t"), sem("h_in")

        def load_sp(sp):
            sp.dma_start(ident[:, :], t["ident"]).then_inc(const_in, 16)
            sp.dma_start(x_tok[:, :, :], t["x"].rearrange("b (c p) d -> p (b c) d", p=P)).then_inc(x_in, 16)
            sp.dma_start(par[:, :], t["par"]).then_inc(const_in, 16)
            sp.dma_start(nar_raw[:, :, 0:16], t["a_w_in"].rearrange("b (k p) n -> p (b k) n", p=P)[:, :, 4096:4112]).then_inc(const_in, 16)

        def load_late_sp(sp):
            sp.dma_start(triu[:, :], t["triu"]).then_inc(late_in, 16)
            sp.dma_start(upmask[:, :], t["upmask"]).then_inc(late_in, 16)
            sp.dma_start(lev[:, :, :], t["lev"]).then_inc(late_in, 16)
            sp.dma_start(rows[:, :], t["rows"].partition_broadcast(P)).then_inc(late_in, 16)

        CONST, LATE = 16 * 3, 16 * 4
        late_in = sem("late_in")
        ones_set = sem("ones_set")
        x_sq = at("x_sq", 56, [P, TT, D])

        def load_pe(pe):
            pe.wait_ge(x_in, 16)
            pe.wait_ge(const_in, CONST)
            for k in range(KD):
                ge(pe, h_in, k - 3)
                for c in range(TT):
                    mm = pe.transpose(bank[k % 4][:, c * P:c * P + P], x_tok[:, c, k * P:k * P + P], ident[:, :])
                mm.then_inc(x_t, 1)

        def load_act(act):
            act.wait_ge(ones_set, 4)
            act.wait_ge(x_in, 16)
            for c in range(TT):
                act.activation(x_sq[:, c, :], x_tok[:, c, :], ACT.Square, accum_out=ncol[:, 0, c:c + 1]).then_inc(n_acc, 1)
            act.wait_ge(n_acc, TT)
            act.activation(ncol[:, 1, :], ncol[:, 0, :], ACT.Sqrt, bias=eps_col[:, 0:1], scale=1.0 / D).then_inc(n_std, 1)
            for s in range(2):
                split_hi(act, s, s, landed(0))
            norm_hi(act, 0, 0)
            act.wait_ge(const_in, CONST)
            narrow_hi_act(act)

        cond_in = sem("cond_in")

        def load_dve(dve):
            dve.memset(ones[:, :], 1.0).then_inc(ones_set, 1)
            dve.memset(eps_col[:, 0:1], EPS1).then_inc(ones_set, 1)
            dve.memset(eps_col[:, 1:2], EPS2).then_inc(ones_set, 1)
            dve.memset(nar_raw[:, :, 16:32], 0.0).then_inc(ones_set, 1)
            for k in range(KD):
                dve.wait_ge(x_t, k + 1)
                dve.tensor_copy(h[:, k, :], bank[k % 4][:, :]).then_inc(h_in, 1)
            dve.wait_ge(h_in, KD)

        qkvz = at("qkvz", 40, [P, 32, T])
        ba_ready = sem("ba_ready")
        silu_done = sem("silu_done")
        BA = bank[6][:, 0:TT * 16].rearrange("p (c n) -> p c n", n=16)

        def qkv(j, a=0, b=T):
            return qkvz[:, ds(j, 1), a:b]

        nar_raw = at("nar_raw", 124, [P, KD, 32])
        nar = at("nar", 122, [32, T])
        nar_split, nar_proj, nar_out = sem("nar_split"), sem("nar_proj"), sem("nar_out")

        def narrow_pe(pe, nth):
            pe.wait_ge(nar_split, 2 * nth)
            for k in range(KD):
                mm = three(pe, bank[7][0:32, :], nar_hi[:, k, :], nar_lo[:, k, :], x_hi[:, k, :], x_lo[:, k, :],
                           k == 0, k == KD - 1)
            mm.then_inc(nar_proj, 1)

        def narrow_turn_pe(pe, nth, dst, n, done):
            pe.wait_ge(nar_out, nth)
            for c in range(TT):
                mm = pe.matmul(dst[:, c, :], nar[:, c * P:c * P + P], ident[0:32, 0:n], start=True, stop=True)
            mm.then_inc(done, 1)

        def narrow_hi_act(act):
            act.activation(nar_hi[:, :, :], nar_raw[:, :, :], ACT.Copy).then_inc(nar_split, 1)

        def narrow_lo_dve(dve, nth):
            dve.wait_ge(nar_split, 2 * nth - 1)
            dve.tensor_tensor(nar_lo[:, :, :], nar_raw[:, :, :], nar_hi[:, :, :].bitcast(F32),
                              ALU.subtract).then_inc(nar_split, 1)

        def narrow_out_act(act, nth):
            act.wait_ge(nar_proj, nth)
            act.activation(nar[:, :], bank[7][0:32, :], ACT.Copy).then_inc(nar_out, 1)

        def a_in_sp(sp):
            w = rows_k(t["a_w_in"][0])
            sp_slots(sp, 0, 2, lambda i, s: halves(w, s, i * 256), peel=True)
            load_late_sp(sp)
            sp_slots(sp, 2, 14, lambda i, s: halves(w, s, i * 256 + 512))

        def a_in_pe(pe):
            first_turn(pe, 0, x_hi, x_lo, normed(0))
            narrow_pe(pe, 1)
            body = slot_body(pe, 0, x_hi, x_lo)
            body(2)
            narrow_turn_pe(pe, 1, BA, 16, ba_ready)
            turns(pe, 14, 2, body, start=4)
            gates_pe(pe)
            unit_sums_pe(pe)
            body(14)
            unit_spread_pe(pe)

        def a_in_act(act):
            def silu(j):
                for o in range(2):
                    act.activation(qkv(j + o), qkv(j + o), ACT.Silu).then_inc(silu_done, 1)

            def conv(i, s):
                for o in range(2):
                    act.wait_ge(gemm_ready, 2 * i + o + 1)
                    act.activation(qkv(2 * i + o), bank[2 * s + o][:, :], ACT.Copy,
                                   scale=pcol("a_conv", 3 * 24 + 2 * i + o)).then_inc(tap_first, 1)
                if not (isinstance(i, int) and i == 0):
                    act.wait_ge(bank_free, 2 * i)
                    silu(2 * i - 2)

            def gate(i, s):
                for o in range(2):
                    act.wait_ge(gemm_ready, 2 * i + o + 1)
                    act.activation(qkv(2 * i + o), bank[2 * s + o][:, :], ACT.Silu).then_inc(bank_free, 1)
            act_slots(act, "a_in", conv, 0, 2, peel=True)
            narrow_out_act(act, 1)
            act_slots(act, "a_in", conv, 2, 10)
            act.wait_ge(bank_free, 24)
            silu(22)
            gates_steps_act(act)
            act_slots(act, "a_in", gate, 12, 2)
            gates_exp_act(act)
            unit_act(act)
            act_slots(act, "a_in", gate, 14, 2)

        def a_in_dve(dve):
            def body(i):
                for s in range(2):
                    for o in range(2):
                        j = 2 * (i + s) + o
                        dve.wait_ge(tap_first, j + 1)
                        for d in (1, 2, 3):
                            if d > 1:
                                dve.wait_ge(tap_mid, 2 * j + d - 1)
                            dve.scalar_tensor_tensor(qkv(j, d), bank[2 * s + o][:, 0:T - d], pcol("a_conv", (3 - d) * 24 + j),
                                                     qkv(j, d), ALU.mult, ALU.add).then_inc(tap_mid if d < 3 else bank_free, 1)
            turns(dve, 12, 2, body)

        gcols = at("gcols", 131.5, [P, 14, 32])

        def gc(n):
            return gcols[:, n, :].rearrange("p (c h) -> p c h", h=AH)
        BETA, A_X, A_ABS, A_E, A_U, A_L, A_G, GCUM, GEND, EGC, EDX, DEC, NBG, EXPA = range(14)
        sp_d, sp_a = sem("softplus_dve"), sem("softplus_act")
        g_pe, g_act, g_dve = sem("gates_pe"), sem("gates_act"), sem("gates_dve")

        def softplus_dve(dve, base, x, ab, e, u, l, res, d0, a0):
            dve.scalar_tensor_tensor(ab, x, -1.0, x, ALU.mult, ALU.min).then_inc(sp_d, 1)
            dve.wait_ge(sp_a, a0 + 1)
            dve.tensor_scalar(u, e, 1.0, None, ALU.add).then_inc(sp_d, 1)
            dve.wait_ge(sp_d, d0 + 2)
            dve.scalar_tensor_tensor(e, u, -1.0, e, ALU.add, ALU.subtract).then_inc(sp_d, 1)
            dve.wait_ge(sp_a, a0 + 2)
            dve.reciprocal(u, u).then_inc(sp_d, 1)
            dve.wait_ge(sp_d, d0 + 4)
            dve.tensor_tensor(e, e, u, ALU.mult).then_inc(sp_d, 1)
            dve.scalar_tensor_tensor(l, x, 0.0, l, ALU.max, ALU.add).then_inc(sp_d, 1)
            dve.wait_ge(sp_d, d0 + 6)
            dve.tensor_tensor(res, l, e, ALU.subtract).then_inc(sp_d, 1)

        def softplus_act(act, ab, e, u, l, d0):
            act.wait_ge(sp_d, d0 + 1)
            act.activation(e, ab, ACT.Exp).then_inc(sp_a, 1)
            act.wait_ge(sp_d, d0 + 2)
            act.activation(l, u, ACT.Ln).then_inc(sp_a, 1)

        def gates_steps_dve(dve):
            dve.wait_ge(ba_ready, 1)
            dve.wait_ge(late_in, LATE)
            dve.tensor_tensor(gc(A_X), BA[:, :, 8:16], rows[:, 8:16].unsqueeze(1).to_broadcast([P, TT, AH]),
                              ALU.add).then_inc(g_dve, 1)
            dve.wait_ge(g_dve, 1)
            softplus_dve(dve, 0, gc(A_X), gc(A_ABS), gc(A_E), gc(A_U), gc(A_L), gc(A_G), 0, 0)
            dve.wait_ge(sp_d, 7)
            dve.wait_ge(g_act, 2)
            dve.scalar_tensor_tensor(gc(A_G), gc(A_G), -1.0, gcols[:, EXPA, 0:AH].unsqueeze(1).to_broadcast([P, TT, AH]),
                                     ALU.mult, ALU.mult).then_inc(g_dve, 1)

        def gates_sums_dve(dve):
            dve.wait_ge(g_pe, 1)
            dve.tensor_copy(gcols[:, GCUM, :], bank[7][:, 0:32]).then_inc(g_dve, 1)
            dve.tensor_copy(gcols[:, GEND, :], bank[7][:, 32:64]).then_inc(g_dve, 1)
            dve.wait_ge(g_dve, 4)
            dve.tensor_tensor(gcols[:, EDX, :], gcols[:, GEND, :], gcols[:, GCUM, :], ALU.subtract).then_inc(g_dve, 1)

        def gates_decay_dve(dve):
            dve.wait_ge(g_act, 5)
            dve.scalar_tensor_tensor(gcols[:, NBG, :], gcols[:, BETA, :], -1.0, gcols[:, EGC, :],
                                     ALU.mult, ALU.mult).then_inc(g_dve, 1)

        def gates_steps_act(act):
            act.wait_ge(ba_ready, 1)
            act.wait_ge(late_in, LATE)
            act.wait_ge(g_dve, 1)
            act.activation(gc(BETA), BA[:, :, 0:8], ACT.Sigmoid).then_inc(g_act, 1)
            act.activation(gcols[:, EXPA, 0:AH], rows[:, 0:8], ACT.Exp).then_inc(g_act, 1)
            softplus_act(act, gc(A_ABS), gc(A_E), gc(A_U), gc(A_L), 0)

        def gates_exp_act(act):
            act.wait_ge(g_dve, 5)
            act.activation(gcols[:, EGC, :], gcols[:, GCUM, :], ACT.Exp).then_inc(g_act, 1)
            act.activation(gcols[:, EDX, :], gcols[:, EDX, :], ACT.Exp).then_inc(g_act, 1)
            act.activation(gcols[:, DEC, :], gcols[:, GEND, :], ACT.Exp).then_inc(g_act, 1)

        def gates_pe(pe):
            pe.wait_ge(g_dve, 2)
            pe.wait_ge(late_in, LATE)
            pe.matmul(bank[7][:, 0:32], triu[:, :], gcols[:, A_G, :], start=True, stop=True)
            pe.matmul(bank[7][:, 32:64], ones[:, :], gcols[:, A_G, :], start=True, stop=True).then_inc(g_pe, 1)

        l_done = sem("l_done")
        h_root = at("h_root", 36, [32, T])
        h_rcp = at("h_rcp", 38, [32, T])

        def head_sums_pe(pe, count, base, sums, per_row=1, first=0, some=None):
            for j in range(first, first + some if some else count):
                row = j // per_row
                pe.wait_ge(hn_sq, base + j + 1)
                one = PAR["one_col"] + 31 - row
                pe.matmul(sums[0:32, :], par[:, one:one + 32], sq[:, j % 2, :], start=(j == 0), stop=(j == count - 1)).then_inc(hn_ss, 1)

        def head_root_act(act, sums, ss, scale, eps):
            act.wait_ge(hn_ss, ss)
            act.activation(h_root[:, :], sums[0:32, :], ACT.Sqrt, bias=eps, scale=scale).then_inc(hn_std, 1)

        def head_rcp_dve(dve, nth):
            dve.wait_ge(hn_std, nth)
            dve.reciprocal(h_rcp[:, :], h_root[:, :]).then_inc(hn_rcp, 1)

        def head_spread_pe(pe, count, nth, used, per=1):
            pe.wait_ge(hn_rcp, nth)
            for j in range(count):
                ge(pe, used, per * (j - 1))
                pe.matmul(bank[6 + j % 2][:, :], ident[0:32, j:j + 1].to_broadcast([32, P]), h_rcp[:, :],
                          start=True, stop=True).then_inc(hn_bc, 1)

        def unit_sums_pe(pe):
            head_sums_pe(pe, 16, 0, bank[4])

        def unit_spread_pe(pe):
            head_spread_pe(pe, 16, 1, l_done)

        def unit_act(act):
            head_root_act(act, bank[4], 16, pcol("unit_scale")[0:32], pcol("unit_eps")[0:32])

        def unit_squares_dve(dve, first, count):
            dve.wait_ge(silu_done, 16)
            for j in range(first, first + count):
                ge(dve, hn_ss, j - 1)
                dve.tensor_tensor(sq[:, j % 2, :], qkvz[:, j, :], qkvz[:, j, :], ALU.mult).then_inc(hn_sq, 1)

        def unit_dve(dve):
            head_rcp_dve(dve, 1)

            def body(j):
                for s in range(2):
                    dve.wait_ge(hn_bc, j + s + 1)
                    dve.tensor_tensor(qkv(j + s), qkv(j + s), bank[6 + s][:, :], ALU.mult).then_inc(l_done, 1)
            turns(dve, 16, 2, body)

        Uall = at("Uall", 0, [P, AH, TT, P])
        Aall = at("Aall", 16, [P, AH, TT, P])
        Kend = at("Kend", 104, [P, AH, TT, P])
        X1 = [at(f"X1_{s}", 32 + 2 * s, [P, TT, P]) for s in range(2)]
        X2 = [at(f"X2_{s}", 36 + 2 * s, [P, TT, P]) for s in range(2)]
        Rm = [at(f"Rm_{s}", 120 + 2 * s, [P, TT, P]) for s in range(2)]
        Vm = [at(f"Vm_{s}", 124 + 2 * s, [P, TT, P]) for s in range(2)]
        (da_gb, da_kk, da_qk, da_bb, da_dt, da_eg, da_ex, da_r1, da_a, da_r, da_qd, da_vt, da_rv, da_kt, da_kend,
         da_mask, da_tr, da_p1, da_p1c, da_tv, da_tu, da_v, da_u) = (sem("da_" + n) for n in (
             "gb kk qk bb dt eg ex r1 a r qd vt rv kt kend mask tr p1 p1c tv tu v u".split()))

        def c4(x):
            return x[:, :].rearrange("p (c i) -> p c i", c=TT)

        def bc4(x):
            return x.unsqueeze(1).to_broadcast([P, TT, P])

        def hd(buf, j):
            return buf[:, ds(j, 1), :, :]

        def inside_pe(pe):
            pe.wait_ge(g_dve, 6)
            pe.wait_ge(l_done, 16)
            pe.wait_ge(bank_free, 32)
            for i in range(AH // 2):
                for s in range(2):
                    j = 2 * i + s
                    ge(pe, da_u, 14 * i - 1 + s if i else 0)
                    ge(pe, da_kend, j - 1)
                    b = bank[4 * s:4 * s + 4]
                    for c in range(TT):
                        mm = pe.matmul(c4(b[0])[:, c, :], gc(A_G)[:, c, j:j + 1].to_broadcast([P, P]), triu[:, :],
                                       start=True, stop=True)
                    mm.then_inc(da_gb, 1)
                    for c in range(TT):
                        kc = qkvz[:, 8 + j, c * P:c * P + P]
                        mm = pe.matmul(c4(b[1])[:, c, :], kc, kc, start=True, stop=True)
                    mm.then_inc(da_kk, 1)
                    for c in range(TT):
                        mm = pe.matmul(c4(b[2])[:, c, :], qkvz[:, 8 + j, c * P:c * P + P], qkvz[:, j, c * P:c * P + P],
                                       start=True, stop=True)
                    mm.then_inc(da_qk, 1)
                    for c in range(TT):
                        mm = pe.matmul(c4(b[3])[:, c, :], gc(BETA)[:, c, j:j + 1].to_broadcast([P, P]), ident[:, :],
                                       start=True, stop=True)
                    mm.then_inc(da_bb, 1)
                for s in range(2):
                    j = 2 * i + s
                    pe.wait_ge(da_r1, j + 1)
                    for c in range(TT):
                        mm = pe.transpose(c4(bank[4 * s + 3])[:, c, :], qkvz[:, 16 + j, c * P:c * P + P], ident[:, :])
                    mm.then_inc(da_vt, 1)
                for s in range(2):
                    pe.wait_ge(da_mask, 14 * i + s + 1)
                    for c in range(TT):
                        mm = pe.transpose(c4(bank[4 * s + 1])[:, c, :], X2[s][:, c, :], ident[:, :])
                    mm.then_inc(da_tr, 1)
                for s in range(2):
                    j = 2 * i + s
                    pe.wait_ge(da_rv, j + 1)
                    for c in range(TT):
                        mm = pe.transpose(c4(bank[4 * s + 3])[:, c, :], qkvz[:, 8 + j, c * P:c * P + P], ident[:, :])
                    mm.then_inc(da_kt, 1)
                for l in range(1, 7):
                    for s in range(2):
                        pe.wait_ge(da_mask, 14 * i + 2 * l + s + 1)
                        pe.wait_ge(da_v, 12 * i + 2 * (l - 1) + s + 1)
                        if l > 1:
                            pe.wait_ge(da_p1c, 12 * i + 2 * (l - 2) + s + 1)
                        else:
                            pe.wait_ge(da_eg, 2 * i + s + 1)
                        for c in range(TT):
                            mm = pe.matmul(c4(bank[4 * s])[:, c, :], X2[s][:, c, :], Vm[s][:, c, :], start=True, stop=True)
                        mm.then_inc(da_p1, 1)
                    for s in range(2):
                        j = 2 * i + s
                        pe.wait_ge(da_p1c, 12 * i + 2 * (l - 1) + s + 1)
                        pe.wait_ge(da_u, 14 * i + 2 * (l - 1) + s + 1)
                        if l == 1:
                            pe.wait_ge(da_a, j + 1)
                        if l < 6:
                            for c in range(TT):
                                mm = pe.matmul(c4(bank[4 * s + 1])[:, c, :], Uall[:, j, c, :], X1[s][:, c, :],
                                               start=True, stop=True)
                            mm.then_inc(da_tv, 1)
                        for c in range(TT):
                            mm = pe.matmul(c4(bank[4 * s + 2])[:, c, :], X1[s][:, c, :], Uall[:, j, c, :],
                                           start=True, stop=True)
                        mm.then_inc(da_tu, 1)

        def inside_act(act):
            def body(j):
                for s in range(2):
                    act.wait_ge(da_dt, j + s + 1)
                    ge(act, da_mask, 7 * j - 1 + s if not isinstance(j, int) or j else 0)
                    ge(act, da_p1, 6 * j - 1 + s if not isinstance(j, int) or j else 0)
                    act.activation(X2[s][:, :, :], c4(bank[4 * s]), ACT.Exp).then_inc(da_eg, 1)
                    act.activation(X1[s][:, :, :], X1[s][:, :, :], ACT.Exp).then_inc(da_ex, 1)
                for l in range(1, 7):
                    for s in range(2):
                        act.wait_ge(da_p1, 6 * j + 2 * (l - 1) + s + 1)
                        if l == 1:
                            act.wait_ge(da_a, j + s + 1)
                        else:
                            act.wait_ge(da_tu, 6 * j + 2 * (l - 2) + s + 1)
                        act.activation(X1[s][:, :, :], c4(bank[4 * s]), ACT.Copy).then_inc(da_p1c, 1)
            turns(act, AH, 2, body, peel=True)

        def inside_pool(pool):
            pool.wait_ge(late_in, LATE)
            def body(j):
                for s in range(2):
                    pool.wait_ge(da_eg, j + s + 1)
                    pool.wait_ge(da_qk, j + s + 1)
                    pool.tensor_tensor(qkv(j + s), qkv(j + s), X2[s][:, :, :].rearrange("p c i -> p (c i)"),
                                       ALU.mult).then_inc(da_qd, 1)
                for l in range(7):
                    for s in range(2):
                        if l == 0:
                            pool.wait_ge(da_r, j + s + 1)
                            pool.wait_ge(da_qd, j + s + 1)
                        elif l == 1:
                            pool.wait_ge(da_tr, j + s + 1)
                            pool.wait_ge(da_u, 7 * j + s + 1)
                        else:
                            pool.wait_ge(da_p1, 6 * j + 2 * (l - 2) + s + 1)
                        pool.tensor_tensor(X2[s][:, :, :], Rm[s][:, :, :], bc4(lev[:, l, :]), ALU.mult).then_inc(da_mask, 1)
            turns(pool, AH, 2, body, peel=False)

        def inside_dve(dve):
            def body(j):
                first = isinstance(j, int) and j == 0
                for s in range(2):
                    dve.wait_ge(da_gb, j + s + 1)
                    if not first:
                        dve.wait_ge(da_tu, 6 * j - 1 + s)
                    for c in range(TT):
                        op = dve.scalar_tensor_tensor(X1[s][:, c, :], c4(bank[4 * s])[:, c, :], gc(GCUM)[:, c, ds(j + s, 1)],
                                                      upmask[:, :], ALU.subtract, ALU.add)
                    op.then_inc(da_dt, 1)
                for s in range(2):
                    dve.wait_ge(da_ex, j + s + 1)
                    dve.wait_ge(da_bb, j + s + 1)
                    if not first:
                        dve.wait_ge(da_mask, 7 * j - 1 + s)
                    dve.tensor_tensor(Rm[s][:, :, :], X1[s][:, :, :], c4(bank[4 * s + 3]), ALU.mult).then_inc(da_r1, 1)
                    dve.wait_ge(da_qk, j + s + 1)
                    dve.tensor_tensor(hd(Aall, j + s), c4(bank[4 * s + 2]), X1[s][:, :, :], ALU.mult).then_inc(da_a, 1)
                    dve.wait_ge(da_kk, j + s + 1)
                    dve.wait_ge(da_r1, j + s + 1)
                    dve.tensor_tensor(Rm[s][:, :, :], c4(bank[4 * s + 1]), Rm[s][:, :, :], ALU.mult).then_inc(da_r, 1)
                for s in range(2):
                    dve.wait_ge(da_vt, j + s + 1)
                    dve.tensor_tensor(qkv(j + s + 16).rearrange("p o (c i) -> p (o c) i", c=TT), c4(bank[4 * s + 3]),
                                      gc(BETA)[:, :, ds(j + s, 1)].to_broadcast([P, TT, P]), ALU.mult).then_inc(da_rv, 1)
                for s in range(2):
                    dve.wait_ge(da_mask, 7 * j + s + 1)
                    dve.tensor_tensor(hd(Uall, j + s), bc4(ident[:, :]), X2[s][:, :, :], ALU.subtract).then_inc(da_u, 1)
                    dve.wait_ge(da_tr, j + s + 1)
                    dve.tensor_tensor(Vm[s][:, :, :], bc4(ident[:, :]), c4(bank[4 * s + 1]), ALU.subtract).then_inc(da_v, 1)
                for s in range(2):
                    dve.wait_ge(da_kt, j + s + 1)
                    dve.tensor_tensor(hd(Kend, j + s), c4(bank[4 * s + 3]), gc(EDX)[:, :, ds(j + s, 1)].to_broadcast([P, TT, P]),
                                      ALU.mult).then_inc(da_kend, 1)
                for l in range(1, 7):
                    for s in range(2):
                        if l < 6:
                            dve.wait_ge(da_tv, 5 * j + 2 * (l - 1) + s + 1)
                            dve.wait_ge(da_v, 6 * j + 2 * (l - 1) + s + 1)
                            dve.tensor_tensor(Vm[s][:, :, :], Vm[s][:, :, :], c4(bank[4 * s + 1]), ALU.subtract).then_inc(da_v, 1)
                        dve.wait_ge(da_tu, 6 * j + 2 * (l - 1) + s + 1)
                        dve.wait_ge(da_u, 7 * j + 2 * (l - 1) + s + 1)
                        dve.tensor_tensor(hd(Uall, j + s), hd(Uall, j + s), c4(bank[4 * s + 2]), ALU.subtract).then_inc(da_u, 1)
            turns(dve, AH, 2, body, peel=True)

        Sst = at("Sst", 120, [P, AH, P])
        Vnew = [at(f"Vnew{g}", 124 + 2 * g, [P, 4, P]) for g in range(2)]
        b_s, b_p, b_r, b_vn, b_vc, b_o, b_oc, b_su = (sem("b_" + n) for n in "s p r vn vc o oc su".split())

        def across_pe(pe):
            pe.wait_ge(da_u, 56)
            pe.wait_ge(da_qd, 8)
            pe.wait_ge(da_kend, 8)
            for c in range(TT):
                tc = slice(c * P, c * P + P)
                for g in range(2):
                    m = 2 * c + g
                    pe.wait_ge(b_s, m + 1)
                    if c:
                        pe.wait_ge(b_r, 2 * c + g - 1)
                    for q in range(4):
                        mm = pe.matmul(c4(bank[4 * g])[:, q, :], qkvz[:, 8 + 4 * g + q, tc], Sst[:, 4 * g + q, :],
                                       start=True, stop=True)
                    mm.then_inc(b_p, 1)
                for g in range(2):
                    m = 2 * c + g
                    pe.wait_ge(b_r, m + 1)
                    for q in range(4):
                        j = 4 * g + q
                        mm = pe.matmul(c4(bank[4 * g + 1])[:, q, :], Uall[:, j, c, :], qkvz[:, 16 + j, tc],
                                       start=True, stop=True)
                    mm.then_inc(b_vn, 1)
                for g in range(2):
                    m = 2 * c + g
                    pe.wait_ge(b_vc, m + 1)
                    if c:
                        pe.wait_ge(b_oc, m - 1)
                    for q in range(4):
                        mm = pe.matmul(c4(bank[4 * g + 3])[:, q, :], Kend[:, 4 * g + q, c, :], Vnew[g][:, q, :],
                                       start=True, stop=True)
                    mm.then_inc(b_su, 1)
                    for q in range(4):
                        j = 4 * g + q
                        pe.matmul(c4(bank[4 * g + 2])[:, q, :], Vnew[g][:, q, :], Aall[:, j, c, :], start=True, stop=False)
                        mm = pe.matmul(c4(bank[4 * g + 2])[:, q, :], Sst[:, j, :], qkvz[:, j, tc], start=False, stop=True)
                    mm.then_inc(b_o, 1)

        def across_dve(dve):
            dve.wait_ge(da_u, 56)
            dve.wait_ge(da_tu, 48)
            for g in range(2):
                dve.memset(Sst[:, 4 * g:4 * g + 4, :], 0.0).then_inc(b_s, 1)
            for c in range(TT):
                tc = slice(c * P, c * P + P)
                for g in range(2):
                    m = 2 * c + g
                    dve.wait_ge(b_p, m + 1)
                    for q in range(4):
                        j = 4 * g + q
                        rv = qkvz[:, 16 + j, tc]
                        op = dve.scalar_tensor_tensor(rv, c4(bank[4 * g])[:, q, :], gc(NBG)[:, c, j:j + 1], rv,
                                                      ALU.mult, ALU.add)
                    op.then_inc(b_r, 1)
                for g in range(2):
                    m = 2 * c + g
                    dve.wait_ge(b_su, m + 1)
                    dve.wait_ge(b_o, m + 1)
                    dve.wait_ge(b_s, m + 1)
                    for q in range(4):
                        j = 4 * g + q
                        op = dve.scalar_tensor_tensor(Sst[:, j, :], Sst[:, j, :], gc(DEC)[:, c, j:j + 1],
                                                      c4(bank[4 * g + 3])[:, q, :], ALU.mult, ALU.add)
                    op.then_inc(b_s, 1)

        def across_act(act):
            act.wait_ge(da_u, 56)
            for c in range(TT):
                tc = slice(c * P, c * P + P)
                for g in range(2):
                    m = 2 * c + g
                    act.wait_ge(b_vn, m + 1)
                    ge(act, b_o, m - 1)
                    act.activation(Vnew[g][:, :, :], c4(bank[4 * g + 1]), ACT.Copy).then_inc(b_vc, 1)
                for g in range(2):
                    m = 2 * c + g
                    act.wait_ge(b_o, m + 1)
                    act.activation(qkvz[:, 16 + 4 * g:20 + 4 * g, tc], c4(bank[4 * g + 2]), ACT.Copy).then_inc(b_oc, 1)

        o_n, o_g = sem("o_n"), sem("o_g")

        def onorm_pe(pe):
            head_sums_pe(pe, AH, 16, bank[0])
            head_spread_pe(pe, AH, 2, o_n)

        def onorm_act(act):
            act.wait_ge(b_oc, 8)
            for j in range(AH):
                act.wait_ge(hn_ss, 15 + j)
                act.activation(sq[:, j % 2, :], qkvz[:, 16 + j, :], ACT.Square).then_inc(hn_sq, 1)
            head_root_act(act, bank[0], 24, 1.0 / P, eps_col[0:32, 0:1])
            for j in range(AH):
                act.wait_ge(o_g, j + 1)
                act.activation(x_hi[:, j, :], qkvz[:, 16 + j, :], ACT.Copy).then_inc(hn_hi, 1)

        def onorm_pool(pool):
            for j in range(AH):
                pool.wait_ge(o_n, j + 1)
                pool.tensor_tensor(qkvz[:, 16 + j, :], qkvz[:, 16 + j, :], qkvz[:, 24 + j, :], ALU.mult).then_inc(o_g, 1)

        def onorm_dve(dve):
            head_rcp_dve(dve, 2)
            for j in range(AH + 2):
                if j < AH:
                    dve.wait_ge(hn_bc, 16 + j + 1)
                    dve.scalar_tensor_tensor(qkvz[:, 16 + j, :], qkvz[:, 16 + j, :], pcol("a_out_norm"), bank[6 + j % 2][:, :],
                                             ALU.mult, ALU.mult).then_inc(o_n, 1)
                if j >= 2:
                    dve.wait_ge(hn_hi, j - 1)
                    dve.tensor_tensor(x_lo[:, j - 2, :], qkvz[:, 14 + j, :], x_hi[:, j - 2, :].bitcast(F32),
                                      ALU.subtract).then_inc(hn_lo, 1)

        def a_out_sp(sp):
            w = rows_k(t["a_w_out"][0])
            sp_slots(sp, SLOTS["a_out"], 4, lambda i, s: halves(w, s, i * 256))

        def a_out_pe(pe):
            projection(pe, "a_out", x_hi, x_lo, lambda k: (hn_lo, k + 1))

        def no_read(i, s):
            pass

        def add_h_slots(dve, base, c):
            squares_start(dve, c, SQ_B)

            def body(i):
                for s in range(2):
                    add_h(dve, base, i + s, s, c, SQ_B)
            turns(dve, 4, 2, body)

        act_hi = at("act_hi", 40, [P, 8, T], F32R)
        act_lo = at("act_lo", 56, [P, 8, T], F32R)
        y_gate = at("y_gate", 72, [P, 2, T])
        y_val = at("y_val", 76, [P, 2, T])
        ada_acc = at("ada_acc", 108, [P, 6, D])
        ada_w = [[at(f"ada_w{r}", at_kb, [P, D]) for r, at_kb in enumerate(lot)] for lot in ((80, 84, 88, 92), (96, 100, 104, 32))]
        (f_tap, f_g, f_v, f_silu, f_a, f_hi, f_lo, ada_in0, ada_in1, ada_used, mod_ready, mod_done) = (
            sem(n) for n in ("f_tap f_g f_v f_silu f_a f_hi f_lo ada_in0 ada_in1 ada_used "
                             "mod_ready mod_done").split())
        ada_in = [ada_in0, ada_in1]
        ADA_HALVES = (((0,), (1,), (2,), (3,)), ((4, 5), (6,), (7, 8), (9,)), ((10,), (11,), (), ()))

        def ada_piece(s, r):
            return ada_w[s][r][:, :]

        def ffn_sp(sp, f):
            up, dn = rows_k(t["f_w_up"][f]), rows_k(t["f_w_down"][f])
            for c in range(3):
                col = F_START[c] * P
                sp_slots(sp, SLOTS[f"f{f}_up{c}"], F_CHUNKS[c],
                         lambda i, s: both(up, s, i * P + col, i * P + (F_DIM + col)))
                sp_slots(sp, SLOTS[f"f{f}_dn{c}"], 4,
                         lambda i, s: halves(dn, s, i * 256, F_CHUNKS[c], F_START[c]))

        def ffn_pe(pe, f, lots):
            for c in range(3):
                if c == 0:
                    projection(pe, f"f{f}_up0", x_hi, x_lo, normed(lots))
                else:
                    turns(pe, F_CHUNKS[c], 2, slot_body(pe, SLOTS[f"f{f}_up{c}"], x_hi, x_lo))
                projection(pe, f"f{f}_dn{c}", act_hi, act_lo,
                           lambda k: (f_lo, 22 * f + F_START[c] + k + 1), F_CHUNKS[c])

        ada_rows = at("ada_rows", 106, [32, T])
        ada_sum, ada_row = sem("ada_sum"), sem("ada_row")

        def ada_sums_pe(pe, f, first, count):
            if first == 0:
                pe.wait_ge(ada_used, 48 * (f + 1))
            for r in range(first, first + count):
                one = PAR["one_col"] + 31 - r
                mm = pe.matmul(bank[5 + f][0:32, :], par[:, one:one + 32], ada_acc[:, r // 2, (r % 2) * T:(r % 2) * T + T],
                               start=(r == 0), stop=(r == 11))
            if first + count == 12:
                mm.then_inc(ada_sum, 1)

        def ada_rows_act(act, f):
            act.wait_ge(ada_sum, f + 1)
            act.activation(ada_rows[:, :], bank[5 + f][0:32, :], ACT.Copy).then_inc(ada_row, 1)

        def ada_turn_pe(pe, f):
            pe.wait_ge(ada_row, f + 1)
            for c in range(4):
                mm = pe.transpose(bank[5 + f][:, c * 32:c * 32 + 32], ada_rows[:, c * P:c * P + P], ident[0:32, 0:32])
            mm.then_inc(mod_ready, 1)

        def ffn_act(act, f, lots):
            w = t["ada_w"][f].rearrange("(k p) n -> p k n", p=P)

            def ada_load(s, pc):
                for r in range(4):
                    act.dma_start(ada_piece(s, r), w[:, 4 * s + r, ds(pc * D, D)]).then_inc(ada_in[s], 16)

            if f == 0:
                act.activation(cond[:, :], par[:, PAR["cond"]:PAR["cond"] + 8], ACT.Silu).then_inc(cond_in, 1)
            for c in range(3):
                base = SLOTS[f"f{f}_up{c}"]
                tile0 = 22 * f + F_START[c]

                def up(i, s):
                    n = base + i
                    act.wait_ge(gemm_ready, 2 * n + 1)
                    ge(act, f_lo, i + (tile0 - 1))
                    act.activation(y_gate[:, s, :], bank[2 * s][:, :], ACT.Identity, bias=pcol("f_conv_b", i + (44 * f + F_START[c])),
                                   scale=pcol("f_conv", i + (3 * 44 * f + 88 + F_START[c]))).then_inc(f_g, 1)
                    act.wait_ge(gemm_ready, 2 * n + 2)
                    act.activation(y_val[:, s, :], bank[2 * s + 1][:, :], ACT.Identity,
                                   bias=pcol("f_conv_b", i + (44 * f + 22 + F_START[c])),
                                   scale=pcol("f_conv", i + (3 * 44 * f + 88 + 22 + F_START[c]))).then_inc(f_v, 1)
                    act.wait_ge(bank_free, 2 * n + 1)
                    act.activation(y_gate[:, s, :], y_gate[:, s, :], ACT.Silu).then_inc(f_silu, 1)
                    act.wait_ge(f_a, i + (tile0 + 1))
                    act.activation(act_hi[:, ds(i, 1), :], y_gate[:, s, :], ACT.Copy).then_inc(f_hi, 1)
                act_slots(act, f"f{f}_up{c}", up, peel=(f == 0 and c == 0))

                if c == 0:
                    act.wait_ge(n_lo, KD * lots)
                    if f:
                        act.wait_ge(ada_used, 48 * f)
                    ada_load(0, 0)
                    ada_load(1, 0)
                for i in (0, 2):
                    for s in range(2):
                        n = SLOTS[f"f{f}_dn{c}"] + i + s
                        split_hi(act, n + 2, s, landed(n - s + 2))
                        for q in ADA_HALVES[c][i + s]:
                            if q + 2 < 12:
                                act.wait_ge(ada_used, 48 * f + 4 * q + 4)
                                ada_load(q % 2, q // 2 + 1)

        def ffn_dve(dve, f, c_norm):
            def ada_half(q):
                pc, s = q // 2, q % 2
                dve.wait_ge(ada_in[s], 64 * (6 * f + pc + 1))
                for r in range(4):
                    k = 4 * s + r
                    if k == 0:
                        if f and pc == 0:
                            dve.wait_ge(mod_ready, f)
                        dve.wait_ge(cond_in, 1)
                        dve.tensor_scalar(ada_acc[:, pc, :], ada_piece(s, r), cond[:, 0:1], None,
                                          ALU.mult).then_inc(ada_used, 1)
                    else:
                        dve.wait_ge(ada_used, 48 * f + 4 * q + r)
                        dve.scalar_tensor_tensor(ada_acc[:, pc, :], ada_piece(s, r), cond[:, k:k + 1], ada_acc[:, pc, :],
                                                 ALU.mult, ALU.add).then_inc(ada_used, 1)

            for c in range(3):
                base = SLOTS[f"f{f}_up{c}"]
                tile0 = 22 * f + F_START[c]

                def up(i):
                    for s in range(2):
                        j = i + (tile0 + s)
                        for o, y, first, col in ((0, y_gate, f_g, 0), (1, y_val, f_v, 22)):
                            dve.wait_ge(first, j + 1)
                            for d in (1, 2):
                                if d == 2:
                                    dve.wait_ge(f_tap, 2 * j + o + 1)
                                dve.scalar_tensor_tensor(
                                    y[:, s, d:T], bank[2 * s + o][:, 0:T - d],
                                    pcol("f_conv", i + (3 * 44 * f + 44 * (2 - d) + col + F_START[c] + s)), y[:, s, d:T],
                                    ALU.mult, ALU.add).then_inc(f_tap if d == 1 else bank_free, 1)
                        dve.wait_ge(f_silu, j + 1)
                        dve.wait_ge(bank_free, 2 * (base + i + s) + 2)
                        dve.tensor_tensor(y_gate[:, s, :], y_gate[:, s, :], y_val[:, s, :], ALU.mult).then_inc(f_a, 1)
                        dve.wait_ge(f_hi, j + 1)
                        dve.tensor_tensor(act_lo[:, ds(i + s, 1), :], y_gate[:, s, :],
                                          act_hi[:, ds(i + s, 1), :].bitcast(F32), ALU.subtract).then_inc(f_lo, 1)
                turns(dve, F_CHUNKS[c], 2, up, peel=(f == 0 and c == 0))
                base_dn = SLOTS[f"f{f}_dn{c}"]
                if c == 2:
                    squares_start(dve, c_norm, SQ_X)
                for i in (0, 2):
                    for s in range(2):
                        n = base_dn + i + s
                        for q in ADA_HALVES[c][i + s]:
                            ada_half(q)
                        add_h(dve, base_dn, i + s, s, c_norm if c == 2 else None, SQ_X)
            dve.wait_ge(ada_used, 48 * (f + 1))

        def ada_mod_dve(dve, f):
            dve.wait_ge(mod_ready, f + 1)
            dve.tensor_tensor(mod[:, f, :].rearrange("p (r c) -> p r c", c=4),
                              bank[5 + f][:, 0:P].rearrange("p (c r) -> p r c", r=32)[:, 0:12, :],
                              par[:, PAR["ada_b"] + 48 * f:PAR["ada_b"] + 48 * f + 48].rearrange("p (r c) -> p r c", c=4),
                              ALU.add).then_inc(mod_done, 1)
            dve.wait_ge(mod_done, 3 * f + 1)
            dve.scalar_tensor_tensor(gain[:, f, 0:8], mod[:, f, 8:16], 1.0, par[:, PAR["mix_g"] + 8 * f:PAR["mix_g"] + 8 * f + 8],
                                     ALU.add, ALU.mult).then_inc(mod_done, 1)
            dve.scalar_tensor_tensor(gain[:, f, 8:16], mod[:, f, 32:40], 1.0, par[:, PAR["mlp_g"] + 8 * f:PAR["mlp_g"] + 8 * f + 8],
                                     ALU.add, ALU.mult).then_inc(mod_done, 1)

        qT = at("qT", 40, [P, KD, T])
        kT = at("kT", 56, [P, KD, T])
        v_tok = at("v_tok", 72, [P, TT, D])
        strip = [at(f"strip{i}", 88 + 2 * i, [P, T]) for i in range(2)]
        prob = [at(f"prob{i}", at_kb, [P, T]) for i, at_kb in enumerate((92, 94, 102, 104))]
        sbank = [bank[i] for i in (0, 1, 6, 7)]
        probT = [at(f"probT{i}", 96 + 2 * i, [P, TT, P]) for i in range(2)]
        acol = at("acol", 100, [P, 3, 8])
        (at_strip0, at_strip1, at_mask, at_s, at_sb, at_m, at_e, at_rs, at_pn, at_t, at_tc, at_o, at_hi, at_lo) = (
            sem(n) for n in "at_strip0 at_strip1 at_mask at_s at_sb at_m at_e at_rs at_pn at_t at_tc at_o at_hi at_lo".split())

        def kvq_sp(sp):
            wkv, wq = rows_k(t["w_kv"]), rows_k(t["b_w_q"][0])
            sp_slots(sp, SLOTS["b_k"], 8, lambda i, s: halves(wkv, s, i * 256))
            sp_slots(sp, SLOTS["b_q"], 4, lambda i, s: halves(wq, s, i * 256))

        def strip_sp(sp):
            for j in range(BH):
                if j >= 2:
                    sp.wait_ge(at_sb, 4 * (j - 1))
                sp.dma_start(strip[j % 2][:, :], t["strips"][j]).then_inc((at_strip0, at_strip1)[j % 2], 16)

        def strip_pool(pool):
            for j in range(BH):
                pool.wait_ge((at_strip0, at_strip1)[j % 2], 16 * (j // 2) + 16)
                pool.memset(strip[j % 2][0:64, 448:512], NEG).then_inc(at_mask, 1)

        def v_pe(pe):
            def body(i):
                for s in range(2):
                    pe_slot_start(pe, SLOTS["b_v"] + i + s)
                    for o in range(2):
                        for c in (2 * o, 2 * o + 1):
                            tc = slice(c * P, c * P + P)
                            for k in range(KD):
                                wc = slice(k * 256, k * 256 + 256)
                                mm = three(pe, bank[2 * s + o][:, (c % 2) * 256:(c % 2) * 256 + 256], x_hi[:, k, tc], x_lo[:, k, tc],
                                           w_hi[s][:, wc], w_lo[s][:, wc], k == 0, k == KD - 1)
                        mm.then_inc(gemm_ready, 1)
            turns(pe, 4, 2, body)

        def kvq_pe(pe, lots):
            projection(pe, "b_k", x_hi, x_lo, normed(lots))
            v_pe(pe)
            projection(pe, "b_q", x_hi, x_lo, normed(lots + 1))

        def kv_act(act):
            def k_out(i, s):
                for o in range(2):
                    act.wait_ge(gemm_ready, 2 * (SLOTS["b_k"] + i) + o + 1)
                    act.activation(kT[:, ds(2 * i + o, 1), :], bank[2 * s + o][:, :], ACT.Copy).then_inc(bank_free, 1)

            def v_out(i, s):
                for o in range(2):
                    act.wait_ge(gemm_ready, 2 * (SLOTS["b_v"] + i) + o + 1)
                    act.activation(v_tok[:, 2 * o:2 * o + 2, ds(i * 256, 256)],
                                   bank[2 * s + o][:, :].rearrange("p (c n) -> p c n", c=2), ACT.Copy).then_inc(bank_free, 1)
            act_slots(act, "b_k", k_out)
            act_slots(act, "b_v", v_out)

        def q_act(act):
            def q_out(i, s):
                for o in range(2):
                    act.wait_ge(gemm_ready, 2 * (SLOTS["b_q"] + i) + o + 1)
                    act.activation(qT[:, ds(2 * i + o, 1), :], bank[2 * s + o][:, :], ACT.Copy,
                                   scale=-float(BD) ** -0.5).then_inc(bank_free, 1)
            act_slots(act, "b_q", q_out)

        def attn_pe(pe):
            pe.wait_ge(bank_free, 2 * SLOTS["b_out"])
            units = 4 * BH

            def scores(u):
                j, it = u // 4, u % 4
                r = slice(64 * (j % 2), 64 * (j % 2) + 64)
                n = P * (it + 1)
                ge(pe, at_sb, u - 3)
                pe.matmul(sbank[u % 4][:, 0:n], qT[r, j // 2, it * P:it * P + P], kT[r, j // 2, 0:n],
                          start=True, stop=True).then_inc(at_s, 1)

            def turn(u):
                it = u % 4
                pe.wait_ge(at_pn, u + 1)
                ge(pe, at_tc, u - 1)
                for c in range(it + 1):
                    mm = pe.transpose(bank[2 + u % 2][:, c * P:c * P + P], prob[u % 4][:, c * P:c * P + P], ident[:, :])
                mm.then_inc(at_t, 1)

            def values(u):
                j, it = u // 4, u % 4
                r = slice(64 * (j % 2), 64 * (j % 2) + 64)
                pe.wait_ge(at_tc, u + 1)
                if u == 8:
                    pe.wait_ge(mod_done, 1)
                if u % 8 == 0:
                    ge(pe, at_lo, j // 2 - 1)
                for c in range(it + 1):
                    mm = pe.matmul(bank[4 + (j // 2) % 2][r, it * P:it * P + P], v_tok[:, c, j * BD:j * BD + BD],
                                   probT[u % 2][:, c, :], start=(c == 0), stop=(c == it))
                mm.then_inc(at_o, 1)
            for u in range(units + 4):
                if u < units:
                    scores(u)
                if u < 6:
                    ada_sums_pe(pe, 0, 2 * u, 2)
                if u == 7:
                    ada_turn_pe(pe, 0)
                if 3 <= u < units + 3:
                    turn(u - 3)
                if u >= 4:
                    values(u - 4)

        def attn_act(act):
            def tcopy(u, k):
                n = P * (k % 4 + 1)
                act.wait_ge(at_t, u + 1)
                ge(act, at_o, u - 1)
                act.activation(probT[k % 2][:, :, :].rearrange("p c i -> p (c i)")[:, 0:n], bank[2 + k % 2][:, 0:n],
                               ACT.Copy).then_inc(at_tc, 1)

            def body(m):
                for k in range(16):
                    u = 8 * m + k
                    n = P * (k % 4 + 1)
                    act.wait_ge(at_m, u + 1)
                    act.activation(prob[k % 4][:, 0:n], prob[k % 4][:, 0:n], ACT.Exp, bias=acol[:, 0, k % 8:k % 8 + 1], scale=-1.0,
                                   accum_out=acol[:, 1, k % 8:k % 8 + 1]).then_inc(at_e, 1)
                    if k >= 2 or not isinstance(m, int):
                        tcopy(u - 2, (k - 2) % 16)
                    if k == 5 and isinstance(m, int):
                        ada_rows_act(act, 0)
                    if k in (4, 12) and not (k == 4 and isinstance(m, int)):
                        pair = m + (k == 12) - 1
                        act.wait_ge(at_o, 8 * pair + 8)
                        act.activation(x_hi[:, ds(pair, 1), :], bank[4 + (k == 4)][:, :], ACT.Copy).then_inc(at_hi, 1)
            turns(act, KD, 2, body, peel=True)
            tcopy(62, 14)
            tcopy(63, 15)
            act.wait_ge(at_o, 64)
            act.activation(x_hi[:, 7, :], bank[5][:, :], ACT.Copy).then_inc(at_hi, 1)

        def attn_dve(dve):
            def reciprocal(u, k):
                dve.wait_ge(at_e, u + 1)
                dve.reciprocal(acol[:, 2, k % 8:k % 8 + 1], acol[:, 1, k % 8:k % 8 + 1]).then_inc(at_rs, 1)

            def normalize(u, k):
                n = P * (k % 4 + 1)
                dve.wait_ge(at_rs, u + 1)
                dve.tensor_scalar(prob[k % 4][:, 0:n], prob[k % 4][:, 0:n], acol[:, 2, k % 8:k % 8 + 1], None,
                                  ALU.mult).then_inc(at_pn, 1)

            def low(pair, b):
                dve.wait_ge(at_hi, pair + 1)
                dve.tensor_tensor(x_lo[:, ds(pair, 1), :], bank[4 + b][:, :], x_hi[:, ds(pair, 1), :].bitcast(F32),
                                  ALU.subtract).then_inc(at_lo, 1)

            def body(m):
                for k in range(16):
                    u = 8 * m + k
                    n = P * (k % 4 + 1)
                    dve.wait_ge(at_s, u + 1)
                    ge(dve, at_mask, 2 * m + k // 4 + 1)
                    if k >= 4 or not isinstance(m, int):
                        dve.wait_ge(at_t, u - 3)
                    dve.tensor_tensor(prob[k % 4][:, 0:n], sbank[k % 4][:, 0:n], strip[(k // 4) % 2][:, T - n:T],
                                      ALU.subtract).then_inc(at_sb, 1)
                    if k >= 2 or not isinstance(m, int):
                        normalize(u - 2, (k - 2) % 16)
                    dve.wait_ge(at_sb, u + 1)
                    dve.tensor_reduce(acol[:, 0, k % 8:k % 8 + 1], prob[k % 4][:, 0:n], AX.X, ALU.min).then_inc(at_m, 1)
                    if k or not isinstance(m, int):
                        reciprocal(u - 1, (k - 1) % 16)
                    if k == 8 and isinstance(m, int):
                        ada_mod_dve(dve, 0)
                    if k in (6, 14) and not (k == 6 and isinstance(m, int)):
                        low(m + (k == 14) - 1, 1 if k == 6 else 0)
            turns(dve, KD, 2, body, peel=True)
            normalize(62, 14)
            reciprocal(63, 15)
            normalize(63, 15)
            low(7, 1)

        def b_out_sp(sp):
            w = rows_k(t["b_w_out"][0])
            sp_slots(sp, SLOTS["b_out"], 4, lambda i, s: halves(w, s, i * 256))

        def b_out_pe(pe):
            projection(pe, "b_out", x_hi, x_lo, lambda k: (at_lo, k + 1))

        mid_done = sem("mid_done")

        def mid_dve(dve, c, c_next):
            norm_root(dve, c)
            squares_start(dve, c_next, SQ_B)
            for k in range(KD):
                dve.scalar_tensor_tensor(h[:, k, :], h[:, k, :], pcol("final_norm", k), RSTD, ALU.mult, ALU.mult).then_inc(mid_done, 1)
                if k:
                    square(dve, c_next, k - 1, (k - 1) % 2, SQ_B, mid_done, k)
            square(dve, c_next, KD - 1, 1, SQ_B, mid_done, KD)

        uT = at("uT", 40, [P, KD, T])
        ct = at("ct", 56, [P, S5N, P])
        st = at("st", 72, [P, S5N, P])
        bt = at("bt", 88, [P, 2, S5Q, P])
        cw = at("cw", 96, [P, 2, S5N, 32])
        ck = at("ck", 104, [P, 3, S5N, 32])
        rt = [at(f"rt{i}", at_kb, [P, 4, P]) for i, at_kb in enumerate((116, 126))]
        gin = [at(f"gin{i}", at_kb, [P, 2, T]) for i, at_kb in enumerate((118, 24))]
        gs = [at(f"gs{i}", at_kb, [P, 2, T]) for i, at_kb in enumerate((122, 28))]
        s_t = [[at(f"s_t{u}{i}", (32, 16)[u] + 2 * i, [P, T]) for i in range(4)] for u in range(2)]
        ubank = [bank[0:2], bank[4:6]]
        pr = at("pr", 96, [P, 4, T])
        scol = at("scol", 133.0625, [P, 16, S5N])
        carry = at("carry", 128, [P, 6, 4])
        um = [at(f"um{i}", 129 + 2 * i, [P, T]) for i in range(2)]
        s_um = sem("s_um")
        dbl = at("dbl", 118, [P, S5N, 64])
        (DT, RA, TH, RR, CO, SI, KR_, KI_, T0, T1, T2, T3, C64, S64, CN, SN) = range(16)
        (s_in, s_dve, s_act, s_bu, s_mul, s_re, s_im, s_gin, s_rc, s_scan, s_pr, s_pp, s_y, s_car, s_out, s_gelu,
         s_lo, s_rt) = (sem("s_" + n) for n in
                        "in dve act bu mul re im gin rc scan pr pp y car out gelu lo rt".split())

        def s_load_sp(sp):
            sp.wait_ge(gemm_ready, 2 * SLOTS["s_in"])
            sp.wait_ge(mod_done, 6)
            sp.dma_start(bt[:, :, :, :], t["s5_bt"]).then_inc(s_in, 16)
            sp.dma_start(cw[:, :, :, :], t["s5_ct"]).then_inc(s_in, 16)

        def s_in_sp(sp):
            w = rows_k(t["s5_w_in"][0])
            sp_slots(sp, SLOTS["s_in"], 4, lambda i, s: halves(w, s, i * 256))

        def s_in_pe(pe, lots):
            projection(pe, "s_in", x_hi, x_lo, normed(lots))

        def s_in_act(act):
            def u_out(i, s):
                for o in range(2):
                    act.wait_ge(gemm_ready, 2 * (SLOTS["s_in"] + i) + o + 1)
                    act.activation(uT[:, ds(2 * i + o, 1), :], bank[2 * s + o][:, :], ACT.Copy).then_inc(bank_free, 1)
            act_slots(act, "s_in", u_out)

        def sc(n):
            return scol[:, n, :]

        def s_par_act(act):
            act.wait_ge(g_dve, 6)
            act.activation(sc(DT), par[:, PAR["log_dt"]:PAR["log_dt"] + 32], ACT.Exp).then_inc(s_act, 1)
            act.wait_ge(s_dve, 1)
            act.activation(sc(RR), sc(RA), ACT.Exp).then_inc(s_act, 1)
            act.wait_ge(s_dve, 12)
            act.activation(sc(SI), sc(T0), ACT.Sin).then_inc(s_act, 1)
            act.activation(sc(CO), sc(T1), ACT.Sin).then_inc(s_act, 1)

        S_SCALARS = 12 + 15 + 2
        s_kap, s_rs = sem("s_kap"), sem("s_rs")
        s_kap_steps = [0]
        s_steps = [0]

        def s_step(dve, op):
            s_steps[0] += 1
            op.then_inc(s_dve, 1)
            dve.wait_ge(s_dve, s_steps[0])

        def s_par_dve(dve):
            def step(op):
                s_step(dve, op)
            lr, li = (par[:, PAR[n]:PAR[n] + 32] for n in ("lam_re", "lam_im"))
            two_pi = [6.28125, 0.0019350051879882812, 3.019916050561517e-07]
            magic = 1.5 * 2.0 ** 23
            dve.wait_ge(s_act, 1)
            step(dve.tensor_tensor(sc(RA), lr, sc(DT), ALU.mult))
            step(dve.tensor_tensor(sc(TH), li, sc(DT), ALU.mult))
            step(dve.tensor_scalar(sc(T0), sc(TH), 1.0 / (2.0 * np.pi), None, ALU.mult))
            step(dve.tensor_scalar(sc(T1), sc(T0), magic, None, ALU.add))
            step(dve.tensor_scalar(sc(T1), sc(T1), magic, None, ALU.subtract))
            step(dve.scalar_tensor_tensor(sc(T0), sc(T1), -two_pi[0], sc(TH), ALU.mult, ALU.add))
            step(dve.scalar_tensor_tensor(sc(T0), sc(T1), -two_pi[1], sc(T0), ALU.mult, ALU.add))
            step(dve.scalar_tensor_tensor(sc(T0), sc(T1), -two_pi[2], sc(T0), ALU.mult, ALU.add))
            step(dve.tensor_scalar(sc(T0), sc(T0), 3.1415925, -3.1415925, ALU.min, ALU.max))
            step(dve.scalar_tensor_tensor(sc(T1), sc(T0), -1.0, sc(T0), ALU.mult, ALU.min))
            step(dve.tensor_scalar(sc(T1), sc(T1), float(np.pi / 2), None, ALU.add))
            step(dve.memset(sc(T2), 0.0))
            dve.wait_ge(s_act, 4)
            step(dve.tensor_tensor(sc(T0), sc(RR), sc(CO), ALU.mult))
            step(dve.tensor_scalar(sc(T0), sc(T0), -1.0, None, ALU.add))
            step(dve.tensor_tensor(sc(T1), sc(RR), sc(SI), ALU.mult))
            step(dve.tensor_tensor(sc(T2), lr, lr, ALU.mult))
            step(dve.tensor_tensor(sc(T3), li, li, ALU.mult))
            step(dve.tensor_tensor(sc(T2), sc(T2), sc(T3), ALU.add))
            step(dve.reciprocal(sc(T2), sc(T2)))
            step(dve.tensor_tensor(sc(KR_), sc(T0), lr, ALU.mult))
            step(dve.tensor_tensor(sc(T3), sc(T1), li, ALU.mult))
            step(dve.tensor_tensor(sc(KR_), sc(KR_), sc(T3), ALU.add))
            step(dve.tensor_tensor(sc(KR_), sc(KR_), sc(T2), ALU.mult))
            step(dve.tensor_tensor(sc(KI_), sc(T1), lr, ALU.mult))
            step(dve.tensor_tensor(sc(T3), sc(T0), li, ALU.mult))
            step(dve.tensor_tensor(sc(KI_), sc(KI_), sc(T3), ALU.subtract))
            step(dve.tensor_tensor(sc(KI_), sc(KI_), sc(T2), ALU.mult))
            step(dve.tensor_scalar(sc(RA), sc(KR_), -1.0, None, ALU.mult))
            step(dve.tensor_scalar(sc(TH), sc(KI_), -1.0, None, ALU.mult))

        def s_kappa_pool(pool):
            def step(op):
                s_kap_steps[0] += 1
                op.then_inc(s_kap, 1)
                pool.wait_ge(s_kap, s_kap_steps[0])
            pool.wait_ge(s_dve, S_SCALARS)
            pool.wait_ge(s_in, 32)
            kr, ki, nkr, nki = (sc(n).unsqueeze(2).to_broadcast([P, S5N, 32]) for n in (KR_, KI_, RA, TH))
            step(pool.tensor_tensor(ck[:, 0], cw[:, 0], kr, ALU.mult))
            step(pool.tensor_tensor(ck[:, 2], cw[:, 1], ki, ALU.mult))
            step(pool.tensor_tensor(ck[:, 1], ck[:, 2], ck[:, 0], ALU.subtract))
            step(pool.tensor_tensor(ck[:, 0], ck[:, 0], ck[:, 2], ALU.subtract))
            step(pool.tensor_tensor(cw[:, 0], cw[:, 0], nki, ALU.mult))
            step(pool.tensor_tensor(cw[:, 1], cw[:, 1], nkr, ALU.mult))
            step(pool.tensor_tensor(ck[:, 2], cw[:, 0], cw[:, 1], ALU.add))
            for i in range(2):
                pool.memset(rt[i][:, :, 0:1], 0.0).then_inc(s_rs, 1)

        def s_tables_dve(dve):
            def step(op):
                s_step(dve, op)
            dve.wait_ge(gemm_ready, 2 * SLOTS["s_in"])
            step(dve.memset(ct[:, :, 0:1], 1.0))
            step(dve.memset(st[:, :, 0:1], 0.0))
            step(dve.tensor_copy(sc(C64), sc(CO)))
            step(dve.tensor_copy(sc(S64), sc(SI)))
            m = 1
            while m <= 64:
                cm, sm = (sc(n).unsqueeze(2).to_broadcast([P, S5N, m]) for n in (C64, S64))
                lo, up = slice(0, m), slice(m, 2 * m)
                tmp = dbl[:, :, 0:m]
                step(dve.tensor_tensor(ct[:, :, up], ct[:, :, lo], cm, ALU.mult))
                step(dve.tensor_tensor(tmp, st[:, :, lo], sm, ALU.mult))
                step(dve.tensor_tensor(ct[:, :, up], ct[:, :, up], tmp, ALU.subtract))
                step(dve.tensor_tensor(st[:, :, up], st[:, :, lo], cm, ALU.mult))
                step(dve.tensor_tensor(tmp, ct[:, :, lo], sm, ALU.mult))
                step(dve.tensor_tensor(st[:, :, up], st[:, :, up], tmp, ALU.add))
                step(dve.tensor_tensor(sc(T0), sc(C64), sc(C64), ALU.mult))
                step(dve.tensor_tensor(sc(T1), sc(S64), sc(S64), ALU.mult))
                step(dve.scalar_tensor_tensor(sc(S64), sc(S64), 2.0, sc(C64), ALU.mult, ALU.mult))
                step(dve.tensor_tensor(sc(C64), sc(T0), sc(T1), ALU.subtract))
                m *= 2
            step(dve.tensor_tensor(sc(CN), sc(RR), sc(C64), ALU.mult))
            step(dve.tensor_tensor(sc(SN), sc(RR), sc(S64), ALU.mult))

        def s5_pe(pe):
            pe.wait_ge(bank_free, 2 * SLOTS["s_glu"])
            pe.wait_ge(s_in, 32)

            def inputs(m):
                q, c = m // 4, m % 4
                ge(pe, s_mul, 4 * m - 4)
                pe.wait_ge(s_um, m + 1)
                for x in range(2):
                    mm = pe.matmul(ubank[m % 2][x][:, :], bt[:, x, q, :], um[m % 2][:, :], start=True, stop=True)
                mm.then_inc(s_bu, 1)

            def outputs(m):
                q, c = m // 4, m % 4
                pe.wait_ge(s_pr, 2 * m + 2)
                pe.wait_ge(s_pp, 2 * m + 2)
                if c == 0:
                    ge(pe, s_out, q - 1)
                for k in range(4):
                    r = slice(32 * k, 32 * k + 32)
                    for x, part in ((0, 0), (1, 1), (2, 2), (2, 3)):
                        mm = pe.matmul(bank[2 + q % 2][r, c * P:c * P + P], ck[:, x, 4 * q + k, :], pr[:, part, k * P:k * P + P],
                                       start=(part == 0), stop=(part == 3))
                mm.then_inc(s_y, 1)
            for m in range(36):
                if m < 32:
                    inputs(m)
                if m == 4:
                    pe.wait_ge(s_kap, 7)
                if m >= 4:
                    outputs(m - 4)

        def s5_dve(dve):
            def v4(x):
                return x.rearrange("p (k i) -> p k i", k=4)

            def inputs(q, c, m):
                def tab(x):
                    return x[:, ds(q * 4, 4), :]
                re, im = (v4(b[:, :]) for b in ubank[c % 2])
                s_to = s_t[c % 2]
                dve.wait_ge(s_bu, m + 1)
                if not isinstance(m, int) or m >= 2:
                    dve.wait_ge(s_im, m - 1)
                dve.tensor_tensor(v4(s_to[0][:, :]), re, tab(ct), ALU.mult).then_inc(s_mul, 1)
                dve.tensor_tensor(v4(s_to[1][:, :]), im, tab(st), ALU.mult).then_inc(s_mul, 1)
                dve.tensor_tensor(v4(s_to[2][:, :]), im, tab(ct), ALU.mult).then_inc(s_mul, 1)
                dve.tensor_tensor(v4(s_to[3][:, :]), re, tab(st), ALU.mult).then_inc(s_mul, 1)

            def yq(q, par_q):
                dve.wait_ge(s_y, q * 4 + 4)
                uq = uT[:, ds(q, 1), :]
                dve.scalar_tensor_tensor(uq, uq, pcol("s5_d", q), bank[2 + par_q][:, :], ALU.mult, ALU.add).then_inc(s_out, 1)

            def products(q, c, m, x):
                tab = (ct, st)[x][:, ds(q * 4, 4), :]
                if x == 0 and not (isinstance(m, int) and m == 0):
                    dve.wait_ge(s_y, m)
                dve.tensor_tensor(v4(pr[:, x, :]), v4(gs[c % 2][:, x, :]), tab, ALU.mult).then_inc(s_pr, 1)

            def quad(q, par_q, last=False):
                first = isinstance(q, int) and q == 0

                def chunk(c):
                    m = q * 4 + c
                    scan_in, scan_out = gin[c % 2], gs[c % 2]
                    for x, done in ((0, s_re), (1, s_im)):
                        g0 = v4(scan_in[:, x, :])[:, :, 0]
                        dve.wait_ge(done, m + 1)
                        if c:
                            dve.wait_ge(s_car, q * 6 + 2 * c)
                            dve.tensor_tensor(g0, g0, carry[:, 4 + x, :], ALU.add).then_inc(s_gin, 1)
                            dve.wait_ge(s_gin, q * 6 + (2 * c - 1 + x))
                        if x == 0:
                            dve.wait_ge(s_rt, q + 1)
                        if not first or c >= 2:
                            dve.wait_ge(s_pp, m * 2 - 2)
                            dve.wait_ge(s_pr, m * 2 - 2)
                        dve.tensor_tensor_scan(scan_out[:, x, :], rt[par_q][:, :, :].rearrange("p k i -> p (k i)"), scan_in[:, x, :],
                                               0.0, ALU.mult, ALU.add).then_inc(s_scan, 1)
                    if c < 2:
                        inputs(q, c + 2, m + 2)
                    elif not last:
                        inputs(q + 1, c - 2, m + 2)
                    if c < 3:
                        dve.wait_ge(s_scan, m * 2 + 2)
                        er, ei = (v4(scan_out[:, x, :])[:, :, P - 1] for x in range(2))
                        cn, sn = (scol[:, n, ds(q * 4, 4)] for n in (CN, SN))
                        dve.tensor_tensor(carry[:, 0, :], er, cn, ALU.mult)
                        dve.tensor_tensor(carry[:, 1, :], ei, sn, ALU.mult)
                        dve.tensor_tensor(carry[:, 2, :], er, sn, ALU.mult)
                        dve.tensor_tensor(carry[:, 3, :], ei, cn, ALU.mult).then_inc(s_rc, 1)
                    prev = (q, c - 1, m - 1) if c else (q - 1, 3, m - 1)
                    if not first or c:
                        for x in range(2):
                            products(*prev, x)
                    if c == 1 and not first:
                        yq(q - 1, 1 - par_q)

                for c in range(4):
                    chunk(c)
            dve.wait_ge(s_rs, 2)
            inputs(0, 0, 0)
            inputs(0, 1, 1)
            dve.wait_ge(s_kap, 7)
            quad(0, 0)
            with dve.Fori(1, S5Q - 2, 2) as q:
                quad(q, 1)
                quad(q + 1, 0)
            quad(S5Q - 1, 1, last=True)
            for x in range(2):
                products(S5Q - 1, 3, 31, x)
            yq(S5Q - 1, 1)

        def s5_pool(pool):
            def v4(x):
                return x.rearrange("p (k i) -> p k i", k=4)

            def inputs(m):
                s_to, scan_in = s_t[m % 2], gin[m % 2]
                pool.wait_ge(s_mul, 4 * m + 2)
                ge(pool, s_scan, 2 * m - 2)
                pool.tensor_tensor(scan_in[:, 0, :], s_to[0][:, :], s_to[1][:, :], ALU.add).then_inc(s_re, 1)
                pool.wait_ge(s_mul, 4 * m + 4)
                pool.tensor_tensor(scan_in[:, 1, :], s_to[2][:, :], s_to[3][:, :], ALU.subtract).then_inc(s_im, 1)

            def products(m):
                q = m // 4
                ctab, stab = ct[:, 4 * q:4 * q + 4, :], st[:, 4 * q:4 * q + 4, :]
                pool.wait_ge(s_scan, 2 * m + 2)
                ge(pool, s_y, m)
                pool.tensor_tensor(v4(pr[:, 2, :]), v4(gs[m % 2][:, 0, :]), stab, ALU.mult).then_inc(s_pp, 1)
                pool.tensor_tensor(v4(pr[:, 3, :]), v4(gs[m % 2][:, 1, :]), ctab, ALU.mult).then_inc(s_pp, 1)

            inputs(0)
            inputs(1)
            for m in range(4 * S5Q):
                if m:
                    products(m - 1)
                if m % 4 < 3:
                    pool.wait_ge(s_rc, 3 * (m // 4) + m % 4 + 1)
                    pool.tensor_tensor(carry[:, 4, :], carry[:, 0, :], carry[:, 1, :], ALU.subtract).then_inc(s_car, 1)
                    pool.tensor_tensor(carry[:, 5, :], carry[:, 2, :], carry[:, 3, :], ALU.add).then_inc(s_car, 1)
                if m + 2 < 4 * S5Q:
                    inputs(m + 2)
            products(4 * S5Q - 1)

        def s5_act(act):
            def spread(q, c):
                m = q * 4 + c
                if not isinstance(m, int) or m >= 2:
                    act.wait_ge(s_bu, m - 1)
                for k in range(4):
                    op = act.activation(um[c % 2][:, k * P:k * P + P], uT[:, ds(q, 1), c * P:c * P + P], ACT.Copy,
                                        scale=par[:, PAR["qmask"] + k:PAR["qmask"] + k + 1])
                op.then_inc(s_um, 1)

            def decay(q, par_q):
                if not isinstance(q, int) or q >= 2:
                    act.wait_ge(s_scan, q * 8 - 8)
                act.activation(rt[par_q][:, :, 1:P], scol[:, RR, ds(q * 4, 4)].unsqueeze(2).to_broadcast([P, 4, P - 1]),
                               ACT.Copy).then_inc(s_rt, 1)

            def gelu(q):
                act.wait_ge(s_out, q + 1)
                act.activation(uT[:, ds(q, 1), :], uT[:, ds(q, 1), :], ACT.Gelu_apprx_tanh).then_inc(s_gelu, 1)
                act.wait_ge(s_gelu, q * 2 + 1)
                act.activation(x_hi[:, ds(q, 1), :], uT[:, ds(q, 1), :], ACT.Copy).then_inc(s_gelu, 1)

            def quad(q, par_q, first=False, last=False):
                decay(q, par_q)
                spread(q, 2)
                spread(q, 3)
                if not last:
                    spread(q + 1, 0)
                    spread(q + 1, 1)
                if not first:
                    gelu(q - 1)
            act.wait_ge(bank_free, 2 * SLOTS["s_glu"])
            act.wait_ge(s_dve, S_SCALARS)
            spread(0, 0)
            spread(0, 1)
            quad(0, 0, first=True)
            with act.Fori(1, S5Q - 2, 2) as q:
                quad(q, 1)
                quad(q + 1, 0)
            quad(S5Q - 1, 1, last=True)
            gelu(S5Q - 1)

        def s_gelu_dve(dve):
            def body(q):
                dve.wait_ge(s_gelu, 2 * q + 2)
                dve.tensor_tensor(x_lo[:, ds(q, 1), :], uT[:, ds(q, 1), :], x_hi[:, ds(q, 1), :].bitcast(F32),
                                  ALU.subtract).then_inc(s_lo, 1)
            turns(dve, S5Q, 1, body)

        glu = at("glu", 56, [P, 4, T])
        g_sig, g_h = sem("g_sig"), sem("g_h")

        def glu_sp(sp):
            w = rows_k(t["s5_w_glu"][0])
            sp_slots(sp, SLOTS["s_glu"], 8, lambda i, s: both(w, s, i * P, i * P + D))

        def glu_pe(pe):
            projection(pe, "s_glu", x_hi, x_lo, lambda k: (s_lo, k + 1))

        def glu_act(act):
            def gate(i, s):
                act.wait_ge(gemm_ready, 2 * (SLOTS["s_glu"] + i) + 2)
                if not (isinstance(i, int) and i < 2):
                    act.wait_ge(bank_free, 2 * (SLOTS["s_glu"] + i) - 2)
                act.activation(glu[:, s, :], bank[2 * s + 1][:, :], ACT.Sigmoid, bias=pcol("s5_b_glu", i + 8)).then_inc(g_sig, 1)
            act_slots(act, "s_glu", gate, peel=True)

        def glu_dve(dve, c):
            squares_start(dve, c, SQ_B)

            def body(i):
                for s in range(2):
                    dve.wait_ge(g_sig, i + s + 1)
                    dve.scalar_tensor_tensor(glu[:, 2 + s, :], bank[2 * s][:, :], pcol("s5_b_glu", i + s), glu[:, s, :],
                                             ALU.add, ALU.mult).then_inc(bank_free, 2)
                    dve.wait_ge(bank_free, 2 * (SLOTS["s_glu"] + i + s) + 2)
                    hk = h[:, ds(i + s, 1), :]
                    dve.scalar_tensor_tensor(hk, glu[:, 2 + s, :], modc(0, 16 + i + s), hk, ALU.mult, ALU.add).then_inc(g_h, 1)
                    square(dve, c, i + s, s, SQ_B, g_h, i + s + 1)
            turns(dve, 8, 2, body)

        def modc(f, i):
            return mod[:, f, ds(i, 1)]

        def gainc(f, i):
            return gain[:, f, i:i + 1]

        m_hi = at("m_hi", 40, [P, 8, T], F32R)
        m_lo = at("m_lo", 56, [P, 8, T], F32R)
        m_r = at("m_r", 72, [P, 2, T])
        p_r, p_hi, p_lo = (sem("p_" + n) for n in ("r", "hi", "lo"))
        PASS = 8

        def mlp_sp(sp, f):
            w1 = rows_k(t["mlp_w1"][f])
            w2 = rows_k(t["mlp_w2"][f])
            base = SLOTS[f"p{f}"]

            def one(c):
                sp_slots(sp, c * PASS + base, 4, lambda i, s: halves(w1, s, c * 1024 + i * 256))
                sp_slots(sp, c * PASS + (base + 4), 4, lambda i, s: halves(w2, s, i * 256, KD, c * KD))
            turns(sp, 4, 1, one)

        def mlp_pe(pe, f, lots):
            base = SLOTS[f"p{f}"]
            for c in range(4):
                if c == 0:
                    projection(pe, None, x_hi, x_lo, normed(lots), count=4, base=base)
                else:
                    turns(pe, 4, 2, slot_body(pe, c * PASS + base, x_hi, x_lo))
                projection(pe, None, m_hi, m_lo, lambda k: (p_lo, 32 * f + 8 * c + k + 1), count=4,
                           base=c * PASS + base + 4)

        def mlp_act(act, f):
            base = SLOTS[f"p{f}"]

            def one(c, end=False):
                def up(i, s):
                    n = c * PASS + base + i
                    for o in range(2):
                        j = c * 8 + 2 * i + (32 * f + o)
                        act.wait_ge(gemm_ready, 2 * n + o + 1)
                        if not (isinstance(j, int) and j < 2):
                            act.wait_ge(p_lo, j - 1)
                        act.activation(m_r[:, o, :], bank[2 * s + o][:, :], ACT.Relu).then_inc(p_r, 1)
                        act.wait_ge(bank_free, 2 * n + o + 1)
                        act.activation(m_hi[:, ds(2 * i + o, 1), :], m_r[:, o, :], ACT.Copy).then_inc(p_hi, 1)
                act_slots(act, None, up, 0, 4, base=c * PASS + base, peel=(f == 0 and isinstance(c, int)))
                act_slots(act, None, no_read, 0, 4, base=c * PASS + (base + 4))
            if f == 0:
                turns(act, 4, 1, one, peel=True)
            else:
                turns(act, 3, 1, one)
                one(3)

        def mlp_dve(dve, f, c_norm):
            base = SLOTS[f"p{f}"]

            def one(c, last=False):
                if last:
                    squares_start(dve, c_norm, SQ_B)

                def up(i):
                    for s in range(2):
                        n = c * PASS + base + i + s
                        for o in range(2):
                            j = c * 8 + 2 * i + (32 * f + 2 * s + o)
                            dve.wait_ge(p_r, j + 1)
                            dve.scalar_tensor_tensor(m_r[:, o, :], bank[2 * s + o][:, :], 0.0, m_r[:, o, :],
                                                     ALU.max, ALU.mult).then_inc(bank_free, 1)
                            dve.wait_ge(p_hi, j + 1)
                            lo = m_lo[:, ds(2 * i + (2 * s + o), 1), :]
                            dve.tensor_tensor(lo, m_r[:, o, :], m_hi[:, ds(2 * i + (2 * s + o), 1), :].bitcast(F32),
                                              ALU.subtract).then_inc(p_lo, 1)
                turns(dve, 4, 2, up)

                def down(i):
                    for s in range(2):
                        n = c * PASS + (base + 4) + i + s
                        for o in range(2):
                            k = 2 * i + (2 * s + o)
                            dve.wait_ge(gemm_ready, 2 * n + o + 1)
                            hk = h[:, ds(k, 1), :]
                            dve.scalar_tensor_tensor(hk, bank[2 * s + o][:, :], modc(f, 40 + k), hk, ALU.mult, ALU.add).then_inc(bank_free, 1)
                            if last:
                                square(dve, c_norm, k, o, SQ_B, bank_free, 2 * n + o + 1)
                turns(dve, 4, 2, down)
            turns(dve, 3, 1, one)
            one(3, last=True)
        zT = at("zT", 40, [P, M_TILES, T])
        xbc = at("xbc", 72, [P, XBC_TILES, T])
        (m_dt, m_silu, wdt_in) = (sem("m_" + n) for n in "dt silu wdt".split())
        mcols = at("mcols", 128, [P, 10, TT * M_H])
        (M_X, M_ABS, M_E, M_U, M_L, M_DT, M_ADT, M_CS, M_EDX, M_DEC) = range(10)
        DTP = bank[6][:, 0:TT * M_H].rearrange("p (c n) -> p c n", n=M_H)

        def mc(n):
            return mcols[:, n, :].rearrange("p (c h) -> p c h", h=M_H)

        def m_in_sp(sp):
            w = t["m2_w_in"][0]
            sp.wait_ge(gemm_ready, 2 * SLOTS["p0"])
            sp.dma_start(nar_raw[:, :, :], rows_k(w)[:, :, 5120:5152]).then_inc(wdt_in, 16)
            sp_slots(sp, SLOTS["m_in"], 20, lambda i, s: halves(rows_k(w), s, i * 256))

        def m_in_pe(pe, lots):
            base = SLOTS["m_in"]
            first_turn(pe, base, x_hi, x_lo, normed(lots))
            narrow_pe(pe, 2)
            body = slot_body(pe, base, x_hi, x_lo)
            body(2)
            narrow_turn_pe(pe, 2, DTP, M_H, m_dt)
            body(4)
            steps_pe(pe)
            turns(pe, 20, 2, body, start=6)

        def xb(j, a=0, b=T):
            return xbc[:, ds(j, 1), a:b]

        def m_in_act(act):
            base = SLOTS["m_in"]

            def silu(j):
                for o in range(2):
                    act.activation(xb(j + o), xb(j + o), ACT.Silu).then_inc(m_silu, 1)

            def gate(i, s):
                for o in range(2):
                    act.wait_ge(gemm_ready, 2 * (base + i) + o + 1)
                    act.activation(zT[:, ds(2 * i + o, 1), :], bank[2 * s + o][:, :], ACT.Silu).then_inc(bank_free, 1)

            def conv(i, s):
                for o in range(2):
                    j = 2 * i + (o - M_TILES)
                    act.wait_ge(gemm_ready, 2 * (base + i) + o + 1)
                    act.activation(xb(j), bank[2 * s + o][:, :], ACT.Identity, bias=pcol("m_conv_b", j),
                                   scale=pcol("m_conv", j + 3 * 24)).then_inc(tap_first, 1)
                if not (isinstance(i, int) and i == 8):
                    act.wait_ge(bank_free, 2 * (base + i))
                    silu(2 * i - (M_TILES + 2))
            act.wait_ge(wdt_in, 16)
            narrow_hi_act(act)
            act_slots(act, "m_in", gate, 0, 2, peel=True)
            narrow_out_act(act, 2)
            act_slots(act, "m_in", gate, 2, 2)
            steps_act(act)
            act_slots(act, "m_in", gate, 4, 2)
            steps_exp_act(act)
            act_slots(act, "m_in", gate, 6, 2)
            act_slots(act, "m_in", lambda i, s: conv(i, s), 8, 2)
            act_slots(act, "m_in", conv, 10, 10)
            act.wait_ge(bank_free, 2 * (base + 20))
            silu(22)

        def m_in_dve(dve):
            narrow_lo_dve(dve, 2)
            steps_dve(dve)

            def body(i):
                for s in range(2):
                    for o in range(2):
                        j = 2 * (i + s) + o
                        dve.wait_ge(tap_first, 24 + j + 1)
                        for d in (1, 2, 3):
                            if d > 1:
                                dve.wait_ge(tap_mid, 48 + 2 * j + d - 1)
                            dve.scalar_tensor_tensor(xb(j, d), bank[2 * s + o][:, 0:T - d], pcol("m_conv", j + (3 - d) * 24),
                                                     xb(j, d), ALU.mult, ALU.add).then_inc(tap_mid if d < 3 else bank_free, 1)
            turns(dve, 12, 2, body)

        d_pe, d_act, d_dve = sem("steps_pe"), sem("steps_act"), sem("steps_dve")

        def bch(row):
            return row.unsqueeze(1).to_broadcast([P, TT, M_H])

        def steps_dve(dve):
            dve.wait_ge(m_dt, 1)
            dve.tensor_tensor(mc(M_X), DTP, bch(rows[:, 48:80]), ALU.add).then_inc(d_dve, 1)
            dve.wait_ge(d_dve, 1)
            softplus_dve(dve, 0, mc(M_X), mc(M_ABS), mc(M_E), mc(M_U), mc(M_L), mc(M_DT), 7, 2)
            dve.wait_ge(sp_d, 14)
            dve.wait_ge(d_act, 1)
            dve.scalar_tensor_tensor(mc(M_ADT), mc(M_DT), -1.0, bch(mcols[:, M_EDX, 0:M_H]), ALU.mult, ALU.mult).then_inc(d_dve, 1)
            dve.wait_ge(d_pe, 1)
            dve.tensor_copy(mcols[:, M_CS, :], bank[7][:, 0:128]).then_inc(d_dve, 1)
            dve.tensor_copy(mcols[:, M_DEC, :], bank[7][:, 128:256]).then_inc(d_dve, 1)
            dve.wait_ge(d_dve, 4)
            dve.tensor_tensor(mcols[:, M_EDX, :], mcols[:, M_DEC, :], mcols[:, M_CS, :], ALU.subtract).then_inc(d_dve, 1)

        def steps_act(act):
            act.wait_ge(m_dt, 1)
            act.activation(mcols[:, M_EDX, 0:M_H], rows[:, 16:48], ACT.Exp).then_inc(d_act, 1)
            softplus_act(act, mc(M_ABS), mc(M_E), mc(M_U), mc(M_L), 7)

        def steps_exp_act(act):
            act.wait_ge(d_dve, 5)
            act.activation(mcols[:, M_EDX, :], mcols[:, M_EDX, :], ACT.Exp).then_inc(d_act, 1)
            act.activation(mcols[:, M_DEC, :], mcols[:, M_DEC, :], ACT.Exp).then_inc(d_act, 1)

        def steps_pe(pe):
            pe.wait_ge(d_dve, 2)
            pe.matmul(bank[7][:, 0:128], triu[:, :], mcols[:, M_ADT, :], start=True, stop=True)
            pe.matmul(bank[7][:, 128:256], ones[:, :], mcols[:, M_ADT, :], start=True, stop=True).then_inc(d_pe, 1)

        xdt = [at(f"xdt{i}", 2 * i, [P, T]) for i in range(2)]
        xdec = [at(f"xdec{i}", 4 + 2 * i, [P, T]) for i in range(2)]
        b_tok = [at(f"b_tok{i}", 8 + 0.5 * i, [P, P]) for i in range(2)]
        egb = [at(f"egb{i}", 10 + 2 * i, [P, 4, P]) for i in range(2)]
        lw = [[at(f"lw{i}{j}", 14 + 4 * i + 2 * j, [P, 4, P]) for j in range(2)] for i in range(2)]
        cdec = [[at(f"cdec{i}{j}", 22 + 4 * i + 2 * j, [P, 4, P]) for j in range(2)] for i in range(2)]
        cbank = [bank[1], bank[7]]
        prev = at("prev", 120, [P, M_H, M_P])
        (m_xt, m_cb, m_gb, m_xd, m_dl, m_le, m_eg, m_w, m_bt, m_xe, m_cd, m_st, m_y, m_y1, m_yz, m_pd, m_pv) = (
            sem("m_" + n) for n in "xt cb gb xd dl le eg w bt xe cd st y y1 yz pd pv".split())

        def v8(x):
            return x.rearrange("p (h n) -> p h n", n=M_P)

        def ssd_pe(pe):
            pe.wait_ge(m_silu, XBC_TILES)
            pe.wait_ge(d_dve, 5)

            def pre(w):
                c, g = w // 4, w % 4
                tc = slice(c * P, c * P + P)
                ge(pe, m_xd, w)
                for k in range(4):
                    mm = pe.transpose(bank[0][:, k * P:k * P + P], xbc[:, 4 * g + k, tc], ident[:, :])
                mm.then_inc(m_xt, 1)
                ge(pe, m_w, 2 * w - 2)
                ge(pe, m_bt, w - 1)
                pe.transpose(cbank[g % 2][:, 0:P], xbc[:, 16 + g, tc], ident[:, :])
                pe.matmul(cbank[g % 2][:, P:2 * P], xbc[:, 16 + g, tc], xbc[:, 20 + g, tc], start=True, stop=True).then_inc(m_cb, 1)
                for f in range(2):
                    ge(pe, m_dl, 2 * w - 1 + f if w else 0)
                    ge(pe, m_eg, 2 * w - 1 + f if w else 0)
                    for k in range(4):
                        j = 8 * g + 4 * f + k
                        mm = pe.matmul(c4(bank[2 + f])[:, k, :], mc(M_ADT)[:, c, j:j + 1].to_broadcast([P, P]), triu[:, :],
                                       start=True, stop=True)
                    mm.then_inc(m_gb, 1)

            def main(w):
                c, g = w // 4, w % 4
                for f in range(2):
                    pe.wait_ge(m_w, 2 * w + f + 1)
                    pe.wait_ge(m_cd, 2 * w + f + 1)
                    ge(pe, m_y1, w)
                    for k in range(4):
                        j = 4 * f + k
                        dst = bank[4 + f][64 * (k % 2):64 * (k % 2) + 64, (k // 2) * P:(k // 2) * P + P]
                        pe.matmul(dst, xdt[g % 2][:, j * M_P:j * M_P + M_P], lw[g % 2][f][:, k, :], start=True, stop=False)
                        mm = pe.matmul(dst, prev[:, 8 * g + j, :], cdec[g % 2][f][:, k, :], start=False, stop=True)
                    mm.then_inc(m_y, 1)
                pe.wait_ge(m_bt, w + 1)
                pe.wait_ge(m_xe, w + 1)
                ge(pe, m_pv, w)
                pe.matmul(bank[6][:, :], b_tok[g % 2][:, :], xdec[g % 2][:, :], start=True, stop=True).then_inc(m_st, 1)
            pe.wait_ge(m_pv0, 1)
            pre(0)
            for w in range(16):
                if w < 15:
                    pre(w + 1)
                main(w)
                if w == 14:
                    pe.wait_ge(m_xd, 16)
                    gnorm_sums_pe(pe, 0, 1)

        m_pv0 = sem("m_pv0")

        def ssd_act(act):
            def chunk(c):
                first = isinstance(c, int)
                for g in range(4):
                    w = c * 4 + g
                    act.wait_ge(m_cb, w + 1)
                    if not first or g >= 2:
                        act.wait_ge(m_st, w - 1)
                    act.activation(b_tok[g % 2][:, :], cbank[g % 2][:, 0:P], ACT.Copy).then_inc(m_bt, 1)
                    for f in range(2):
                        act.wait_ge(m_dl, 2 * w + f + 1)
                        if not first or g:
                            act.wait_ge(m_cd, 2 * w - 1 + f)
                        act.activation(egb[f][:, :, :], c4(bank[2 + f]), ACT.Exp).then_inc(m_eg, 1)
                        act.activation(lw[g % 2][f][:, :, :], lw[g % 2][f][:, :, :], ACT.Exp).then_inc(m_le, 1)
            turns(act, TT, 1, chunk, peel=True)

        def ssd_pool(pool):
            pool.wait_ge(d_act, 3)

            def decay(c, g, w):
                pool.wait_ge(m_y, 2 * w + 2)
                ps = prev[:, 8 * g:8 * g + 8, :]
                pool.tensor_tensor(ps, ps, mcols[:, M_DEC, ds(c * M_H + 8 * g, 8)].unsqueeze(2).to_broadcast([P, 8, M_P]),
                                   ALU.mult).then_inc(m_pd, 1)

            def gate(c, g, w):
                pool.wait_ge(m_y1, w + 1)
                ys = xbc[:, 4 * g:4 * g + 4, ds(c * P, P)]
                pool.tensor_tensor(ys, ys, zT[:, 4 * g:4 * g + 4, ds(c * P, P)], ALU.mult).then_inc(m_yz, 1)

            def chunk(c):
                first = c == 0
                for g in range(4):
                    w = c * 4 + g
                    last = (c, g - 1, w - 1) if g else None if first else (c - 1, 3, w - 1)
                    if last:
                        decay(*last)
                    for f in range(2):
                        pool.wait_ge(m_eg, 2 * w + f + 1)
                        if not first or g >= 2:
                            pool.wait_ge(m_y, 2 * w - 3 + f)
                        pool.tensor_tensor(cdec[g % 2][f][:, :, :], bc4(xbc[:, 20 + g, ds(c * P, P)]), egb[f][:, :, :],
                                           ALU.mult).then_inc(m_cd, 1)
                    pool.wait_ge(m_xd, w + 1)
                    if not first or g >= 2:
                        pool.wait_ge(m_st, w - 1)
                    pool.tensor_tensor(v8(xdec[g % 2][:, :]), v8(xdt[g % 2][:, :]),
                                       mcols[:, M_EDX, ds(c * M_H + 8 * g, 8)].unsqueeze(2).to_broadcast([P, 8, M_P]),
                                       ALU.mult).then_inc(m_xe, 1)
                    if last:
                        gate(*last)
            for c in range(TT):
                chunk(c)
            decay(3, 3, 15)
            gate(3, 3, 15)

        def ssd_dve(dve):
            dve.memset(prev[:, :, :], 0.0).then_inc(m_pv0, 1)
            dve.wait_ge(d_act, 3)

            def outputs(c, g, w):
                dve.wait_ge(m_y, 2 * w + 2)
                for k in range(4):
                    ys = xbc[:, 4 * g + k, ds(c * P, P)]
                    op = dve.scalar_tensor_tensor(ys, ys, pcol("m_d", 4 * g + k), bank[4 + k // 2][:, (k % 2) * P:(k % 2) * P + P],
                                                  ALU.mult, ALU.add)
                op.then_inc(m_y1, 1)

            def states(c, g, w):
                dve.wait_ge(m_st, w + 1)
                dve.wait_ge(m_pd, w + 1)
                ps = prev[:, 8 * g:8 * g + 8, :]
                dve.tensor_tensor(ps, ps, v8(bank[6][:, :]), ALU.add).then_inc(m_pv, 1)

            def chunk(c):
                first = isinstance(c, int)
                for g in range(4):
                    w = c * 4 + g
                    dve.wait_ge(m_xt, w + 1)
                    if not first or g >= 2:
                        dve.wait_ge(m_y, 2 * w - 2)
                        dve.wait_ge(m_xe, w - 1)
                    dve.tensor_tensor(v8(xdt[g % 2][:, :]), v8(bank[0][:, :]),
                                      mcols[:, M_DT, ds(c * M_H + 8 * g, 8)].unsqueeze(2).to_broadcast([P, 8, M_P]),
                                      ALU.mult).then_inc(m_xd, 1)
                    for f in range(2):
                        dve.wait_ge(m_gb, 2 * w + f + 1)
                        for k in range(4):
                            op = dve.scalar_tensor_tensor(lw[g % 2][f][:, k, :], c4(bank[2 + f])[:, k, :],
                                                          mcols[:, M_CS, ds(c * M_H + (8 * g + 4 * f + k), 1)], upmask[:, :],
                                                          ALU.subtract, ALU.add)
                        op.then_inc(m_dl, 1)
                    last = (c, g - 1, w - 1) if g else (c - 1, 3, w - 1)
                    if g or not first:
                        outputs(*last)
                    for f in range(2):
                        dve.wait_ge(m_le, 2 * w + f + 1)
                        dve.wait_ge(m_cb, w + 1)
                        dve.tensor_tensor(lw[g % 2][f][:, :, :], lw[g % 2][f][:, :, :], bc4(cbank[g % 2][:, P:2 * P]),
                                          ALU.mult).then_inc(m_w, 1)
                    if g or not first:
                        states(*last)
            turns(dve, TT, 1, chunk, peel=True)
            outputs(3, 3, 15)
            states(3, 3, 15)

        y_hi = at("y_hi", 0, [P, M_TILES, T], F32R)
        y_lo = at("y_lo", 40, [P, M_TILES, T], F32R)
        y_n = sem("y_n")

        def gnorm_sums_pe(pe, first, some):
            head_sums_pe(pe, M_TILES, 24, bank[0], 4, 4 * first, 4 * some)

        def gnorm_pe(pe):
            gnorm_sums_pe(pe, 1, 3)
            head_spread_pe(pe, M_G, 3, y_n, 4)

        def gnorm_act(act):
            def squares_of(g):
                act.wait_ge(m_yz, 13 + g)
                for j in range(4 * g, 4 * g + 4):
                    act.wait_ge(hn_ss, 24 + j - 1)
                    act.activation(sq[:, j % 2, :], xbc[:, j, :], ACT.Square).then_inc(hn_sq, 1)

            for g in range(M_G):
                squares_of(g)
            head_root_act(act, bank[0], 40, 1.0 / 512, eps_col[0:32, 1:2])
            for j in range(M_TILES):
                act.wait_ge(y_n, j + 1)
                act.activation(y_hi[:, j, :], xbc[:, j, :], ACT.Copy).then_inc(hn_hi, 1)

        def gnorm_dve(dve):
            head_rcp_dve(dve, 3)
            for j in range(M_TILES):
                g = j // 4
                dve.wait_ge(hn_bc, 24 + g + 1)
                dve.scalar_tensor_tensor(xbc[:, j, :], xbc[:, j, :], pcol("m_norm_g", j), bank[6 + g % 2][:, :],
                                         ALU.mult, ALU.mult).then_inc(y_n, 1)

        def gnorm_pool(pool):
            for j in range(M_TILES):
                pool.wait_ge(hn_hi, 8 + j + 1)
                pool.tensor_tensor(y_lo[:, j, :], xbc[:, j, :], y_hi[:, j, :].bitcast(F32), ALU.subtract).then_inc(hn_lo, 1)

        def m_out_sp(sp):
            w = rows_k(t["m2_w_out"][0])
            sp_slots(sp, SLOTS["m_out"], 8, lambda i, s: halves(w, s, (i - s) * P, KD, KD * s))

        def m_out_pe(pe):
            base = SLOTS["m_out"]

            def body(i, first=False):
                for s4 in range(4):
                    n, s, pair = base + i + s4, s4 % 2, s4 // 2
                    pe.wait_ge(lo_done, n + 1)
                    if s == 0:
                        pe.wait_ge(bank_free, 2 * n - 4)
                    for o, k in ([(o, k) for k in range(KD) for o in range(2)] if first and s4 < 2 else
                                 [(o, k) for o in range(2) for k in range(KD)]):
                        if first and s4 < 2 and o == 0:
                            pe.wait_ge(hn_lo, AH + KD * s + k + 1)
                        c = slice(k * 256 + o * P, k * 256 + o * P + P)
                        mm = three(pe, bank[2 * pair + o][:, :], w_hi[s][:, c], w_lo[s][:, c],
                                   y_hi[:, KD * s + k, :], y_lo[:, KD * s + k, :], s == 0 and k == 0, s == 1 and k == KD - 1)
                        if k == KD - 1:
                            mm.then_inc(gemm_ready, 1)
            body(0, first=True)
            body(4)

        def m_out_dve(dve, c):
            base = SLOTS["m_out"]
            squares_start(dve, c, SQ_B)

            def body(i):
                for pair in range(2):
                    for o in range(2):
                        dve.wait_ge(gemm_ready, 2 * (base + i + 2 * pair + 1) + o + 1)
                        hk = h[:, ds(i + (2 * pair + o), 1), :]
                        dve.scalar_tensor_tensor(hk, bank[2 * pair + o][:, :], modc(1, 16 + i + (2 * pair + o)), hk,
                                                 ALU.mult, ALU.add).then_inc(bank_free, 2)
                        square(dve, c, i + (2 * pair + o), o, SQ_B, bank_free, i * 2 + 2 * (base + 2 * pair + o + 1))
            turns(dve, 8, 4, body)

        o_tok = at("o_tok", 40, [P, TT, D])

        hg = at("hg", 0, [P, KD, T])
        end_bank = [bank[i] for i in (6, 7, 5, 0, 1, 2, 3, 6)]
        by_act = (1, 4, 7)
        out_act = sem("out_act")

        def end_pe(pe, c, lots):
            def turn(k):
                pe.wait_ge(n_xt, KD * lots + k + 1)
                if k == 3:
                    pe.wait_ge(bank_free, 2 * TOTAL)
                if k == KD - 1:
                    pe.wait_ge(h_in, KD + 1)
                for b in range(TT):
                    mm = pe.transpose(end_bank[k][:, b * P:b * P + P], hg[:, k, b * P:b * P + P], ident[:, :])
                mm.then_inc(x_t, 1)
            for k in range(KD - 2):
                turn(k)
            norm_sums_pe(pe, c, SQ_B)
            turn(KD - 2)
            turn(KD - 1)

        def end_scale_act(act):
            for k in range(KD):
                act.wait_ge(bank_free, 2 * TOTAL - KD + k + 1)
                act.activation(hg[:, k, :], h[:, k, :], ACT.Copy, scale=pcol("final_g", k)).then_inc(n_xt, 1)

        def end_act(act, c):
            act.wait_ge(n_rcp, c + 1)
            for k in by_act:
                act.wait_ge(x_t, KD + k + 1)
                for b in range(TT):
                    op = act.activation(o_tok[:, b, k * P:k * P + P], end_bank[k][:, b * P:b * P + P], ACT.Copy, scale=ncol[:, 2, b:b + 1])
                op.then_inc(out_act, 1)

        def end_dve(dve, c):
            dve.wait_ge(n_std, c + 1)
            dve.reciprocal(ncol[:, 2, :], ncol[:, 1, :]).then_inc(n_rcp, 1)
            dve.wait_ge(n_rcp, c + 1)
            for k in range(KD):
                if k not in by_act:
                    dve.wait_ge(x_t, KD + k + 1)
                    dve.tensor_tensor(o_tok[:, :, k * P:k * P + P], c4(end_bank[k]), ncol[:, 2, :].unsqueeze(2).to_broadcast([P, TT, P]),
                                      ALU.mult).then_inc(h_in, 1)

        def end_sp(sp):
            dst = out.rearrange("b (c p) d -> p (b c) d", p=P)
            for e in range(2):
                by_a = sum(k < 4 * e + 4 for k in by_act)
                sp.wait_ge(h_in, KD + 4 * e + 4 - by_a)
                sp.wait_ge(out_act, by_a)
                sp.dma_start(dst[:, :, e * 512:e * 512 + 512], o_tok[:, :, e * 512:e * 512 + 512]).then_inc(stored, 16)
            sp.wait_ge(stored, 32)

        block = ctx.enter_context(nc.Block())

        @block.sync
        def _(sp):
            load_sp(sp)
            a_in_sp(sp)
            a_out_sp(sp)
            ffn_sp(sp, 0)
            kvq_sp(sp)
            b_out_sp(sp)
            strip_sp(sp)
            ffn_sp(sp, 1)
            s_in_sp(sp)
            s_load_sp(sp)
            glu_sp(sp)
            mlp_sp(sp, 0)
            m_in_sp(sp)
            m_out_sp(sp)
            mlp_sp(sp, 1)
            end_sp(sp)

        @block.gpsimd
        def _(pool):
            done = [0]

            def upto(name, more=2):
                n = min(SLOTS[name] + more, TOTAL)
                pool_slots(pool, done[0], n - done[0])
                done[0] = n
            upto("a_out")
            inside_pool(pool)
            onorm_pool(pool)
            upto("b_out")
            strip_pool(pool)
            upto("s_glu", 0)
            s_kappa_pool(pool)
            upto("s_glu")
            s5_pool(pool)
            upto("m_out")
            ssd_pool(pool)
            gnorm_pool(pool)
            pool_slots(pool, done[0], TOTAL - done[0])

        @block.scalar
        def _(act):
            load_act(act)
            a_in_act(act)
            inside_act(act)
            across_act(act)
            onorm_act(act)
            act_slots(act, "a_out", no_read)
            norm_act(act, 1, 0, 1, slot=SLOTS["f0_up0"])
            ffn_act(act, 0, 2)
            norm_act(act, 2, 0, 2, slot=SLOTS["b_k"])
            s_par_act(act)
            kv_act(act)
            norm_hi(act, 3, SLOTS["b_q"])
            q_act(act)
            attn_act(act)
            act_slots(act, "b_out", no_read)
            norm_act(act, 3, 0, 4, slot=SLOTS["f1_up0"])
            ffn_act(act, 1, 5)
            norm_act(act, 4, 0, split=False)
            ada_rows_act(act, 1)
            norm_act(act, 5, 1, 5, shift=lambda k: mod[:, 0, k:k + 1], slot=SLOTS["s_in"])
            s_in_act(act)
            s5_act(act)
            glu_act(act)
            norm_act(act, 6, 1, 6, shift=lambda k: mod[:, 0, 24 + k:25 + k], slot=SLOTS["p0"])
            mlp_act(act, 0)
            norm_act(act, 7, 1, 7, shift=lambda k: mod[:, 1, k:k + 1], slot=SLOTS["m_in"])
            m_in_act(act)
            ssd_act(act)
            gnorm_act(act)
            act_slots(act, "m_out", no_read)
            norm_act(act, 8, 1, 8, shift=lambda k: mod[:, 1, 24 + k:25 + k], slot=SLOTS["p1"])
            mlp_act(act, 1)
            end_scale_act(act)
            norm_act(act, 9, 1, split=False)
            end_act(act, 9)

        @block.tensor
        def _(pe):
            pe.wait_ge(ones_set, 4)
            load_pe(pe)
            norm_spread_pe(pe, 0)
            a_in_pe(pe)
            inside_pe(pe)
            across_pe(pe)
            onorm_pe(pe)
            a_out_pe(pe)
            norm_pe(pe, 1, SQ_B)
            ffn_pe(pe, 0, 1)
            norm_pe(pe, 2, SQ_X)
            kvq_pe(pe, 2)
            attn_pe(pe)
            b_out_pe(pe)
            norm_pe(pe, 3, SQ_B)
            ffn_pe(pe, 1, 4)
            norm_pe(pe, 4, SQ_X)
            ada_sums_pe(pe, 1, 0, 12)
            ada_turn_pe(pe, 1)
            norm_pe(pe, 5, SQ_B)
            s_in_pe(pe, 5)
            s5_pe(pe)
            glu_pe(pe)
            norm_pe(pe, 6, SQ_B)
            mlp_pe(pe, 0, 6)
            norm_pe(pe, 7, SQ_B)
            m_in_pe(pe, 7)
            ssd_pe(pe)
            gnorm_pe(pe)
            m_out_pe(pe)
            norm_pe(pe, 8, SQ_B)
            mlp_pe(pe, 1, 8)
            end_pe(pe, 9, 9)

        @block.vector
        def _(dve):
            load_dve(dve)
            norm_dve(dve, 0, 0, lambda k: pcol("a_norm", k))
            narrow_lo_dve(dve, 1)
            a_in_dve(dve)
            gates_steps_dve(dve)
            unit_squares_dve(dve, 0, 2)
            gates_sums_dve(dve)
            unit_squares_dve(dve, 2, 14)
            gates_decay_dve(dve)
            unit_dve(dve)
            inside_dve(dve)
            across_dve(dve)
            onorm_dve(dve)
            add_h_slots(dve, SLOTS["a_out"], 1)
            norm_dve(dve, 1, 1, lambda k: pcol("f_norm", k), slot=SLOTS["f0_up0"])
            ffn_dve(dve, 0, 2)
            norm_dve(dve, 2, 2, lambda k: pcol("kv_norm", k), slot=SLOTS["b_k"])
            s_par_dve(dve)
            norm_dve(dve, 2, 3, lambda k: pcol("b_norm", k), root=False, slot=SLOTS["b_q"])
            attn_dve(dve)
            add_h_slots(dve, SLOTS["b_out"], 3)
            norm_dve(dve, 3, 4, lambda k: pcol("f_norm", 8 + k), slot=SLOTS["f1_up0"])
            ffn_dve(dve, 1, 4)
            mid_dve(dve, 4, 5)
            norm_dve(dve, 5, 5, lambda k: gainc(0, k), shift=lambda k: mod[:, 0, k:k + 1], slot=SLOTS["s_in"])
            ada_mod_dve(dve, 1)
            s_tables_dve(dve)
            s5_dve(dve)
            s_gelu_dve(dve)
            glu_dve(dve, 6)
            norm_dve(dve, 6, 6, lambda k: gainc(0, 8 + k), shift=lambda k: mod[:, 0, 24 + k:25 + k], slot=SLOTS["p0"])
            mlp_dve(dve, 0, 7)
            norm_dve(dve, 7, 7, lambda k: gainc(1, k), shift=lambda k: mod[:, 1, k:k + 1], slot=SLOTS["m_in"])
            m_in_dve(dve)
            ssd_dve(dve)
            gnorm_dve(dve)
            m_out_dve(dve, 8)
            norm_dve(dve, 8, 8, lambda k: gainc(1, 8 + k), shift=lambda k: mod[:, 1, 24 + k:25 + k], slot=SLOTS["p1"])
            mlp_dve(dve, 1, 9)
            end_dve(dve, 9)


def lay_out(inp):
    def cols(v):
        return np.ascontiguousarray(np.asarray(v).reshape(-1, P).T)

    def a(name):
        return np.asarray(inp[name])
    parts = {
        "a_norm": cols(a("a_norm")), "kv_norm": cols(a("kv_norm")), "b_norm": cols(a("b_norm")),
        "f_norm": cols(a("f_norm")), "final_norm": cols(a("final_norm")), "mix_g": cols(a("norm_mix_g_2")),
        "mlp_g": cols(a("norm_mlp_g_2")), "final_g": cols(a("final_norm_g_2")), "a_conv": cols(a("a_conv")),
        "a_out_norm": cols(a("a_out_norm")), "f_conv": cols(a("f_conv")), "f_conv_b": cols(a("f_conv_b")),
        "cond": cols(a("c_2")), "ada_b": cols(a("ada_b_2")), "s5_d": cols(a("s5_d_2")), "s5_b_glu": cols(a("s5_b_glu_2")),
        "lam_re": cols(a("s5_lambda_re_2")), "lam_im": cols(a("s5_lambda_im_2")),
        "log_dt": cols(np.repeat(a("s5_log_dt_2").reshape(-1), 64)),
        "m_conv": cols(a("m2_conv_w_2")), "m_conv_b": cols(a("m2_conv_b_2")),
        "m_d": cols(np.repeat(a("m2_d_2").reshape(-1), M_P)), "m_norm_g": cols(a("m2_norm_g_2")),
        "unit_scale": np.where(np.arange(P) < AH, float(P), 1.0)[:, None],
        "unit_eps": (np.where(np.arange(P) < AH, float(P), 1.0) * EPS1)[:, None],
        "one_col": np.repeat(np.arange(63)[None, :] == 31, P, axis=0).astype(np.float32),
        "qmask": np.kron(np.eye(4, dtype=np.float32), np.ones((32, 1), np.float32)),
    }
    par = np.zeros((P, PAR_N), np.float32)
    for name, v in parts.items():
        par[:, PAR[name]:PAR[name] + v.shape[1]] = v
    rows = np.concatenate([a(n).reshape(-1) for n in ("a_A_log", "a_dt_bias", "m2_a_log_2", "m2_dt_bias_2")])
    rel = np.clip(384 + np.arange(P)[:, None] - np.arange(T)[None, :], -256, 256) + 256
    strips = np.ascontiguousarray(a("b_rel_bias")[0][:, rel])
    bt = np.zeros((P, 2, S5Q, P), np.float32)
    ct = np.zeros((P, 2, S5N, 32), np.float32)
    for x, (b, c) in enumerate((("s5_b_re_2", "s5_c_re_2"), ("s5_b_im_2", "s5_c_im_2"))):
        for g in range(64):
            q, r = g // 8, 16 * (g % 8)
            e = 64 * (g % 2)
            bt[r:r + 16, x, q, e:e + 64] = a(b)[0, g].T
            ct[e:e + 64, x, g // 2, 16 * (g % 2):16 * (g % 2) + 16] = a(c)[0, g].T
    i = np.arange(P)
    lev = np.stack([(i[None, :] // (2 * s) == i[:, None] // (2 * s)) & (i[None, :] // s % 2 == 1) & (i[:, None] // s % 2 == 0)
                    for s in (1, 2, 4, 8, 16, 32, 64)], axis=1).astype(np.float32)
    upper = i[:, None] <= i[None, :]
    return {
        "x": a("x"), "par": par, "rows": rows[None, :], "strips": strips, "s5_bt": bt, "s5_ct": ct,
        "ident": np.eye(P, dtype=np.float32), "triu": upper.astype(np.float32),
        "upmask": np.where(upper, 0.0, NEG).astype(np.float32), "lev": lev,
        "a_w_in": a("a_w_in"), "a_w_out": a("a_w_out"), "f_w_up": a("f_w_up"), "f_w_down": a("f_w_down"),
        "w_kv": a("w_kv"), "b_w_q": a("b_w_q"), "b_w_out": a("b_w_out"), "ada_w": a("ada_w_2"),
        "s5_w_in": a("s5_w_in_2"), "s5_w_glu": a("s5_w_glu_2"), "mlp_w1": a("mlp_w1_2"), "mlp_w2": a("mlp_w2_2"),
        "m2_w_in": a("m2_w_in_2"), "m2_w_out": a("m2_w_out_2"),
    }


def kernel(**inputs):
    import concourse.bacc as bacc
    from concourse.bass_utils import run_bass_kernel_spmd

    nc = bacc.Bacc("TRN2", target_bir_lowering=False, num_devices=1)
    arrays = {f"in_{n}": np.ascontiguousarray(v) for n, v in lay_out(inputs).items()}
    t = {n[3:]: nc.dram_tensor(n, v.shape, mybir.dt.from_np(v.dtype), kind="ExternalInput").ap() for n, v in arrays.items()}
    out = nc.dram_tensor("out", (1, T, D), F32, kind="ExternalOutput").ap()
    build(nc, t, out)
    return run_bass_kernel_spmd(nc, [arrays], core_ids=[0]).results[0]["out"]
```
